# Optimizing a Trainium2 kernel written in Bass

```python
import math
import jax, jax.numpy as jnp
from jax import lax
import numpy as np

D_MODEL = 1024
BATCH = 1
SEQ = 256
DEPTH = 2
DEC_BATCH = 8
DEC_SEQ = 4
PAST_LEN = 256
PAGE_SIZE = 128

N_A_LAYERS = DEPTH // 2
N_B_LAYERS = DEPTH - N_A_LAYERS
GDN_DK = 128
GDN_DV = 128
GDN_HEADS = D_MODEL // GDN_DK
GDN_QK = GDN_HEADS * GDN_DK
GDN_VW = GDN_HEADS * GDN_DV
GDN_CONV_CH = 2 * GDN_QK + GDN_VW
GDN_IN = GDN_CONV_CH + GDN_VW + 2 * GDN_HEADS
CONV_W = 4
GDN_CHUNK = 64
DIFF_HEADS = 8
DIFF_DH = D_MODEL // (2 * DIFF_HEADS)
ROPE_THETA = 10000.0
Q_BLOCK = 128
N_GROUPS = 4
EXP_PER_GROUP = 8
N_EXPERTS = N_GROUPS * EXP_PER_GROUP
D_FF_EXPERT = 512
TOP_K = 2
MOE_BLOCK = 128
EPS = 1e-6

kernel_name = 'yoco_gdn_diffattn_hmoe_step'

F32 = jnp.float32

def rms_norm(x, g):
    xf = x.astype(F32)
    y = xf * lax.rsqrt(jnp.mean(xf * xf, axis=-1, keepdims=True) + EPS)
    return (y * g.astype(F32)).astype(x.dtype)

def rope(x, pos):
    half = x.shape[-1] // 2
    inv = ROPE_THETA ** (-jnp.arange(half, dtype=F32) / half)
    ang = pos.astype(F32)[:, None] * inv[None, :]
    cos = jnp.cos(ang)[:, None, None, :]
    sin = jnp.sin(ang)[:, None, None, :]
    xf = x.astype(F32)
    x1, x2 = xf[..., :half], xf[..., half:]
    return jnp.concatenate([x1 * cos - x2 * sin, x2 * cos + x1 * sin], axis=-1).astype(x.dtype)

def lambda_init(layer):
    return 0.8 - 0.6 * math.exp(-0.3 * layer)

def causal_conv_silu(u, buf, w):
    L = u.shape[1]
    full = jnp.concatenate([buf.astype(u.dtype), u], axis=1)
    acc = full[:, 0:L] * w[0]
    for i in range(1, CONV_W):
        acc = acc + full[:, i:i + L] * w[i]
    return jax.nn.silu(acc), full[:, -(CONV_W - 1):]

def gated_delta_chunked(q, k, v, beta, g, s0):
    B, L, H, DK = q.shape
    DV = v.shape[-1]
    C = min(GDN_CHUNK, L)
    n = -(-L // C)
    pad = n * C - L

    def blocks(t):
        t = jnp.pad(t, [(0, 0), (0, pad)] + [(0, 0)] * (t.ndim - 2))
        t = t.reshape((B, n, C) + t.shape[2:])
        return jnp.moveaxis(jnp.moveaxis(t, 1, 0), 2, 3)

    incl = jnp.tril(jnp.ones((C, C), bool))
    strict = jnp.tril(jnp.ones((C, C), bool), -1)
    eye = jnp.eye(C, dtype=F32)

    def step(S, inp):
        qc, kc, vc, bc, gc = inp
        G = jnp.cumsum(gc, axis=-1)
        decay = jnp.exp(jnp.where(incl, G[..., :, None] - G[..., None, :], -jnp.inf))
        kk = jnp.einsum('bhik,bhjk->bhij', kc, kc)
        lmat = jnp.where(strict, bc[..., :, None] * kk * decay, 0.0)
        rhs = jnp.concatenate([bc[..., None] * vc, (bc * jnp.exp(G))[..., None] * kc], axis=-1)
        sol = lax.linalg.triangular_solve(lmat + eye, rhs, left_side=True, lower=True, unit_diagonal=True)
        u = sol[..., :DV] - jnp.einsum('bhck,bhkv->bhcv', sol[..., DV:], S)
        qk = jnp.einsum('bhik,bhjk->bhij', qc, kc) * decay
        o = jnp.einsum('bhck,bhkv->bhcv', qc * jnp.exp(G)[..., None], S) + jnp.einsum('bhij,bhjv->bhiv', qk, u)
        g_last = G[..., -1:]
        S_new = jnp.exp(g_last)[..., None] * S + jnp.einsum('bhck,bhcv->bhkv', kc * jnp.exp(g_last - G)[..., None], u)
        return S_new, o

    s_fin, o = lax.scan(step, s0, (blocks(q), blocks(k), blocks(v), blocks(beta), blocks(g)))
    o = jnp.moveaxis(jnp.moveaxis(o, 3, 2), 0, 1).reshape(B, n * C, H, DV)[:, :L]
    return o, s_fin

def gdn_mixer(xn, conv_buf, s0, w_in, conv_w, a_log, dt_bias, onorm, w_out):
    B, L, _ = xn.shape
    proj = xn @ w_in
    qkv, new_buf = causal_conv_silu(proj[..., :GDN_CONV_CH], conv_buf, conv_w)
    z = proj[..., GDN_CONV_CH:GDN_CONV_CH + GDN_VW].reshape(B, L, GDN_HEADS, GDN_DV)
    b_raw = proj[..., GDN_CONV_CH + GDN_VW:GDN_CONV_CH + GDN_VW + GDN_HEADS].astype(F32)
    a_raw = proj[..., GDN_CONV_CH + GDN_VW + GDN_HEADS:].astype(F32)
    q = qkv[..., :GDN_QK].reshape(B, L, GDN_HEADS, GDN_DK).astype(F32)
    k = qkv[..., GDN_QK:2 * GDN_QK].reshape(B, L, GDN_HEADS, GDN_DK).astype(F32)
    v = qkv[..., 2 * GDN_QK:].reshape(B, L, GDN_HEADS, GDN_DV).astype(F32)
    q = q * lax.rsqrt(jnp.sum(q * q, axis=-1, keepdims=True) + EPS) * (GDN_DK ** -0.5)
    k = k * lax.rsqrt(jnp.sum(k * k, axis=-1, keepdims=True) + EPS)
    beta = jax.nn.sigmoid(b_raw)
    g = -jnp.exp(a_log.astype(F32)) * jax.nn.softplus(a_raw + dt_bias.astype(F32))
    o, s_new = gated_delta_chunked(q, k, v, beta, g, s0.astype(F32))
    o = rms_norm(o, onorm) * jax.nn.silu(z.astype(F32))
    return o.reshape(B, L, GDN_VW).astype(xn.dtype) @ w_out, new_buf, s_new

def shared_kv(h, pos, kv_norm, w_kv):
    B, L, _ = h.shape
    kv = rms_norm(h, kv_norm) @ w_kv
    k = rope(kv[..., :D_MODEL].reshape(B, L, DIFF_HEADS, 2, DIFF_DH), pos)
    k = k.reshape(B, L, DIFF_HEADS, 2 * DIFF_DH)
    v = kv[..., D_MODEL:].reshape(B, L, DIFF_HEADS, 2 * DIFF_DH)
    return k, v

def diff_attention(q, k, v, q_pos, k_pos, lam):
    B, Lq, H, _, d = q.shape
    qb = Q_BLOCK if Lq % Q_BLOCK == 0 else Lq
    nb = Lq // qb
    qs = q.reshape(B, nb, qb, H, 2, d).swapaxes(0, 1)
    ps = q_pos.reshape(nb, qb)

    def block(args):
        qblk, pblk = args
        s = jnp.einsum('bqhcd,bkhcd->bhcqk', qblk, k).astype(F32)
        mask = k_pos[None, :] <= pblk[:, None]
        p = jax.nn.softmax(jnp.where(mask, s, -jnp.inf), axis=-1)
        a = p[:, :, 0] - lam * p[:, :, 1]
        return jnp.einsum('bhqk,bkhe->bqhe', a.astype(v.dtype), v)

    o = lax.map(block, (qs, ps))
    return o.swapaxes(0, 1).reshape(B, Lq, H, 2 * d)

def diff_mixer(xn, k_rows, v_rows, q_pos, k_pos, w_q, lam_p, subln, w_out, lam_init):
    B, L, _ = xn.shape
    q = (xn @ w_q).reshape(B, L, DIFF_HEADS, 2, DIFF_DH)
    q = rope(q, q_pos) * (DIFF_DH ** -0.5)
    k = k_rows.reshape(k_rows.shape[0], k_rows.shape[1], DIFF_HEADS, 2, DIFF_DH)
    lp = lam_p.astype(F32)
    lam = jnp.exp(jnp.sum(lp[0] * lp[1])) - jnp.exp(jnp.sum(lp[2] * lp[3])) + lam_init
    o = diff_attention(q, k, v_rows, q_pos, k_pos, lam)
    o = rms_norm(o, subln) * (1.0 - lam_init)
    return o.reshape(B, L, D_MODEL).astype(xn.dtype) @ w_out

def routed_experts(xt, eidx, gate, w_gate, w_up, w_down):
    T, D = xt.shape
    A = T * TOP_K
    flat_e = eidx.reshape(-1)
    order = jnp.argsort(flat_e)
    sorted_e = flat_e[order]
    counts = jnp.bincount(flat_e, length=N_EXPERTS)
    padded = (counts + MOE_BLOCK - 1) // MOE_BLOCK * MOE_BLOCK
    pad_end = jnp.cumsum(padded)
    pad_start = pad_end - padded
    start = jnp.cumsum(counts) - counts
    dest = (pad_start[sorted_e] + jnp.arange(A) - start[sorted_e]).astype(jnp.int32)
    n_blocks = -(-A // MOE_BLOCK) + N_EXPERTS
    P = n_blocks * MOE_BLOCK
    row_tok = jnp.zeros((P,), jnp.int32).at[dest].set((order // TOP_K).astype(jnp.int32))
    block_e = jnp.minimum(jnp.searchsorted(pad_end, jnp.arange(n_blocks) * MOE_BLOCK, side='right'), N_EXPERTS - 1)
    xb = xt[row_tok].reshape(n_blocks, MOE_BLOCK, D)

    def expert_block(args):
        xblk, e = args
        hid = jax.nn.silu(xblk @ w_gate[e]) * (xblk @ w_up[e])
        return hid @ w_down[e]

    ys = lax.map(expert_block, (xb, block_e)).reshape(P, D)
    dest_orig = jnp.zeros((A,), jnp.int32).at[order].set(dest)
    return jnp.einsum('tkd,tk->td', ys[dest_orig].reshape(T, TOP_K, D), gate.astype(ys.dtype))

def hier_moe(xn, w_rg, b_rg, w_re, b_re, w_gate, w_up, w_down):
    B, L, D = xn.shape
    T = B * L
    xt = xn.reshape(T, D)
    p_g = jax.nn.softmax((xt @ w_rg).astype(F32) + b_rg.astype(F32), axis=-1)
    g_sel = jnp.argmax(p_g, axis=-1)
    pg_sel = jnp.max(p_g, axis=-1, keepdims=True)
    e_logits = ((xt @ w_re).astype(F32) + b_re.astype(F32)).reshape(T, N_GROUPS, EXP_PER_GROUP)
    e_in = e_logits[jnp.arange(T), g_sel]
    top_p, top_i = lax.top_k(jax.nn.softmax(e_in, axis=-1), TOP_K)
    gate = pg_sel * top_p / jnp.sum(top_p, axis=-1, keepdims=True)
    eidx = (g_sel[:, None] * EXP_PER_GROUP + top_i).astype(jnp.int32)
    return routed_experts(xt, eidx, gate, w_gate, w_up, w_down).reshape(B, L, D)

def setup_inputs(seed: int = 0) -> dict:
    key = jax.random.key(seed)
    ks = jax.random.split(key, 32)

    def nrm(i, shape, scale):
        return jax.random.normal(ks[i], shape, F32) * scale

    n_pages = PAST_LEN // PAGE_SIZE
    n_used = DEC_BATCH * n_pages
    n_phys = n_used + max(1, n_used // 4)
    page_table = jax.random.permutation(ks[0], n_phys)[:n_used].reshape(DEC_BATCH, n_pages).astype(jnp.int32)
    dt = jnp.exp(jax.random.uniform(ks[9], (N_A_LAYERS, GDN_HEADS), F32, math.log(1e-3), math.log(1e-1)))
    dt_bias = dt + jnp.log(-jnp.expm1(-dt))
    a_log = jnp.log(jax.random.uniform(ks[8], (N_A_LAYERS, GDN_HEADS), F32, 1.0, 16.0))
    return {
        'x_prompt': nrm(1, (BATCH, SEQ, D_MODEL), 1.0),
        'x_sample': nrm(2, (DEC_BATCH, DEC_SEQ, D_MODEL), 1.0),
        'state_delta': nrm(3, (N_A_LAYERS, DEC_BATCH, GDN_HEADS, GDN_DK, GDN_DV), GDN_DK ** -0.5),
        'state_conv': nrm(4, (N_A_LAYERS, DEC_BATCH, CONV_W - 1, GDN_CONV_CH), 1.0),
        'cache_k': nrm(5, (n_phys, PAGE_SIZE, DIFF_HEADS, 2 * DIFF_DH), 1.0),
        'cache_v': nrm(6, (n_phys, PAGE_SIZE, DIFF_HEADS, 2 * DIFF_DH), 1.0),
        'page_table': page_table,
        'norm_a': 1.0 + nrm(7, (N_A_LAYERS, D_MODEL), 0.02),
        'w_in_a': nrm(10, (N_A_LAYERS, D_MODEL, GDN_IN), D_MODEL ** -0.5),
        'conv_w_a': nrm(11, (N_A_LAYERS, CONV_W, GDN_CONV_CH), CONV_W ** -0.5),
        'a_log': a_log,
        'dt_bias': dt_bias,
        'onorm_a': 1.0 + nrm(12, (N_A_LAYERS, GDN_DV), 0.02),
        'w_out_a': nrm(13, (N_A_LAYERS, GDN_VW, D_MODEL), 0.5 * GDN_VW ** -0.5),
        'kv_norm': 1.0 + nrm(14, (D_MODEL,), 0.02),
        'w_kv': nrm(15, (D_MODEL, 2 * D_MODEL), D_MODEL ** -0.5),
        'norm_b': 1.0 + nrm(16, (N_B_LAYERS, D_MODEL), 0.02),
        'w_q_b': nrm(17, (N_B_LAYERS, D_MODEL, D_MODEL), D_MODEL ** -0.5),
        'lam_b': nrm(18, (N_B_LAYERS, 4, DIFF_DH), 0.1),
        'subln_b': 1.0 + nrm(19, (N_B_LAYERS, 2 * DIFF_DH), 0.02),
        'w_out_b': nrm(20, (N_B_LAYERS, D_MODEL, D_MODEL), 0.5 * D_MODEL ** -0.5),
        'norm_m': 1.0 + nrm(21, (DEPTH, D_MODEL), 0.02),
        'w_rg': nrm(22, (DEPTH, D_MODEL, N_GROUPS), D_MODEL ** -0.5),
        'b_rg': nrm(23, (DEPTH, N_GROUPS), 0.01),
        'w_re': nrm(24, (DEPTH, D_MODEL, N_EXPERTS), D_MODEL ** -0.5),
        'b_re': nrm(25, (DEPTH, N_EXPERTS), 0.01),
        'w_gate_e': nrm(26, (DEPTH, N_EXPERTS, D_MODEL, D_FF_EXPERT), D_MODEL ** -0.5),
        'w_up_e': nrm(27, (DEPTH, N_EXPERTS, D_MODEL, D_FF_EXPERT), D_MODEL ** -0.5),
        'w_down_e': nrm(28, (DEPTH, N_EXPERTS, D_FF_EXPERT, D_MODEL), 0.5 * D_FF_EXPERT ** -0.5),
        'final_norm': 1.0 + nrm(29, (D_MODEL,), 0.02),
    }

def reference(x_prompt, x_sample, state_delta, state_conv, cache_k, cache_v, page_table,
              norm_a, w_in_a, conv_w_a, a_log, dt_bias, onorm_a, w_out_a,
              kv_norm, w_kv, norm_b, w_q_b, lam_b, subln_b, w_out_b,
              norm_m, w_rg, b_rg, w_re, b_re, w_gate_e, w_up_e, w_down_e, final_norm):

    def trunk(x, conv0, s0, past_k, past_v, past_len):
        B, L, _ = x.shape
        pos = past_len + jnp.arange(L, dtype=jnp.int32)
        k_pos = jnp.arange(past_len + L, dtype=jnp.int32)
        h = x
        convs, states = [], []
        k_new = v_new = k_all = v_all = None
        for layer in range(DEPTH):
            if layer < N_A_LAYERS:
                i = layer
                o, cb, s = gdn_mixer(rms_norm(h, norm_a[i]), conv0[i], s0[i], w_in_a[i], conv_w_a[i],
                                     a_log[i], dt_bias[i], onorm_a[i], w_out_a[i])
                convs.append(cb)
                states.append(s)
            else:
                j = layer - N_A_LAYERS
                if j == 0:
                    k_new, v_new = shared_kv(h, pos, kv_norm, w_kv)
                    if past_k is None:
                        k_all, v_all = k_new, v_new
                    else:
                        k_all = jnp.concatenate([past_k.astype(k_new.dtype), k_new], axis=1)
                        v_all = jnp.concatenate([past_v.astype(v_new.dtype), v_new], axis=1)
                o = diff_mixer(rms_norm(h, norm_b[j]), k_all, v_all, pos, k_pos, w_q_b[j], lam_b[j],
                               subln_b[j], w_out_b[j], lambda_init(layer))
            h = h + o
            h = h + hier_moe(rms_norm(h, norm_m[layer]), w_rg[layer], b_rg[layer], w_re[layer], b_re[layer],
                             w_gate_e[layer], w_up_e[layer], w_down_e[layer])
        return rms_norm(h, final_norm), jnp.stack(states), jnp.stack(convs), k_new, v_new

    bp = x_prompt.shape[0]
    conv0_p = jnp.zeros((N_A_LAYERS, bp, CONV_W - 1, GDN_CONV_CH), x_prompt.dtype)
    s0_p = jnp.zeros((N_A_LAYERS, bp, GDN_HEADS, GDN_DK, GDN_DV), F32)
    y_prompt, sd_p, sc_p, k_p, v_p = trunk(x_prompt, conv0_p, s0_p, None, None, 0)

    db = x_sample.shape[0]
    n_pages = page_table.shape[1]
    past_len = n_pages * PAGE_SIZE
    past_k = cache_k[page_table].reshape(db, past_len, DIFF_HEADS, 2 * DIFF_DH)
    past_v = cache_v[page_table].reshape(db, past_len, DIFF_HEADS, 2 * DIFF_DH)
    y_sample, sd_s, sc_s, k_s, v_s = trunk(x_sample, state_conv, state_delta, past_k, past_v, past_len)

    return (y_prompt, y_sample, sd_p, sc_p, k_p, v_p, sd_s, sc_s, k_s, v_s)


_drawn_inputs = setup_inputs


def setup_inputs(seed=0):
    import zlib

    import numpy as np

    out = dict(_drawn_inputs(seed))
    spreads = {}
    factors = {'onorm_a': 3.62,
     'kv_norm': 2.87,
     'norm_b': 5.477,
     'subln_b': 5.125,
     'norm_m': 2.88,
     'b_rg': 5.126,
     'b_re': 3.867,
     'final_norm': 2.917}
    for name, (base, spread) in spreads.items():
        noise = np.random.default_rng([zlib.crc32(name.encode()), seed]).standard_normal(out[name].shape)
        drawn = base * np.exp(spread * noise) if base else spread * noise
        out[name] = __import__('jax').numpy.asarray(drawn.astype(out[name].dtype))
    for name, factor in factors.items():
        out[name] = (out[name] * factor).astype(out[name].dtype)
    return out
```

```python
import math
from contextlib import ExitStack

import numpy as np

import concourse.bass as bass
from concourse import mybir

F32 = mybir.dt.float32
U32 = mybir.dt.uint32
I32 = mybir.dt.int32
ACT = mybir.ActivationFunctionType
ALU = mybir.AluOpType
AX = mybir.AxisListType

D_MODEL = 1024
SEQ = 256
DEC_BATCH = 8
DEC_SEQ = 4
PAST_LEN = 256
PAGE_SIZE = 128
N_PAGES = PAST_LEN // PAGE_SIZE
N_PHYS = DEC_BATCH * N_PAGES + max(1, DEC_BATCH * N_PAGES // 4)
HEADS = 8
DK = 128
CONV_CH = 3 * D_MODEL
GDN_IN = CONV_CH + D_MODEL + 2 * HEADS
CONV_W = 4
DH = 64
N_GROUPS = 4
EXP_PER_GROUP = 8
N_EXPERTS = 32
D_FF_EXPERT = 512
TOP_K = 2
EPS = 1e-6
LAYERS = 2

T_DEC = DEC_BATCH * DEC_SEQ
T_ALL = SEQ + T_DEC
TILE_ROWS = [128, 128, T_DEC]
TOK_TILES = len(TILE_ROWS)
KT = D_MODEL // 128
FT = D_FF_EXPERT // 128

SLOTS = 64
MAIN_GROUPS = N_EXPERTS // 2
OVER_LEVELS = -(-T_ALL // SLOTS) - 1
OVER_GROUPS = -(-((TOP_K * T_ALL) // SLOTS - 1) // 2)
N_COLS = MAIN_GROUPS + OVER_GROUPS
FAR = 1e30
NOWHERE = 16384.0


def shape_constants():
    p = np.arange(128)
    c = {}
    c["ident"] = np.eye(128)
    c["ones"] = np.ones((128, 128))
    c["before"] = (p[:, None] < p[None, :])
    c["lanes"] = np.tile(p, (128, 1))
    c["eps"] = np.full((128, 1), EPS)
    c["falling"] = np.tile(N_EXPERTS - np.arange(N_EXPERTS), (128, 1))
    c["odd_slots"] = np.tile(64 * (np.arange(N_EXPERTS) % 2), (128, 1))
    tok = p[:, None] + 128 * np.arange(TOK_TILES)[None, :]
    c["valid"] = tok < T_ALL
    c["token_no"] = np.stack([np.stack([tok + 1, TOP_K * tok + k + 1], 1) for k in range(TOP_K)], 1)
    c.update(mixer_constants())
    return {n: np.ascontiguousarray(a, np.float32).reshape(128, -1) for n, a in c.items()}


def mixer_constants():
    return {**gdn_constants(), **attn_constants()}


CW_COLS = SEQ + CONV_W - 1 + DEC_BATCH * (DEC_SEQ + CONV_W - 1)
DEC0 = SEQ + CONV_W - 1
DEC_STRIDE = DEC_SEQ + CONV_W - 1
ACC_COLS = CW_COLS - (CONV_W - 1)
CHUNK = 128
LEVELS = 7
V_STEPS = 31


def gdn_constants():
    c = {}
    p = np.arange(128)
    same = (p[:, None] // DEC_SEQ) == (p[None, :] // DEC_SEQ)
    upto = p[:, None] <= p[None, :]
    dec = np.zeros((128, T_DEC))
    dec[:T_DEC] = (same & upto)[:T_DEC, :T_DEC]
    c["upto"] = np.concatenate([upto, upto, dec], 1)
    c["floor"] = np.where(c["upto"] > 0, 0.0, -FAR)
    c["dec_same"] = np.where(np.arange(128)[:, None] < T_DEC, same[:, :T_DEC], 0)
    c["dec_seq"] = (p[:, None] // DEC_SEQ) == np.arange(DEC_BATCH)[None, :]
    lev = []
    for n in range(LEVELS):
        s = 1 << n
        lev.append((p[:, None] // (2 * s) == p[None, :] // (2 * s)) & ((p[:, None] // s) % 2 == 0) & ((p[None, :] // s) % 2 == 1))
    c["levels"] = np.stack(lev, 1)
    return c


def gdn_phase(nc, m):
    ctx, sems = ExitStack(), []
    with ctx:
        def sb(name, shape, dt=F32):
            return ctx.enter_context(nc.sbuf_tensor(f"gdn_{name}", shape, dt))

        def sem(name):
            sems.append(nc.alloc_semaphore(f"gdn_{name}"))
            return sems[-1]

        NT, rows, H = TOK_TILES, TILE_ROWS, HEADS
        at = [slice(128 * t, 128 * t + rows[t]) for t in range(NT)]
        resid, ident, ones = m["resid"], m["ident"], m["ones"]
        norm_b, sq, xn = (m["ring"][1][:, 1, D_MODEL * j:D_MODEL * (j + 1)] for j in range(3))
        ss = sb("ss", [128, NT])
        xT = sb("xT", [128, KT, T_ALL])
        w_ab = sb("w_ab", [128, KT, 2 * H])
        ab_bias = sb("ab_bias", [128, 2, H])
        ab = sb("ab", [128, NT, 2 * H])
        g = sb("g", [128, NT, H])
        gt = sb("gt", [128, NT, H])
        gt2 = sb("gt2", [128, NT, H])
        beta = sb("beta", [128, NT, H])
        G = sb("G", [128, NT, H])
        eG = sb("eG", [128, NT, H])
        beG = sb("beG", [128, NT, H])
        eL = sb("eL", [128, NT, H])
        decg = sb("decg", [T_DEC, DEC_BATCH, H])
        eLast = sb("eLast", [128, 2 + DEC_BATCH, H])
        w4 = m["ring"][1][:, 0, :].rearrange("p (j k c) -> p j k c", j=4, k=KT)
        st_in = sb("st_in", [28, 3, 128])
        cw = sb("cw", [128, 3, CONV_W])
        cin = sb("cin", [128, 3, CW_COLS])
        ends = sb("ends", [128, 3, 27])
        ends_tok = sb("ends_tok", [27, 3, 128])
        acc = sb("acc", [128, 3, CW_COLS])
        zraw = sb("zraw", [128, T_ALL])
        zs = sb("zs", [128, T_ALL])
        qkv = sb("qkv", [128, 3, T_ALL])
        qk2 = sb("qk2", [128, 2, T_ALL])
        rn = sb("rn", [128, 2, T_ALL])
        kbq = sb("kbq", [128, 2, T_ALL])
        kT = sb("kT", [128, T_ALL])
        eGB = sb("eGB", [128, T_ALL])
        gsrc = sb("gsrc", [128, T_ALL])
        bsrc = sb("bsrc", [128, T_ALL])
        D = sb("D", [128, T_ALL])
        KQD = sb("KQD", [128, 2, 2, 128])
        KQD2 = sb("KQD2", [T_DEC, 2, T_DEC])
        Mlev = sb("Mlev", [128, LEVELS, 2, 128])
        M2 = sb("M2", [T_DEC, 2, T_DEC])
        TU = sb("TU", [128, 2, 2, 128])
        TU2 = sb("TU2", [T_DEC, 2, T_DEC])
        Y = sb("Y", [128, 2, 128])
        Y2 = sb("Y2", [T_DEC, T_DEC])
        vb = sb("vb", [128, NT, 128])
        kg = sb("kg", [128, NT, 128])
        kd = sb("kd", [128, NT, 128])
        WQ = sb("WQ", [128, 2, T_ALL])
        wsT = sb("wsT", [128, 2, T_DEC])
        u = sb("u", [128, NT, 128])
        uB = sb("uB", [T_DEC, DEC_BATCH, 128])
        S1 = sb("S1", [128, 128])
        S2 = sb("S2", [128, 128])
        Sd = sb("Sd", [128, DEC_BATCH, 128])
        Sn = sb("Sn", [128, DEC_BATCH, 128])
        oT = sb("oT", [128, T_ALL])
        o2 = sb("o2", [128, T_ALL])
        ro = sb("ro", [128, T_ALL])
        ozT = sb("ozT", [128, H, T_ALL])
        onorm = sb("onorm", [128, 1])
        w_out = m["ring"][2][:].rearrange("p a n -> p (a n)").rearrange("p (h n) -> p h n", h=H)

        B = [ctx.enter_context(nc.psum_tensor(f"gdn_bank{i}", [128, 512], F32)) for i in range(8)]

        s = {n: sem(n) for n in (
            "x_in0 x_in1 x_in2 consts_in squares mean_made roots normed xT_made xT_kept ab_made ab_kept exp_in exp_out soft_in soft_out gates_made sums_made "
            "decays_in decays_out "
            "q_in k_in v_in z_in st_loaded st_T proj proj_kept prior_kept ends_copied conv_done silued squares2 sums2 roots2 ends_T ends_kept ends_stored "
            "src_made bcast eGB_made D_in D_made kb_made kv_T kv_kept KQ_made lev_made T1_made TU_kept Y_made Y_kept TU_made "
            "W_made W_kept z_kept rows_kept kT_made Y2_kept u0_made u_kept S1_made S1_kept ws_made ws_kept u2_made u1_made o_made oT_kept S2_made S2_kept Sd_in Sn_made uB_made Sn_kept "
            "S_stored o2_made osum_made oroot oz_made wout_in out_made out_kept v").split()}

        w_in = m["w_in_a"][0].rearrange("(p t) n -> p t n", t=KT)
        heads_of = [w_in[:, :, j * D_MODEL:(j + 1) * D_MODEL] for j in range(4)]
        slot_in = [s["q_in"], s["k_in"], s["v_in"], s["z_in"]]
        st_conv = m["state_conv"][0].rearrange("b j c -> (b j) c").rearrange("r (s c) -> r s c", s=3)
        cv_w = m["conv_w_a"][0].rearrange("j (s c) -> j s c", s=3)
        st_delta = m["state_delta"][0].rearrange("b h k v -> k h b v")
        out_delta = m["sd_sample"][0].rearrange("b h k v -> k h b v")
        out_delta_p = m["sd_prompt"][0, 0].rearrange("h k v -> k h v")
        out_conv = m["sc_sample"][0].rearrange("b j c -> (b j) c").rearrange("r (s c) -> r s c", s=3)
        out_conv_p = m["sc_prompt"][0, 0].rearrange("j (s c) -> j s c", s=3)
        dec_cin = cin[:, :, DEC0:].rearrange("p s (b c) -> p s b c", c=DEC_STRIDE)
        dec_acc = acc[:, :, DEC0:].rearrange("p s (b c) -> p s b c", c=DEC_STRIDE)[:, :, :, 0:DEC_SEQ]

        block = ctx.enter_context(nc.Block())

        @block.sync
        def _(sp):
            for t in range(NT):
                src = m["x_prompt"][0, at[t], :] if t < 2 else m["x_sample"].rearrange("b l d -> (b l) d")
                sp.dma_start(resid[0:rows[t], t, :], src).then_inc((s["x_in0"], s["x_in1"], s["x_in2"])[t], 16)
            sp.dma_start(norm_b[:], m["norm_a"][0:1, :].broadcast_to([128, D_MODEL])).then_inc(s["consts_in"], 16)
            sp.dma_start(m["consts"][:], m["consts_dram"]).then_inc(s["consts_in"], 16)
            sp.dma_start(w_ab[:], w_in[:, :, CONV_CH + D_MODEL:GDN_IN]).then_inc(s["consts_in"], 16)
            sp.dma_start(ab_bias[:, 0, :], m["a_log"][0:1, :].broadcast_to([128, H])).then_inc(s["consts_in"], 16)
            sp.dma_start(ab_bias[:, 1, :], m["dt_bias"][0:1, :].broadcast_to([128, H])).then_inc(s["consts_in"], 16)
            sp.dma_start(onorm[:], m["onorm_a"].rearrange("a v -> v a")).then_inc(s["consts_in"], 16)

            def load(h, first=False):
                if not first:
                    sp.wait_ge(s["st_T"], h)
                for r, src in ((slice(0, 24), st_conv), (slice(24, 28), cv_w)):
                    sp.dma_start(st_in[r, :, :], src[:, :, bass.ds(h * 128, 128)]).then_inc(s["st_loaded"], 16)
                for j in range(4):
                    if not first:
                        sp.wait_ge(s["proj"], 4 * h - 3 + j)
                    sp.dma_start(w4[:, j], heads_of[j][:, :, bass.ds(h * 128, 128)]).then_inc(slot_in[j], 16)

            def load_state(h, first=False):
                if not first:
                    sp.wait_ge(s["Sn_kept"], 2 * h)
                sp.dma_start(Sd[:], st_delta[:, bass.ds(h, 1), :, :].rearrange("k h b v -> k (h b) v")).then_inc(s["Sd_in"], 16)

            def store(h):
                sp.wait_ge(s["ends_kept"], h + 1)
                sp.dma_start(out_conv_p[:, :, bass.ds(h * 128, 128)], ends_tok[0:3, :, :]).then_inc(s["ends_stored"], 16)
                sp.dma_start(out_conv[:, :, bass.ds(h * 128, 128)], ends_tok[3:27, :, :]).then_inc(s["ends_stored"], 16)
                sp.wait_ge(s["S2_kept"], h + 1)
                sp.dma_start(out_delta_p[:, bass.ds(h, 1), :].rearrange("k h v -> k (h v)"), S2[:]).then_inc(s["S_stored"], 16)
                sp.wait_ge(s["Sn_kept"], 2 * h + 2)
                sp.dma_start(out_delta[:, bass.ds(h, 1), :, :].rearrange("k h b v -> k (h b) v"), Sn[:]).then_inc(s["S_stored"], 16)

            load(0, True)
            load_state(0, True)
            with sp.Fori(0, H - 1) as h:
                load(h + 1)
                store(h)
                load_state(h + 1)
            sp.dma_start(w_out, m["w_out_a"][0].rearrange("(h p) n -> p h n", p=128)).then_inc(s["wout_in"], 16)
            m["prefetch"](sp, 0, (0,))
            sp.wait_ge(s["proj"], 4 * H)
            m["prefetch"](sp, 0, (1,))
            store(H - 1)
            sp.wait_ge(s["ends_stored"], 32 * H)
            sp.wait_ge(s["S_stored"], 32 * H)
            sp.wait_ge(s["out_made"], 2 * NT)
            m["prefetch"](sp, 0, (2,))

        @block.gpsimd
        def _(pool):
            nc.gpsimd.memset(cin[:, :, 0:CONV_W - 1], 0.0).then_inc(s["prior_kept"], 1)
            pool.wait_ge(s["gates_made"], 1)

            def head(h):
                pool.wait_ge(s["bcast"], h)
                pool.wait_ge(s["proj_kept"], 6 * h + 6)
                pool.wait_ge(s["ends_T"], h)
                for t in range(NT):
                    r = rows[t]
                    nc.gpsimd.tensor_tensor(gsrc[0:r, at[t]], m["upto"][0:r, at[t]], g[0:r, t, bass.ds(h, 1)].broadcast_to([r, r]), ALU.mult).then_inc(s["src_made"], 1)
                    nc.gpsimd.tensor_tensor(bsrc[0:r, at[t]], ident[0:r, 0:r], beta[0:r, t, bass.ds(h, 1)].broadcast_to([r, r]), ALU.mult).then_inc(s["src_made"], 1)
                nc.gpsimd.tensor_copy(ends[:, :, 0:3], cin[:, :, SEQ:SEQ + 3]).then_inc(s["ends_copied"], 1)
                for j in range(3):
                    nc.gpsimd.tensor_copy(ends[:, j, 3:27].rearrange("p (b c) -> p b c", c=3), dec_cin[:, j, :, DEC_SEQ:]).then_inc(s["ends_copied"], 1)

            with pool.Fori(0, H) as h:
                head(h)

        @block.scalar
        def _(act):
            A = nc.scalar
            for t in range(NT):
                r = rows[t]
                act.wait_ge((s["x_in0"], s["x_in1"], s["x_in2"])[t], 16)
                if t == 0:
                    act.wait_ge(s["squares"], 1)
                A.activation(sq[0:r, :], resid[0:r, t, :], ACT.Square, accum_out=ss[0:r, t:t + 1]).then_inc(s["squares"], 1)
                act.wait_ge(s["squares"], t + 2)
            act.wait_ge(s["mean_made"], 1)
            A.activation(ss[:, :], ss[:, :], ACT.Sqrt).then_inc(s["roots"], 1)
            for t in range(NT):
                act.wait_ge(s["xT_made"], 2 * t + 2)
                A.copy(xT[:, 4:8, at[t]], B[1][:, :].rearrange("p (k r) -> p k r", k=4)[:, :, 0:rows[t]]).then_inc(s["xT_kept"], 1)
            act.wait_ge(s["exp_in"], 1)
            A.activation(gt[:], gt[:], ACT.Exp).then_inc(s["exp_out"], 1)
            A.activation(beta[:], beta[:], ACT.Exp).then_inc(s["exp_out"], 1)
            A.activation(ab_bias[:, 0, :], ab_bias[:, 0, :], ACT.Exp).then_inc(s["exp_out"], 1)
            act.wait_ge(s["exp_out"], 3)
            act.wait_ge(s["soft_in"], 1)
            A.activation(gt[:], gt[:], ACT.Ln).then_inc(s["soft_out"], 1)

            def evacuate(h, j, first=False):
                act.wait_ge(s["proj"], 4 * h + j + 1)
                if not first and j == 0:
                    act.wait_ge(s["conv_done"], h)
                    act.wait_ge(s["ends_copied"], 4 * h)
                src = B[j % 2]
                if j < 3:
                    A.copy(cin[:, j, 3:3 + SEQ], src[:, 0:SEQ]).then_inc(s["proj_kept"], 1)
                    A.copy(dec_cin[:, j, :, 3:], src[:, SEQ:T_ALL].rearrange("p (b c) -> p b c", c=DEC_SEQ)).then_inc(s["proj_kept"], 1)
                else:
                    if not first:
                        act.wait_ge(s["silued"], 3 * h)
                    A.copy(zraw[:, :], src[:, 0:T_ALL]).then_inc(s["z_kept"], 1)

            def chain(h, more):
                act.wait_ge(s["conv_done"], h + 1)
                act.wait_ge(s["oz_made"], h)
                A.activation(zs[:, :], zraw[:, :], ACT.Silu).then_inc(s["silued"], 1)
                A.activation(qkv[:, :, 0:SEQ], acc[:, :, 0:SEQ], ACT.Silu).then_inc(s["silued"], 1)
                A.activation(qkv[:, :, SEQ:].rearrange("p s (b c) -> p s b c", c=DEC_SEQ),
                             dec_acc, ACT.Silu).then_inc(s["silued"], 1)
                act.wait_ge(s["sums2"], h + 1)
                for j in range(2):
                    A.activation(rn[:, j, :], B[2 + j][:, 0:T_ALL], ACT.Sqrt, bias=m["eps"][:, 0:1]).then_inc(s["roots2"], 1)
                act.wait_ge(s["bcast"], h + 1)
                A.activation(eGB[:, :], B[2][:, 0:T_ALL], ACT.Exp).then_inc(s["eGB_made"], 1)
                act.wait_ge(s["D_in"], h + 1)
                A.activation(D[:, 0:256], D[:, 0:256], ACT.Exp).then_inc(s["D_made"], 1)
                A.activation(D[0:T_DEC, 256:], D[0:T_DEC, 256:], ACT.Exp).then_inc(s["D_made"], 1)
                act.wait_ge(s["kv_T"], h + 1)
                for t in range(2):
                    kt, vt = B[6][:, 256 * t:256 * t + 128], B[6][:, 256 * t + 128:256 * t + 256]
                    A.activation(vb[:, t, :], vt, ACT.Copy, scale=beta[:, t, bass.ds(h, 1)]).then_inc(s["kv_kept"], 1)
                    A.activation(kg[:, t, :], kt, ACT.Copy, scale=beG[:, t, bass.ds(h, 1)]).then_inc(s["kv_kept"], 1)
                    A.activation(kd[:, t, :], kt, ACT.Copy, scale=eL[:, t, bass.ds(h, 1)]).then_inc(s["kv_kept"], 1)
                kt, vt = B[7][0:T_DEC, 0:128], B[7][0:T_DEC, 128:256]
                A.activation(vb[0:T_DEC, 2, :], vt, ACT.Copy, scale=beta[0:T_DEC, 2, bass.ds(h, 1)]).then_inc(s["kv_kept"], 1)
                A.activation(kg[0:T_DEC, 2, :], kt, ACT.Copy, scale=beG[0:T_DEC, 2, bass.ds(h, 1)]).then_inc(s["kv_kept"], 1)
                A.activation(kd[0:T_DEC, 2, :], kt, ACT.Copy, scale=eL[0:T_DEC, 2, bass.ds(h, 1)]).then_inc(s["kv_kept"], 1)
                act.wait_ge(s["ends_T"], h + 1)
                act.wait_ge(s["ends_stored"], 32 * h)
                A.copy(ends_tok[:, :, :], B[7][0:27, 0:384].rearrange("p (s c) -> p s c", s=3)).then_inc(s["ends_kept"], 1)
                if more:
                    for j in range(4):
                        evacuate(h + 1, j)
                act.wait_ge(s["osum_made"], h + 1)
                A.activation(ro[:, :], B[2][:, 0:T_ALL], ACT.Sqrt, scale=1.0 / DK, bias=m["eps"][:, 0:1]).then_inc(s["oroot"], 1)

            for j in range(4):
                evacuate(0, j, True)
            act.wait_ge(s["decays_in"], 1)
            A.activation(eG[:], G[:], ACT.Exp).then_inc(s["decays_out"], 1)
            A.activation(eL[:], eL[:], ACT.Exp).then_inc(s["decays_out"], 1)
            A.activation(eLast[:], eLast[:], ACT.Exp).then_inc(s["decays_out"], 1)
            with act.Fori(0, H - 1) as h:
                chain(h, True)
            chain(H - 1, False)

        @block.vector
        def _(dve):
            V = nc.vector
            st = {"base": 0, "n": 0}

            def link(ins):
                st["n"] += 1
                ins.then_inc(s["v"], 1)
                dve.wait_ge(s["v"], st["base"] + st["n"])

            V.memset(ss[:], 1.0).then_inc(s["squares"], 1)
            link(V.memset(ab[:], 0.0))
            link(V.memset(G[:], 0.0))
            link(V.memset(eL[:], 0.0))
            dve.wait_ge(s["squares"], NT + 1)
            V.tensor_scalar(ss[:, :], ss[:, :], 1.0 / D_MODEL, EPS, ALU.mult, ALU.add).then_inc(s["mean_made"], 1)
            dve.wait_ge(s["roots"], 1)
            link(V.reciprocal(ss[:, :], ss[:, :]))
            dve.wait_ge(s["consts_in"], 16 * 6)
            for t in range(NT):
                r = rows[t]
                if t:
                    dve.wait_ge(s["xT_made"], 2 * t)
                V.scalar_tensor_tensor(xn[0:r, :], resid[0:r, t, :], ss[0:r, t:t + 1], norm_b[0:r, :], ALU.mult, ALU.mult).then_inc(s["normed"], 1)
                dve.wait_ge(s["xT_made"], 2 * t + 1)
                V.tensor_copy(xT[:, 0:4, at[t]], B[0][:, :].rearrange("p (k r) -> p k r", k=4)[:, :, 0:r]).then_inc(s["xT_kept"], 1)
            dve.wait_ge(s["ab_made"], 1)
            for t in range(NT):
                r = rows[t]
                link(V.tensor_copy(ab[0:r, t, :], B[2][0:r, 16 * t:16 * t + 16]))

            def all_tiles(a):
                return a.unsqueeze(1).broadcast_to([128, NT, H])

            link(V.tensor_scalar(beta[:], ab[:, :, 0:H], -1.0, None, ALU.mult))
            link(V.tensor_tensor(g[:], ab[:, :, H:], all_tiles(ab_bias[:, 1, :]), ALU.add))
            link(V.tensor_scalar(gt2[:], g[:], -1.0, None, ALU.mult))
            V.tensor_tensor(gt[:], gt2[:], g[:], ALU.min).then_inc(s["exp_in"], 1)
            link(V.tensor_scalar(g[:], g[:], 0.0, None, ALU.max))
            dve.wait_ge(s["exp_out"], 3)
            V.tensor_scalar(gt[:], gt[:], 1.0, None, ALU.add).then_inc(s["soft_in"], 1)
            link(V.tensor_scalar(beta[:], beta[:], 1.0, None, ALU.add))
            link(V.reciprocal(beta[:], beta[:]))
            dve.wait_ge(s["soft_out"], 1)
            link(V.tensor_tensor(g[:], g[:], gt[:], ALU.add))
            link(V.tensor_tensor(g[:], g[:], all_tiles(ab_bias[:, 0, :]), ALU.mult))
            link(V.tensor_scalar(g[:], g[:], -1.0, None, ALU.mult))
            V.tensor_tensor(decg[:], g[0:T_DEC, 2, :].unsqueeze(1).broadcast_to([T_DEC, DEC_BATCH, H]),
                            m["dec_seq"][0:T_DEC, :].unsqueeze(2).broadcast_to([T_DEC, DEC_BATCH, H]), ALU.mult).then_inc(s["gates_made"], 1)
            dve.wait_ge(s["sums_made"], 1)
            for t in range(NT):
                r = rows[t]
                link(V.tensor_copy(G[0:r, t, :], B[2][0:r, 8 * t:8 * t + 8]))
                link(V.tensor_tensor(eL[0:r, t, :], B[2][0:r, 24 + 8 * t:32 + 8 * t], G[0:r, t, :], ALU.subtract))
            link(V.tensor_copy(eLast[:, 0:2, :], B[2][:, 24:40].rearrange("p (t h) -> p t h", t=2)))
            V.tensor_copy(eLast[:, 2:, :], B[2][:, 64:128].rearrange("p (b h) -> p b h", h=H)).then_inc(s["decays_in"], 1)
            dve.wait_ge(s["decays_out"], 3)
            link(V.tensor_tensor(beG[:], beta[:], eG[:], ALU.mult))
            pre = st["n"]

            def conv_rows(h):
                dve.wait_ge(s["st_T"], h + 1)
                v = B[7][:, 0:84].rearrange("p (s c) -> p s c", s=3)
                V.tensor_copy(cw[:, :, :], v[:, :, 24:28]).then_inc(s["rows_kept"], 1)
                for j in range(3):
                    V.tensor_copy(dec_cin[:, j, :, 0:3], v[:, j, 0:24].rearrange("p (b c) -> p b c", c=3)).then_inc(s["rows_kept"], 1)

            def chain(h, more):
                dve.wait_ge(s["rows_kept"], 4 * h + 4)
                for j in range(3):
                    if j == 0:
                        dve.wait_ge(s["proj_kept"], 6 * h + 6)
                        dve.wait_ge(s["silued"], 3 * h)
                    for tap in range(CONV_W):
                        src = cin[:, j, tap:tap + ACC_COLS]
                        if tap == 0:
                            ins = V.tensor_scalar(acc[:, j, 0:ACC_COLS], src, cw[:, j, 0:1], None, ALU.mult)
                        else:
                            ins = V.scalar_tensor_tensor(acc[:, j, 0:ACC_COLS], src, cw[:, j, tap:tap + 1], acc[:, j, 0:ACC_COLS], ALU.mult, ALU.add)
                        if j == 2 and tap == CONV_W - 1:
                            ins.then_inc(s["conv_done"], 1)
                        else:
                            link(ins)
                dve.wait_ge(s["silued"], 3 * h + 3)
                V.tensor_tensor(qk2[:], qkv[:, 0:2, :], qkv[:, 0:2, :], ALU.mult).then_inc(s["squares2"], 1)
                dve.wait_ge(s["roots2"], 2 * h + 2)
                link(V.reciprocal(rn[:], rn[:]))
                link(V.scalar_tensor_tensor(kbq[:, 1, :], qkv[:, 0, :], DK ** -0.5, rn[:, 0, :], ALU.mult, ALU.mult))
                V.tensor_tensor(kT[:, :], qkv[:, 1, :], rn[:, 1, :], ALU.mult).then_inc(s["kT_made"], 1)
                dve.wait_ge(s["kT_made"], h + 1)
                dve.wait_ge(s["bcast"], h + 1)
                V.tensor_tensor(kbq[:, 0, :], kT[:, :], B[3][:, 0:T_ALL], ALU.mult).then_inc(s["kb_made"], 1)
                dve.wait_ge(s["eGB_made"], h + 1)
                for t in range(NT):
                    r = rows[t]
                    ins = V.scalar_tensor_tensor(D[0:r, at[t]], B[2][0:r, at[t]], G[0:r, t, bass.ds(h, 1)], m["floor"][0:r, at[t]], ALU.subtract, ALU.min)
                    if t < 2:
                        link(ins)
                ins.then_inc(s["D_in"], 1)
                dve.wait_ge(s["W_made"], h)
                link(V.tensor_tensor(WQ[:, 1, :], kbq[:, 1, :], eGB[:, :], ALU.mult))
                dve.wait_ge(s["D_made"], 2 * h + 2)
                dve.wait_ge(s["KQ_made"], h + 1)
                link(V.tensor_tensor(KQD[:].rearrange("p t a i -> p t a i"), B[4][:, :].rearrange("p (t a i) -> p t a i", t=2, a=2),
                                     D[:, 0:256].rearrange("p (t i) -> p t i", t=2).unsqueeze(2).broadcast_to([128, 2, 2, 128]), ALU.mult))
                link(V.tensor_tensor(KQD2[:], B[5][0:T_DEC, 0:2 * T_DEC].rearrange("p (a i) -> p a i", a=2),
                                     D[0:T_DEC, 256:].unsqueeze(1).broadcast_to([T_DEC, 2, T_DEC]), ALU.mult))
                for n in range(LEVELS):
                    link(V.tensor_tensor(Mlev[:, n], KQD[:, :, 0, :], m["levels"][:, n, :].unsqueeze(1).broadcast_to([128, 2, 128]), ALU.mult))
                for n in range(2):
                    link(V.tensor_tensor(M2[:, n, :], KQD2[:, 0, :], m["levels"][0:T_DEC, n, 0:T_DEC], ALU.mult))
                link(V.tensor_tensor(TU[:, :, 1, :], ident[:, :].unsqueeze(1).broadcast_to([128, 2, 128]), Mlev[:, 0], ALU.subtract))
                V.tensor_tensor(TU2[:, 1, :], ident[0:T_DEC, 0:T_DEC], M2[:, 0, :], ALU.subtract).then_inc(s["lev_made"], 1)
                dve.wait_ge(s["T1_made"], h + 1)
                V.tensor_copy(TU[:, :, 0, :], B[4][:, 0:256].rearrange("p (t i) -> p t i", t=2)).then_inc(s["TU_kept"], 1)
                V.tensor_copy(TU2[:, 0, :], B[4][0:T_DEC, 256:288]).then_inc(s["TU_kept"], 1)
                for n in range(1, LEVELS):
                    k = (LEVELS - 1) * h + n
                    dve.wait_ge(s["Y_made"], k)
                    V.tensor_copy(Y[:], B[4][:, 0:256].rearrange("p (t i) -> p t i", t=2)).then_inc(s["Y_kept"], 1)
                    if n == 1:
                        V.tensor_copy(Y2[:], B[4][0:T_DEC, 256:288]).then_inc(s["Y2_kept"], 1)
                    dve.wait_ge(s["TU_made"], k)
                    V.tensor_tensor(TU[:], TU[:], B[5][:, :].rearrange("p (t a i) -> p t a i", t=2, a=2), ALU.subtract).then_inc(s["TU_kept"], 1)
                    if n == 1:
                        V.tensor_tensor(TU2[:], TU2[:], B[7][0:T_DEC, 0:64].rearrange("p (a i) -> p a i", a=2), ALU.subtract).then_inc(s["TU_kept"], 1)
                if more:
                    conv_rows(h + 1)
                dve.wait_ge(s["W_made"], h + 1)
                V.tensor_scalar(WQ[:, 0, :], B[6][:, 0:T_ALL], -1.0, None, ALU.mult).then_inc(s["W_kept"], 1)
                dve.wait_ge(s["u0_made"], h + 1)
                V.tensor_copy(u[:, 0, :], B[7][:, 0:128]).then_inc(s["u_kept"], 1)
                dve.wait_ge(s["ws_made"], h + 1)
                V.tensor_copy(wsT[:], B[3][:, 0:64].rearrange("p (b a c) -> p a b c", a=2, c=DEC_SEQ)).then_inc(s["ws_kept"], 1)
                dve.wait_ge(s["S1_made"], h + 1)
                V.tensor_copy(S1[:, :], B[4][:, 0:128]).then_inc(s["S1_kept"], 1)
                dve.wait_ge(s["u2_made"], h + 1)
                V.tensor_copy(u[:, 1, :], B[7][:, 0:128]).then_inc(s["u_kept"], 1)
                V.tensor_copy(u[0:T_DEC, 2, :], B[7][0:T_DEC, 128:256]).then_inc(s["u_kept"], 1)
                dve.wait_ge(s["u_kept"], 3 * h + 3)
                V.tensor_tensor(uB[:], u[0:T_DEC, 2, :].unsqueeze(1).broadcast_to([T_DEC, DEC_BATCH, 128]),
                                m["dec_seq"][0:T_DEC, :].unsqueeze(2).broadcast_to([T_DEC, DEC_BATCH, 128]), ALU.mult).then_inc(s["uB_made"], 1)
                dve.wait_ge(s["o_made"], h + 1)
                V.tensor_copy(oT[:, :], B[6][:, 0:T_ALL]).then_inc(s["oT_kept"], 1)
                dve.wait_ge(s["oT_kept"], h + 1)
                V.tensor_tensor(o2[:, :], oT[:, :], oT[:, :], ALU.mult).then_inc(s["o2_made"], 1)
                dve.wait_ge(s["S_stored"], 32 * h)
                dve.wait_ge(s["S2_made"], h + 1)
                V.scalar_tensor_tensor(S2[:, :], S1[:, :], eLast[:, 1, bass.ds(h, 1)], B[3][:, 0:128], ALU.mult, ALU.add).then_inc(s["S2_kept"], 1)
                dve.wait_ge(s["Sd_in"], 16 * h + 16)
                link(V.tensor_tensor(Sn[:], Sd[:], eLast[:, 2:, bass.ds(h, 1)].broadcast_to([128, DEC_BATCH, 128]), ALU.mult))
                dve.wait_ge(s["Sn_made"], h + 1)
                for j in range(2):
                    V.tensor_tensor(Sn[:, 4 * j:4 * j + 4, :], Sn[:, 4 * j:4 * j + 4, :], B[4 + j][:, :].rearrange("p (b v) -> p b v", b=4), ALU.add).then_inc(s["Sn_kept"], 1)
                dve.wait_ge(s["oroot"], h + 1)
                link(V.reciprocal(ro[:, :], ro[:, :]))
                link(V.tensor_tensor(ro[:, :], ro[:, :], oT[:, :], ALU.mult))
                V.scalar_tensor_tensor(ozT[:, bass.ds(h, 1), :].rearrange("p o t -> p (o t)"), ro[:, :], onorm[:, 0:1], zs[:, :], ALU.mult, ALU.mult).then_inc(s["oz_made"], 1)

            dve.wait_ge(s["prior_kept"], 1)
            conv_rows(0)
            with dve.Fori(0, H - 1) as h:
                st["base"], st["n"] = h * V_STEPS + pre, 0
                chain(h, True)
                assert st["n"] == V_STEPS, st["n"]
            st["base"], st["n"] = (H - 1) * V_STEPS + pre, 0
            chain(H - 1, False)
            for t in range(NT):
                r = rows[t]
                for j in range(2):
                    dve.wait_ge(s["out_made"], 2 * t + j + 1)
                    V.tensor_tensor(resid[0:r, t, 512 * j:512 * j + 512], resid[0:r, t, 512 * j:512 * j + 512], B[j][0:r, :], ALU.add).then_inc(s["out_kept"], 1)
            dve.wait_ge(s["out_kept"], 2 * NT)

        @block.tensor
        def _(pe):
            T = nc.tensor
            xv = xn[:, :].rearrange("p (c k) -> p k c", k=KT)
            for t in range(NT):
                r = rows[t]
                pe.wait_ge(s["normed"], t + 1)
                if t:
                    pe.wait_ge(s["xT_kept"], 2 * t)
                for k in range(KT):
                    last = T.transpose(B[k // 4][:, 128 * (k % 4):128 * (k % 4) + r], xv[0:r, k, :], ident[0:r, 0:r])
                    if k % 4 == 3:
                        last.then_inc(s["xT_made"], 1)
            pe.wait_ge(s["xT_kept"], 2 * NT)
            for t in range(NT):
                for k in range(KT):
                    last = T.matmul(B[2][0:rows[t], 16 * t:16 * t + 16], xT[:, k, at[t]], w_ab[:, k, :], start=(k == 0), stop=(k == KT - 1))
            last.then_inc(s["ab_made"], 1)

            def project(h, j, first=False):
                pe.wait_ge(slot_in[j], 16 * h + 16)
                if not first:
                    if j == 0:
                        pe.wait_ge(s["proj_kept"], 6 * h)
                    elif j == 1:
                        pe.wait_ge(s["z_kept"], h)
                if j == 2:
                    pe.wait_ge(s["proj_kept"], 6 * h + 2)
                elif j == 3:
                    pe.wait_ge(s["proj_kept"], 6 * h + 4)
                for k in range(KT):
                    last = T.matmul(B[j % 2][:, 0:T_ALL], w4[:, j, k, :], xT[:, k, :], start=(k == 0), stop=(k == KT - 1))
                last.then_inc(s["proj"], 1)

            def conv_rows(h):
                for j in range(3):
                    last = T.transpose(B[7][:, 28 * j:28 * j + 28], st_in[:, j, :], ident[0:28, 0:28])
                last.then_inc(s["st_T"], 1)

            def chain(h, more):
                pe.wait_ge(s["squares2"], h + 1)
                for j in range(2):
                    last = T.matmul(B[2 + j][:, 0:T_ALL], ones[:, :], qk2[:, j, :], start=True, stop=True)
                last.then_inc(s["sums2"], 1)
                pe.wait_ge(s["ends_copied"], 4 * h + 4)
                pe.wait_ge(s["src_made"], 6 * h + 6)
                pe.wait_ge(s["roots2"], 2 * h + 2)
                for src, bank in ((gsrc, 2), (bsrc, 3)):
                    for t in range(NT):
                        last = T.matmul(B[bank][:, at[t]], ones[0:rows[t], :], src[0:rows[t], at[t]], start=True, stop=True)
                last.then_inc(s["bcast"], 1)
                pe.wait_ge(s["kT_made"], h + 1)
                for t in range(2):
                    T.transpose(B[6][:, 256 * t:256 * t + 128], kT[:, at[t]], ident[:, :])
                    T.transpose(B[6][:, 256 * t + 128:256 * t + 256], qkv[:, 2, at[t]], ident[:, :])
                T.transpose(B[7][0:T_DEC, 0:128], kT[:, at[2]], ident[:, :])
                T.transpose(B[7][0:T_DEC, 128:256], qkv[:, 2, at[2]], ident[:, :]).then_inc(s["kv_T"], 1)
                pe.wait_ge(s["kb_made"], h + 1)
                for t in range(2):
                    T.matmul(B[4][:, 256 * t:256 * t + 256].rearrange("p (a i) -> p a i", a=2), kT[:, at[t]], kbq[:, :, at[t]], start=True, stop=True)
                T.matmul(B[5][0:T_DEC, 0:64].rearrange("p (a i) -> p a i", a=2), kT[:, at[2]], kbq[:, :, at[2]], start=True, stop=True).then_inc(s["KQ_made"], 1)
                pe.wait_ge(s["kv_kept"], 9 * h + 9)
                for j in range(3):
                    last = T.transpose(B[7][0:27, 128 * j:128 * j + 128], ends[:, j, :], ident[:, :])
                last.then_inc(s["ends_T"], 1)
                if more:
                    project(h + 1, 0)
                pe.wait_ge(s["lev_made"], h + 1)
                for t in range(2):
                    T.transpose(B[4][:, 128 * t:128 * t + 128], TU[:, t, 1, :], ident[:, :])
                T.transpose(B[4][0:T_DEC, 256:288], TU2[:, 1, :], ident[0:T_DEC, 0:T_DEC]).then_inc(s["T1_made"], 1)
                for n in range(1, LEVELS):
                    k = (LEVELS - 1) * h + n
                    kept = (LEVELS + 2) * h + n + (1 if n == 1 else 2)
                    pe.wait_ge(s["TU_kept"], kept)
                    for t in range(2):
                        last = T.matmul(B[4][:, 128 * t:128 * t + 128], Mlev[:, n, t, :], TU[:, t, 0, :], start=True, stop=True)
                    if n == 1:
                        last = T.matmul(B[4][0:T_DEC, 256:288], M2[:, 1, :], TU2[:, 0, :], start=True, stop=True)
                    last.then_inc(s["Y_made"], 1)
                    pe.wait_ge(s["Y_kept"], k)
                    if n == 1:
                        pe.wait_ge(s["Y2_kept"], h + 1)
                        pe.wait_ge(s["ends_kept"], h + 1)
                    for t in range(2):
                        T.matmul(B[5][:, 256 * t:256 * t + 128], TU[:, t, 1, :], Y[:, t, :], start=True, stop=True)
                        last = T.matmul(B[5][:, 256 * t + 128:256 * t + 256], Y[:, t, :], TU[:, t, 1, :], start=True, stop=True)
                    if n == 1:
                        T.matmul(B[7][0:T_DEC, 0:32], TU2[:, 1, :], Y2[:, :], start=True, stop=True)
                        last = T.matmul(B[7][0:T_DEC, 32:64], Y2[:, :], TU2[:, 1, :], start=True, stop=True)
                    last.then_inc(s["TU_made"], 1)
                    if more and n in (1, 3, 5):
                        project(h + 1, (n + 1) // 2)
                pe.wait_ge(s["TU_kept"], (LEVELS + 2) * h + LEVELS + 2)
                if more:
                    pe.wait_ge(s["st_loaded"], 32 * h + 64)
                for t in range(NT):
                    r = rows[t]
                    inv = TU[:, t, 1, :] if t < 2 else TU2[:, 1, :]
                    last = T.matmul(B[6][:, at[t]], kg[0:r, t, :], inv, start=True, stop=True)
                last.then_inc(s["W_made"], 1)
                if more:
                    conv_rows(h + 1)
                    pe.wait_ge(s["rows_kept"], 4 * h + 8)
                T.matmul(B[7][:, 0:128], TU[:, 0, 1, :], vb[:, 0, :], start=True, stop=True).then_inc(s["u0_made"], 1)
                pe.wait_ge(s["W_kept"], h + 1)
                pe.wait_ge(s["Sd_in"], 16 * h + 16)
                for b in range(DEC_BATCH):
                    c = SEQ + DEC_SEQ * b
                    last = T.matmul(B[3][:, 8 * b:8 * b + 8].rearrange("p (a c) -> p a c", a=2), Sd[:, b, :], WQ[:, :, c:c + DEC_SEQ], start=True, stop=True)
                last.then_inc(s["ws_made"], 1)
                pe.wait_ge(s["u_kept"], 3 * h + 1)
                T.matmul(B[4][:, 0:128], kd[:, 0, :], u[:, 0, :], start=True, stop=True).then_inc(s["S1_made"], 1)
                pe.wait_ge(s["S1_kept"], h + 1)
                pe.wait_ge(s["ws_kept"], h + 1)
                T.matmul(B[7][:, 0:128], TU[:, 1, 1, :], vb[:, 1, :], start=True, stop=False)
                T.matmul(B[7][:, 0:128], WQ[:, 0, at[1]], S1[:, :], start=False, stop=True)
                T.matmul(B[7][0:T_DEC, 128:256], TU2[:, 1, :], vb[0:T_DEC, 2, :], start=True, stop=False)
                T.matmul(B[7][0:T_DEC, 128:256], wsT[:, 0, :], ident[:, :], start=False, stop=True).then_inc(s["u2_made"], 1)
                T.matmul(B[6][:, at[0]], u[:, 0, :], KQD[:, 0, 1, :], start=True, stop=True)
                pe.wait_ge(s["u_kept"], 3 * h + 3)
                T.matmul(B[6][:, at[1]], u[:, 1, :], KQD[:, 1, 1, :], start=True, stop=False)
                T.matmul(B[6][:, at[1]], S1[:, :], WQ[:, 1, at[1]], start=False, stop=True)
                T.matmul(B[6][:, at[2]], u[0:T_DEC, 2, :], KQD2[:, 1, :], start=True, stop=False)
                T.matmul(B[6][:, at[2]], ident[:, :], wsT[:, 1, :], start=False, stop=True).then_inc(s["o_made"], 1)
                T.matmul(B[3][:, 0:128], kd[:, 1, :], u[:, 1, :], start=True, stop=True).then_inc(s["S2_made"], 1)
                pe.wait_ge(s["uB_made"], h + 1)
                for j in range(2):
                    last = T.matmul(B[4 + j][:, :], kd[0:T_DEC, 2, :], uB[:, 4 * j:4 * j + 4, :], start=True, stop=True)
                last.then_inc(s["Sn_made"], 1)
                pe.wait_ge(s["o2_made"], h + 1)
                T.matmul(B[2][:, 0:T_ALL], ones[:, :], o2[:, :], start=True, stop=True).then_inc(s["osum_made"], 1)

            for j in range(4):
                project(0, j, True)
            pe.wait_ge(s["st_loaded"], 32)
            conv_rows(0)
            pe.wait_ge(s["gates_made"], 1)
            for t in range(NT):
                r = rows[t]
                T.matmul(B[2][0:r, 8 * t:8 * t + 8], m["upto"][0:r, at[t]], g[0:r, t, :], start=True, stop=True)
                T.matmul(B[2][0:r, 24 + 8 * t:32 + 8 * t], ones[:, :] if t < 2 else m["dec_same"][0:r, :], g[0:r, t, :], start=True, stop=True)
            T.matmul(B[2][:, 64:128], ones[0:T_DEC, :], decg[:, :, :].rearrange("p b h -> p (b h)"), start=True, stop=True).then_inc(s["sums_made"], 1)
            with pe.Fori(0, H - 1) as h:
                chain(h, True)
            chain(H - 1, False)
            pe.wait_ge(s["wout_in"], 16)
            pe.wait_ge(s["oz_made"], H)
            for t in range(NT):
                if t:
                    pe.wait_ge(s["out_kept"], 2 * t)
                for j in range(2):
                    for h in range(H):
                        last = T.matmul(B[j][0:rows[t], :], ozT[:, h, at[t]], w_out[:, h, 512 * j:512 * j + 512], start=(h == 0), stop=(h == H - 1))
                    last.then_inc(s["out_made"], 1)

    nc.clear_and_free_semaphores(sems)
    nc.all_engine_barrier(sem_only=True)


LAM_INIT = 0.8 - 0.6 * math.exp(-0.3 * 1)
ROPE_THETA = 10000.0
SCORES = 128 + 256
S_STEPS = 5
P_STEPS = 8


def attn_constants():
    c = {}
    half = DH // 2
    p = np.arange(128)
    pos = np.stack([p, 128 + p, PAST_LEN + p % DEC_SEQ], 1).astype(np.float32)
    inv = (np.float32(ROPE_THETA) ** (-np.arange(half, dtype=np.float32) / np.float32(half))).astype(np.float32)
    ang = pos[:, :, None] * inv
    c["cos"] = np.cos(ang)
    c["sin"] = np.sin(ang)
    causal = np.where(p[None, :] <= p[:, None], 0.0, -FAR)
    c["causal"] = np.concatenate([causal, np.zeros((128, 128)), causal], 1)
    rb, rc, rh, rq = p // 64, (p // 32) % 2, (p // 4) % 8, p % 4
    kb, kq = np.arange(T_DEC) // DEC_SEQ, np.arange(T_DEC) % DEC_SEQ
    pair = np.arange(DEC_BATCH // 2)
    seen = (kb[None, None, :] == 2 * pair[None, :, None] + rb[:, None, None]) & (kq[None, None, :] <= rq[:, None, None])
    c["new_keys"] = np.where(seen, 0.0, -FAR)
    col = np.arange(64)
    c["halves"] = (rb[:, None] == col // 32) & (rh[:, None] == (col // 4) % 8) & (rq[:, None] == col % 4)
    c["first_half"] = rc[:, None] == 0
    c["second_half"] = rc[:, None] == 1
    return c


def attn_phase(nc, m):
    ctx, sems = ExitStack(), []
    with ctx:
        def sb(name, shape, dt=F32):
            return ctx.enter_context(nc.sbuf_tensor(f"at_{name}", shape, dt))

        def sem(name):
            sems.append(nc.alloc_semaphore(f"at_{name}"))
            return sems[-1]

        NT, rows, H = TOK_TILES, TILE_ROWS, HEADS
        at = [slice(128 * t, 128 * t + rows[t]) for t in range(NT)]
        resid, ident, ones = m["resid"], m["ident"], m["ones"]
        ss = sb("ss", [128, NT])
        gains = sb("gains", [128, 2, KT])
        XK = sb("XK", [128, 2, KT, T_ALL])
        kvq = [sb(n, [128, NT, D_MODEL]) for n in ("k", "v", "q")]
        k_t, v_t, q_t = kvq
        rot = sb("rot", [128, 512])
        rot2 = sb("rot2", [128, 512])
        lam_in = sb("lam_in", [128, 4, DH])
        lam = sb("lam", [128, 4])
        coef = sb("coef", [128, 1])
        pages = sb("pages", [1, DEC_BATCH * N_PAGES], I32)
        subln = sb("subln", [128, 1])
        qTd = sb("qTd", [128, H, T_DEC])
        QBs = sb("QBs", [128, 2, H, 64])
        P = sb("P", [128, SCORES * 2])
        aT = sb("aT", [128, 3, 128])
        mx = sb("mx", [128, 4])
        sm = sb("sm", [128, 4])
        o_ss = sb("o_ss", [128, 2, H])
        oT = sb("oT", [128, H, T_ALL])
        qk_h = sb("qk_h", [128, 2, 2, 128])
        qkT = sb("qkT", [128, 2, 256])
        o_t = q_t
        flat = [m["ring"][n][:].rearrange("p a n -> p (a n)") for n in range(3)]
        wslot = [flat[0][:, 0:4096], flat[0][:, 4096:], flat[1][:, 0:4096]]
        wslot = [w.rearrange("p (k n) -> p k n", k=KT) for w in wslot]
        xh = flat[2][:, 0:1024]
        sq = flat[2][:, 1024:2048]
        QB = flat[1][:, 4096:].rearrange("p (b h r) -> p b h r", b=DEC_BATCH, h=H)
        Kc = flat[2][:, 0:4096].rearrange("p (b i n) -> p b i n", b=2, i=N_PAGES)
        Vc = flat[2][:, 4096:].rearrange("p (b i n) -> p b i n", b=2, i=N_PAGES)
        w_out = flat[0].rearrange("p (h n) -> p h n", h=H)
        o_sq = P[:, 0:512]

        B = [ctx.enter_context(nc.psum_tensor(f"at_bank{i}", [128, 512], F32)) for i in range(2)]
        BB = ctx.enter_context(nc.psum_tensor("at_pair", [128, 2, 512], F32))
        B += [None, None] + [ctx.enter_context(nc.psum_tensor(f"at_bank{i}", [128, 512], F32)) for i in range(4, 8)]
        B[2], B[3] = BB[:, 0, :], BB[:, 1, :]

        s = {n: sem(n) for n in (
            "consts_in w0_in w1_in w2_in squares mean_made roots xh_made xT_made xT_kept lam_in lam_out kv_made kv_kept rotated q_rotated stored "
            "dT_made dT_kept QB_clear QB_made K0_in V0_in KT_made KT_kept QBs_made S_made S_kept S_exp a_made aT_made aT_kept od_made od_kept "
            "od_sq od_sum od_root od_done sliced qk_T qkT_kept sc_made sc_kept sc_exp pa_made paT_made paT_kept o_made o_kept on_sq on_root on_made onT_made onT_kept "
            "wout_in out_made out_kept v").split()}
        w_kv = m["w_kv"].rearrange("(p t) n -> p t n", t=KT)
        w_q = m["w_q_b"][0].rearrange("(p t) n -> p t n", t=KT)
        w_src = [w_kv[:, :, 0:D_MODEL], w_kv[:, :, D_MODEL:], w_q]
        slot_in = [s["w0_in"], s["w1_in"], s["w2_in"]]
        outs = [(m["k_prompt"][0].rearrange("l h e -> l (h e)"), m["k_sample"].rearrange("b l h e -> (b l) (h e)")),
                (m["v_prompt"][0].rearrange("l h e -> l (h e)"), m["v_sample"].rearrange("b l h e -> (b l) (h e)"))]
        caches = [m["cache_k"].rearrange("n s h e -> s n (h e)"), m["cache_v"].rearrange("n s h e -> s n (h e)")]
        PAIRS = DEC_BATCH // 2

        def kbank(t):
            return (B[0], B[1], B[2])[t]

        def vbank(t):
            return (B[3], B[4], B[5])[t]

        def qbank(t):
            return (B[6], B[7], B[0])[t]

        block = ctx.enter_context(nc.Block())

        @block.sync
        def _(sp):
            sp.dma_start(gains[:, 0, :], m["kv_norm"].rearrange("(p t) -> p t", t=KT)).then_inc(s["consts_in"], 16)
            sp.dma_start(gains[:, 1, :], m["norm_b"][0].rearrange("(p t) -> p t", t=KT)).then_inc(s["consts_in"], 16)
            sp.dma_start(lam_in[:].rearrange("p a d -> p (a d)"), m["lam_b"].rearrange("a l d -> a (l d)").broadcast_to([128, 4 * DH])).then_inc(s["consts_in"], 16)
            sp.dma_start(subln[:], m["subln_b"].rearrange("a v -> v a")).then_inc(s["consts_in"], 16)
            sp.dma_start(pages[:], m["page_table"].rearrange("(a b) i -> a (b i)", a=1)).then_inc(s["consts_in"], 16)

            def weights(half, first=False):
                for j in range(3):
                    if not first:
                        sp.wait_ge(s["kv_made"], 9 * half - 6 + 3 * j)
                    sp.dma_start(wslot[j], w_src[j][:, :, 512 * half:512 * half + 512]).then_inc(slot_in[j], 16)

            weights(0, True)
            weights(1)
            for j in range(2):
                for t in range(NT):
                    sp.wait_ge((s["rotated"], s["kv_kept"])[j], 6)
                    dst = outs[j][0][at[t], :] if t < 2 else outs[j][1]
                    sp.dma_start(dst, kvq[j][0:rows[t], t, :]).then_inc(s["stored"], 16)

            def cache(j, pair, later):
                for b in range(2):
                    for i in range(N_PAGES):
                        page = sp.value_load(pages[0:1, bass.ds(4 * pair + 2 * b + i, 1)], min_val=0, max_val=N_PHYS - 1)
                        if later and b == 0 and i == 0:
                            if j == 0:
                                sp.wait_ge(s["KT_made"], 8 * pair)
                            else:
                                sp.wait_ge(s["od_made"], pair)
                        dst = (Kc, Vc)[j][:, b, i, :]
                        sp.dma_start(dst, caches[j][:, bass.ds(page, 1), :].rearrange("s o n -> s (o n)")).then_inc((s["K0_in"], s["V0_in"])[j], 16)

            sp.wait_ge(s["consts_in"], 16 * 5)
            sp.wait_ge(s["xT_made"], 2 * NT)
            cache(0, 0, False)
            cache(1, 0, False)
            with sp.Fori(1, PAIRS) as pair:
                cache(0, pair, True)
                cache(1, pair, True)
            sp.wait_ge(s["kv_made"], 18)
            sp.dma_start(w_out, m["w_out_b"][0].rearrange("(h p) n -> p h n", p=128)).then_inc(s["wout_in"], 16)
            sp.wait_ge(s["QBs_made"], PAIRS)
            m["prefetch"](sp, 1, (1,))
            sp.wait_ge(s["od_made"], PAIRS)
            m["prefetch"](sp, 1, (2,))
            sp.wait_ge(s["stored"], 16 * 2 * NT)
            sp.wait_ge(s["out_made"], 2 * NT)
            m["prefetch"](sp, 1, (0,))

        @block.gpsimd
        def _(pool):
            nc.gpsimd.memset(QB[:, :, :, :], 0.0).then_inc(s["QB_clear"], 1)
            pool.wait_ge(s["QB_made"], 2 * H)

            with pool.Fori(0, PAIRS) as pair:
                pool.wait_ge(s["S_made"], pair)
                nc.gpsimd.tensor_copy(QBs[:, :, :, :], QB[:, bass.ds(2 * pair, 2), :, :]).then_inc(s["QBs_made"], 1)

            def cut(h):
                pool.wait_ge(s["qk_T"], h)
                nc.gpsimd.tensor_copy(qk_h[:, 0, :, :], q_t[:, 0:2, bass.ds(128 * h, 128)]).then_inc(s["sliced"], 1)
                nc.gpsimd.tensor_copy(qk_h[:, 1, :, :], k_t[:, 0:2, bass.ds(128 * h, 128)]).then_inc(s["sliced"], 1)

            with pool.Fori(0, H) as h:
                cut(h)

        @block.scalar
        def _(act):
            A = nc.scalar
            act.wait_ge(s["squares"], 1)
            for t in range(NT):
                r = rows[t]
                A.activation(sq[0:r, :], resid[0:r, t, :], ACT.Square, accum_out=ss[0:r, t:t + 1]).then_inc(s["squares"], 1)
                act.wait_ge(s["squares"], t + 2)
            act.wait_ge(s["mean_made"], 1)
            A.activation(ss[:, :], ss[:, :], ACT.Sqrt).then_inc(s["roots"], 1)
            act.wait_ge(s["lam_in"], 1)
            A.activation(lam[:, 0:2], lam[:, 0:2], ACT.Exp).then_inc(s["lam_out"], 1)
            for half in range(2):
                for t in range(NT):
                    act.wait_ge(s["kv_made"], 9 * half + 3 + t + 1)
                    A.copy(v_t[0:rows[t], t, 512 * half:512 * half + 512], vbank(t)[0:rows[t], :]).then_inc(s["kv_kept"], 1)
            act.wait_ge(s["dT_made"], 1)
            A.copy(qTd[:, :, :], B[4][:, 0:256].rearrange("p (h r) -> p h r", h=H)).then_inc(s["dT_kept"], 1)
            for b in range(2):
                A.copy(XK[:, b, :, PAST_LEN:], B[5][:, 0:256].rearrange("p (h r) -> p h r", h=H)).then_inc(s["dT_kept"], 1)
            with act.Fori(0, PAIRS) as pair:
                for b in range(2):
                    for j in (1, 3):
                        act.wait_ge(s["KT_made"], 8 * pair + 4 * b + j + 1)
                        if b == 0 and j == 1:
                            act.wait_ge(s["S_made"], pair)
                        A.copy(XK[:, b, 2 * j:2 * j + 2, 0:PAST_LEN], B[4 + j][:, :].rearrange("p (h r) -> p h r", h=2)).then_inc(s["KT_kept"], 1)
                act.wait_ge(s["S_kept"], pair + 1)
                A.activation(P[:, 0:T_ALL], P[:, 0:T_ALL], ACT.Exp, bias=mx[:, 1:2], scale=DH ** -0.5, accum_out=sm[:, 0:1]).then_inc(s["S_exp"], 1)
            act.wait_ge(s["od_sum"], 1)
            A.activation(rot[:, 0:256], B[0][:, 0:256], ACT.Sqrt, scale=1.0 / DK, bias=m["eps"][:, 0:1]).then_inc(s["od_root"], 1)

            def turned(h):
                act.wait_ge(s["qk_T"], h + 1)
                A.copy(qkT[:, 0, :], B[4][:, 0:256]).then_inc(s["qkT_kept"], 1)
                A.copy(qkT[:, 1, :], B[4][:, 256:512]).then_inc(s["qkT_kept"], 1)

            def head(h, more):
                act.wait_ge(s["sc_kept"], h + 1)
                for t in range(2):
                    for c in range(2):
                        lo = SCORES * c + 128 * t
                        n = 128 * (t + 1)
                        A.activation(P[:, lo:lo + n], P[:, lo:lo + n], ACT.Exp, bias=mx[:, 2 * t + c:2 * t + c + 1],
                                     scale=DH ** -0.5, accum_out=sm[:, 2 * t + c:2 * t + c + 1]).then_inc(s["sc_exp"], 1)
                if more:
                    turned(h + 1)
                act.wait_ge(s["paT_made"], h + 1)
                A.copy(aT[:, :, :], B[6][:, 0:384].rearrange("p (j r) -> p j r", j=3)).then_inc(s["paT_kept"], 1)
                act.wait_ge(s["o_made"], h + 1)
                A.copy(o_t[:, 0:2, bass.ds(128 * h, 128)], B[7][:, 0:256].rearrange("p (t e) -> p t e", t=2)).then_inc(s["o_kept"], 1)

            turned(0)
            with act.Fori(0, H - 1) as h:
                head(h, True)
            head(H - 1, False)
            act.wait_ge(s["on_sq"], 1)
            A.activation(o_ss[:, :, :], o_ss[:, :, :], ACT.Sqrt, scale=1.0 / DK, bias=m["eps"][:, 0:1]).then_inc(s["on_root"], 1)
            for t in range(2):
                for j in range(2):
                    act.wait_ge(s["onT_made"], 2 * t + j + 1)
                    A.activation(oT[:, 4 * j:4 * j + 4, at[t]], B[2 * t + j][:, :].rearrange("p (h r) -> p h r", h=4), ACT.Copy, scale=subln[:, 0:1]).then_inc(s["onT_kept"], 1)

        @block.vector
        def _(dve):
            V = nc.vector
            st = {"base": 0, "n": 0}

            def link(ins):
                st["n"] += 1
                ins.then_inc(s["v"], 1)
                dve.wait_ge(s["v"], st["base"] + st["n"])

            V.memset(ss[:], 1.0).then_inc(s["squares"], 1)
            dve.wait_ge(s["consts_in"], 16 * 5)
            for j in range(2):
                link(V.tensor_tensor(lam_in[:, 2 * j, :], lam_in[:, 2 * j, :], lam_in[:, 2 * j + 1, :], ALU.mult))
                ins = V.tensor_reduce(lam[:, j:j + 1], lam_in[:, 2 * j, :], AX.X, ALU.add)
                ins.then_inc(s["lam_in"], 1) if j else link(ins)
            dve.wait_ge(s["squares"], NT + 1)
            V.tensor_scalar(ss[:, :], ss[:, :], 1.0 / D_MODEL, EPS, ALU.mult, ALU.add).then_inc(s["mean_made"], 1)
            dve.wait_ge(s["roots"], 1)
            link(V.reciprocal(ss[:, :], ss[:, :]))
            for t in range(NT):
                r = rows[t]
                if t:
                    dve.wait_ge(s["xT_made"], 2 * t)
                V.tensor_scalar(xh[0:r, :], resid[0:r, t, :], ss[0:r, t:t + 1], None, ALU.mult).then_inc(s["xh_made"], 1)
                for j in range(2):
                    dve.wait_ge(s["xT_made"], 2 * t + j + 1)
                    for x in range(2):
                        V.tensor_tensor(XK[:, x, 4 * j:4 * j + 4, at[t]], B[j][:, :].rearrange("p (k r) -> p k r", k=4)[:, :, 0:r],
                                        gains[:, x, 4 * j:4 * j + 4].unsqueeze(2).broadcast_to([128, 4, r]), ALU.mult).then_inc(s["xT_kept"], 1)
            dve.wait_ge(s["lam_out"], 1)
            link(V.tensor_tensor(lam[:, 2:3], lam[:, 1:2], lam[:, 0:1], ALU.subtract))
            link(V.tensor_scalar(lam[:, 2:3], lam[:, 2:3], -LAM_INIT, None, ALU.add))
            link(V.scalar_tensor_tensor(coef[:, :], m["second_half"][:, :], lam[:, 2:3], m["first_half"][:, :], ALU.mult, ALU.add))
            link(V.tensor_scalar(subln[:, :], subln[:, :], 1.0 - LAM_INIT, None, ALU.mult))

            def rotate(half, dst, bank, t):
                r = rows[t]
                G = 512 // DH
                x = bank[0:r, :].rearrange("p (g a d) -> p g a d", g=G, a=2)
                c, sn = (a[0:r, t, :].unsqueeze(1).broadcast_to([r, G, DH // 2]) for a in (m["cos"], m["sin"]))
                y = rot[0:r, :].rearrange("p (g a d) -> p g a d", g=G, a=2)
                z = rot2[0:r, :].rearrange("p (g a d) -> p g a d", g=G, a=2)
                o = dst[0:r, t, 512 * half:512 * half + 512].rearrange("p (g a d) -> p g a d", g=G, a=2)
                for a in range(2):
                    V.tensor_tensor(y[:, :, a, :], x[:, :, a, :], c, ALU.mult)
                    last = V.tensor_tensor(z[:, :, a, :], x[:, :, 1 - a, :], sn, ALU.mult)
                    if a:
                        link(last)
                V.tensor_tensor(o[:, :, 0, :], y[:, :, 0, :], z[:, :, 0, :], ALU.subtract)
                V.tensor_tensor(o[:, :, 1, :], y[:, :, 1, :], z[:, :, 1, :], ALU.add).then_inc(s["rotated"] if dst is k_t else s["q_rotated"], 1)

            for half in range(2):
                for j, (dst, bank, done) in enumerate(((k_t, kbank, s["rotated"]), (q_t, qbank, s["q_rotated"]))):
                    for t in range(NT):
                        dve.wait_ge(s["kv_made"], 9 * half + 6 * j + t + 1)
                        rotate(half, dst, bank(t), t)
                        dve.wait_ge(done, 3 * half + t + 1)
            dve.wait_ge(s["dT_kept"], 3)
            dve.wait_ge(s["QB_clear"], 1)
            for c in range(2):
                for h in range(H):
                    V.tensor_copy(QB[64 * c:64 * c + 64, :, h, 32 * c + 4 * h:32 * c + 4 * h + 4],
                                  qTd[64 * c:64 * c + 64, h, :].rearrange("p (b q) -> p b q", q=DEC_SEQ)).then_inc(s["QB_made"], 1)
            pre = st["n"]
            with dve.Fori(0, PAIRS) as pair:
                st["base"], st["n"] = pair * S_STEPS + pre, 0
                for b in range(2):
                    for j in (0, 2):
                        dve.wait_ge(s["KT_made"], 8 * pair + 4 * b + j + 1)
                        if b == 0 and j == 0:
                            dve.wait_ge(s["S_made"], pair)
                        V.tensor_copy(XK[:, b, 2 * j:2 * j + 2, 0:PAST_LEN], B[4 + j][:, :].rearrange("p (h r) -> p h r", h=2)).then_inc(s["KT_kept"], 1)
                dve.wait_ge(s["S_made"], pair + 1)
                dve.wait_ge(s["aT_made"], pair)
                link(V.tensor_copy(P[:, 0:PAST_LEN], B[0][:, 0:PAST_LEN]))
                link(V.tensor_tensor(P[:, PAST_LEN:T_ALL], B[0][:, PAST_LEN:T_ALL], m["new_keys"][:, bass.ds(pair, 1), :].rearrange("p o k -> p (o k)"), ALU.add))
                link(V.tensor_reduce(mx[:, 0:1], P[:, 0:T_ALL], AX.X, ALU.max))
                V.tensor_scalar(mx[:, 1:2], mx[:, 0:1], -(DH ** -0.5), None, ALU.mult).then_inc(s["S_kept"], 1)
                dve.wait_ge(s["S_exp"], pair + 1)
                link(V.reciprocal(sm[:, 1:2], sm[:, 0:1]))
                link(V.tensor_tensor(sm[:, 1:2], sm[:, 1:2], coef[:, :], ALU.mult))
                V.tensor_scalar(P[:, 0:T_ALL], P[:, 0:T_ALL], sm[:, 1:2], None, ALU.mult).then_inc(s["a_made"], 1)
                dve.wait_ge(s["aT_made"], pair + 1)
                dve.wait_ge(s["od_made"], pair)
                V.tensor_copy(aT[:, 0:2, 0:64], B[1][:, 0:128].rearrange("p (i r) -> p i r", i=2)).then_inc(s["aT_kept"], 1)
                V.tensor_copy(aT[0:T_DEC, 2, 0:64], B[1][0:T_DEC, 128:192]).then_inc(s["aT_kept"], 1)
                dve.wait_ge(s["od_made"], pair + 1)
                V.tensor_copy(oT[:, :, bass.ds(8 * pair + SEQ, 8)], B[2][:, 0:64].rearrange("p (h r) -> p h r", h=H)).then_inc(s["od_kept"], 1)
                assert st["n"] == S_STEPS, st["n"]
            st["base"], st["n"] = PAIRS * S_STEPS + pre, 0
            dve.wait_ge(s["od_kept"], PAIRS)
            V.tensor_tensor(rot2[:, 0:256].rearrange("p (h r) -> p h r", h=H), oT[:, :, SEQ:], oT[:, :, SEQ:], ALU.mult).then_inc(s["od_sq"], 1)
            dve.wait_ge(s["od_root"], 1)
            link(V.reciprocal(rot[:, 0:256], rot[:, 0:256]))
            link(V.scalar_tensor_tensor(oT[:, :, SEQ:], rot[:, 0:256].rearrange("p (h r) -> p h r", h=H), subln[:, 0:1], oT[:, :, SEQ:], ALU.mult, ALU.mult))
            pre = PAIRS * S_STEPS + pre + st["n"]

            def head(h, more):
                dve.wait_ge(s["sc_made"], h + 1)
                dve.wait_ge(s["paT_made"], h)
                link(V.tensor_tensor(P[:, :].rearrange("p (c n) -> p c n", c=2), BB[:, :, 0:SCORES], m["causal"][:, :].unsqueeze(1).broadcast_to([128, 2, SCORES]), ALU.add))
                for t in range(2):
                    v = P[:, :].rearrange("p (c n) -> p c n", c=2)[:, :, 128 * t:128 * t + 128 * (t + 1)]
                    link(V.tensor_reduce(mx[:, 2 * t:2 * t + 2], v, AX.X, ALU.max))
                V.tensor_scalar(mx[:, :], mx[:, :], -(DH ** -0.5), None, ALU.mult).then_inc(s["sc_kept"], 1)
                dve.wait_ge(s["sc_exp"], 4 * h + 4)
                link(V.reciprocal(sm[:, :], sm[:, :]))
                link(V.tensor_scalar(sm[:, 1:2], sm[:, 1:2], lam[:, 2:3], None, ALU.mult))
                link(V.tensor_scalar(sm[:, 3:4], sm[:, 3:4], lam[:, 2:3], None, ALU.mult))
                for t in range(2):
                    lo, n = 128 * t, 128 * (t + 1)
                    p0, p1 = P[:, lo:lo + n], P[:, SCORES + lo:SCORES + lo + n]
                    link(V.tensor_scalar(p1, p1, sm[:, 2 * t + 1:2 * t + 2], None, ALU.mult))
                    ins = V.scalar_tensor_tensor(p0, p0, sm[:, 2 * t:2 * t + 1], p1, ALU.mult, ALU.add)
                    ins.then_inc(s["pa_made"], 1)

            with dve.Fori(0, H - 1) as h:
                st["base"], st["n"] = h * P_STEPS + pre, 0
                head(h, True)
                assert st["n"] == P_STEPS, st["n"]
            st["base"], st["n"] = (H - 1) * P_STEPS + pre, 0
            head(H - 1, False)
            dve.wait_ge(s["o_kept"], H)
            for t in range(2):
                for j in range(2):
                    v = o_t[:, t, 512 * j:512 * j + 512]
                    link(V.tensor_tensor(o_sq, v, v, ALU.mult))
                    ins = V.tensor_reduce(o_ss[:, t, 4 * j:4 * j + 4], o_sq.rearrange("p (h e) -> p h e", h=4), AX.X, ALU.add)
                    ins.then_inc(s["on_sq"], 1) if t and j else link(ins)
            dve.wait_ge(s["on_root"], 1)
            link(V.reciprocal(o_ss[:], o_ss[:]))
            for t in range(2):
                v = o_t[:, t, :].rearrange("p (h e) -> p h e", h=H)
                V.tensor_tensor(v, v, o_ss[:, t, :].unsqueeze(2).broadcast_to([128, H, 128]), ALU.mult).then_inc(s["on_made"], 1)
            for t in range(NT):
                r = rows[t]
                for j in range(2):
                    dve.wait_ge(s["out_made"], 2 * t + j + 1)
                    V.tensor_tensor(resid[0:r, t, 512 * j:512 * j + 512], resid[0:r, t, 512 * j:512 * j + 512], B[4 + j][0:r, :], ALU.add).then_inc(s["out_kept"], 1)
            dve.wait_ge(s["out_kept"], 2 * NT)

        @block.tensor
        def _(pe):
            T = nc.tensor
            xv = xh.rearrange("p (c k) -> p k c", k=KT)
            for t in range(NT):
                r = rows[t]
                pe.wait_ge(s["xh_made"], t + 1)
                if t:
                    pe.wait_ge(s["xT_kept"], 4 * t)
                for k in range(KT):
                    last = T.transpose(B[k // 4][:, 128 * (k % 4):128 * (k % 4) + r], xv[0:r, k, :], ident[0:r, 0:r])
                    if k % 4 == 3:
                        last.then_inc(s["xT_made"], 1)
            pe.wait_ge(s["xT_kept"], 4 * NT)
            for half in range(2):
                for j in range(3):
                    pe.wait_ge(slot_in[j], 16 * half + 16)
                    for t in range(NT):
                        if half:
                            if j == 0:
                                pe.wait_ge(s["q_rotated"] if t == 0 else s["rotated"], 3)
                            elif j == 1:
                                pe.wait_ge(s["kv_kept"], t + 1)
                            else:
                                pe.wait_ge(s["q_rotated"], 3)
                        if j == 2 and t == 2:
                            pe.wait_ge(s["rotated"], 3 * half + 1)
                        bank = (kbank, vbank, qbank)[j](t)
                        for k in range(KT):
                            last = T.matmul(bank[0:rows[t], :], XK[:, 0 if j < 2 else 1, k, at[t]], wslot[j][:, k, :], start=(k == 0), stop=(k == KT - 1))
                        last.then_inc(s["kv_made"], 1)
            pe.wait_ge(s["q_rotated"], 6)
            pe.wait_ge(s["rotated"], 6)
            pe.wait_ge(s["kv_kept"], 6)
            for j, src in ((4, q_t), (5, k_t)):
                for h in range(H):
                    last = T.transpose(B[j][:, 32 * h:32 * h + 32], src[0:T_DEC, 2, 128 * h:128 * h + 128], ident[0:T_DEC, 0:T_DEC])
            last.then_inc(s["dT_made"], 1)
            pe.wait_ge(s["dT_kept"], 3)
            with pe.Fori(0, PAIRS) as pair:
                pe.wait_ge(s["K0_in"], 64 * pair + 64)
                for b in range(2):
                    for j in range(4):
                        if b == 0:
                            pe.wait_ge(s["KT_kept"], 8 * pair)
                        elif j == 0:
                            pe.wait_ge(s["KT_kept"], 8 * pair + 4)
                        for h in range(2):
                            for i in range(N_PAGES):
                                last = T.transpose(B[4 + j][:, 256 * h + 128 * i:256 * h + 128 * i + 128],
                                                   Kc[:, b, i, 128 * (2 * j + h):128 * (2 * j + h) + 128], ident[:, :])
                        last.then_inc(s["KT_made"], 1)
                pe.wait_ge(s["KT_kept"], 8 * pair + 8)
                pe.wait_ge(s["S_kept"], pair)
                pe.wait_ge(s["QBs_made"], pair + 1)
                for h in range(H):
                    for b in range(2):
                        last = T.matmul(B[0][64 * b:64 * b + 64, 0:T_ALL], QBs[:, b, h, :], XK[:, b, h, :], start=(h == 0), stop=(h == H - 1))
                last.then_inc(s["S_made"], 1)
                pe.wait_ge(s["a_made"], pair + 1)
                T.matmul(B[1][:, 0:64], P[:, 0:128], m["halves"][:, :], start=True, stop=True)
                T.matmul(B[1][:, 64:128], P[:, 128:256], m["halves"][:, :], start=True, stop=True)
                T.matmul(B[1][0:T_DEC, 128:192], P[:, 256:T_ALL], m["halves"][:, :], start=True, stop=True).then_inc(s["aT_made"], 1)
                pe.wait_ge(s["aT_kept"], 2 * pair + 2)
                pe.wait_ge(s["V0_in"], 64 * pair + 64)
                pe.wait_ge(s["od_kept"], pair)
                for b in range(2):
                    for h in range(H):
                        out = B[2][:, 8 * h + 4 * b:8 * h + 4 * b + 4]
                        c = 32 * b + 4 * h
                        for i in range(N_PAGES):
                            T.matmul(out, Vc[:, b, i, 128 * h:128 * h + 128], aT[:, i, c:c + 4], start=(i == 0), stop=False)
                        last = T.matmul(out, v_t[0:T_DEC, 2, 128 * h:128 * h + 128], aT[0:T_DEC, 2, c:c + 4], start=False, stop=True)
                last.then_inc(s["od_made"], 1)
            pe.wait_ge(s["od_sq"], 1)
            T.matmul(B[0][:, 0:256], ones[:, :], rot2[:, 0:256], start=True, stop=True).then_inc(s["od_sum"], 1)

            def turn(h):
                pe.wait_ge(s["sliced"], 2 * h + 2)
                pe.wait_ge(s["qkT_kept"], 2 * h)
                for j in range(2):
                    for t in range(2):
                        last = T.transpose(B[4][:, 256 * j + 128 * t:256 * j + 128 * t + 128], qk_h[:, j, t, :], ident[:, :])
                last.then_inc(s["qk_T"], 1)

            def head(h, more):
                pe.wait_ge(s["qkT_kept"], 2 * h + 2)
                pe.wait_ge(s["sc_kept"], h)
                for t in range(2):
                    for c in range(2):
                        lane = slice(64 * c, 64 * c + 64)
                        last = T.matmul(BB[:, c, 128 * t:128 * t + 128 * (t + 1)], qkT[lane, 0, 128 * t:128 * t + 128], qkT[lane, 1, 0:128 * (t + 1)],
                                        start=True, stop=True)
                last.then_inc(s["sc_made"], 1)
                if more:
                    turn(h + 1)
                pe.wait_ge(s["pa_made"], 2 * h + 2)
                pe.wait_ge(s["paT_kept"], h)
                for j, lo in enumerate((0, 128, 256)):
                    last = T.transpose(B[6][:, 128 * j:128 * j + 128], P[:, lo:lo + 128], ident[:, :])
                last.then_inc(s["paT_made"], 1)
                pe.wait_ge(s["paT_kept"], h + 1)
                pe.wait_ge(s["o_kept"], h)
                e = bass.ds(128 * h, 128)
                T.matmul(B[7][:, 0:128], aT[:, 0, :], v_t[:, 0, e], start=True, stop=True)
                T.matmul(B[7][:, 128:256], aT[:, 1, :], v_t[:, 0, e], start=True, stop=False)
                T.matmul(B[7][:, 128:256], aT[:, 2, :], v_t[:, 1, e], start=False, stop=True).then_inc(s["o_made"], 1)

            turn(0)
            with pe.Fori(0, H - 1) as h:
                head(h, True)
            head(H - 1, False)
            for t in range(2):
                pe.wait_ge(s["on_made"], t + 1)
                for j in range(2):
                    for h in range(4):
                        last = T.transpose(B[2 * t + j][:, 128 * h:128 * h + 128], o_t[:, t, 128 * (4 * j + h):128 * (4 * j + h) + 128], ident[:, :])
                    last.then_inc(s["onT_made"], 1)
            pe.wait_ge(s["onT_kept"], 4)
            pe.wait_ge(s["wout_in"], 16)
            for t in range(NT):
                if t:
                    pe.wait_ge(s["out_kept"], 2 * t)
                for j in range(2):
                    for h in range(H):
                        last = T.matmul(B[4 + j][0:rows[t], :], oT[:, h, at[t]], w_out[:, h, 512 * j:512 * j + 512], start=(h == 0), stop=(h == H - 1))
                    last.then_inc(s["out_made"], 1)

    nc.clear_and_free_semaphores(sems)
    nc.all_engine_barrier(sem_only=True)


def moe_phase(nc, m, layer):
    ctx, sems = ExitStack(), []
    with ctx:
        def sb(name, shape, dt=F32):
            return ctx.enter_context(nc.sbuf_tensor(f"moe{layer}_{name}", shape, dt))

        def pb(name, shape, dt=F32):
            return ctx.enter_context(nc.psum_tensor(f"moe{layer}_{name}", shape, dt))

        def sem(name):
            sems.append(nc.alloc_semaphore(f"moe{layer}_{name}"))
            return sems[-1]

        NT = TOK_TILES
        rows = TILE_ROWS
        resid, ident = m["resid"], m["ident"]
        norm_b = sb("norm_b", [128, D_MODEL])
        w_router = sb("w_router", [128, KT, N_GROUPS + N_EXPERTS])
        b_router = sb("b_router", [128, N_GROUPS + N_EXPERTS])
        xn = sb("xn", [128, NT, D_MODEL])
        xnT = sb("xnT", [128, KT, 128])
        logits = sb("logits", [128, NT, N_GROUPS + N_EXPERTS])
        sq = sb("sq", [128, D_MODEL])
        ss = sb("ss", [128, NT])
        rstd = sb("rstd", [128, NT])
        gmax = sb("gmax", [128, NT])
        gexp = sb("gexp", [128, NT, N_GROUPS])
        gsum = sb("gsum", [128, NT])
        gpick = sb("gpick", [128, NT, N_GROUPS])
        gbest = sb("gbest", [128, NT])
        masked = sb("masked", [128, NT, N_EXPERTS])
        etmp = sb("etmp", [128, NT, N_EXPERTS])
        ebest = sb("ebest", [128, NT])
        top = sb("top", [128, TOP_K, NT])
        oneh = sb("oneh", [128, TOP_K, NT, N_EXPERTS])
        both = sb("both", [128, NT, N_EXPERTS])
        gate = sb("gate", [128, TOP_K, NT])
        ratio = sb("ratio", [128, NT])
        rank = sb("rank", [128, NT, N_EXPERTS])
        counts = sb("counts", [128, N_EXPERTS])
        nover = sb("nover", [128, N_EXPERTS])
        cend = sb("cend", [128, N_EXPERTS])
        cstart = sb("cstart", [128, N_EXPERTS])
        rk = sb("rk", [128, TOP_K, NT])
        inmain = sb("inmain", [128, TOP_K, NT])
        lmain = sb("lmain", [128, TOP_K, NT])
        opos = sb("opos", [128, TOP_K, NT])
        oge = sb("oge", [128, TOP_K, NT, OVER_GROUPS + 1])
        olow = sb("olow", [128, TOP_K, NT])
        lpos = sb("lpos", [128, TOP_K, NT])
        colhot = sb("colhot", [128, TOP_K, NT, N_COLS])
        entry = sb("entry", [128, TOP_K, NT, 2, N_COLS])
        place = sb("place", [128, TOP_K, NT, 128])
        tabf = sb("tabf", [128, 2, N_COLS])
        tabz = sb("tabz", [128, 2, N_COLS])
        table = sb("table", [128, 2, N_COLS], U32)
        obf = sb("obf", [1, 2 * OVER_GROUPS, N_EXPERTS])
        obf2 = sb("obf2", [1, 2 * OVER_GROUPS, N_EXPERTS])
        ovalf = sb("ovalf", [1, 2 * OVER_GROUPS + 2])
        ngf = sb("ngf", [1, 4])
        steer = sb("steer", [1, 2 * OVER_GROUPS + 2], I32)
        xg = sb("xg", [128, D_MODEL])
        xgT = sb("xgT", [128, KT, 128])
        silu = sb("silu", [128, D_FF_EXPERT])
        hid = sb("hid", [128, D_FF_EXPERT])
        hidT = sb("hidT", [128, FT, 128])
        y_sb = sb("y_sb", [128, D_MODEL])
        rows_in = sb("rows_in", [128, 1], U32)
        rows_out = sb("rows_out", [128, 1], U32)

        ps_x = pb("ps_x", [128, 2, 4, 128])
        ps_gate = pb("ps_gate", [128, D_FF_EXPERT])
        ps_up = pb("ps_up", [128, D_FF_EXPERT])
        ps_hid = pb("ps_hid", [128, FT, 128])
        ps_y = pb("ps_y", [128, 2, 512])
        ps_rank = ps_gate[:, 0:NT * N_EXPERTS].rearrange("p (a e) -> p a e", a=NT)
        ps_count = ps_gate[:, NT * N_EXPERTS:NT * N_EXPERTS + N_EXPERTS]
        ps_tab = ps_up[:, 0:2 * N_COLS]
        ps_log = ps_hid[:, 0, 0:N_GROUPS + N_EXPERTS]

        consts_in = sem("consts_in")
        squares = sem("squares")
        roots = sem("roots")
        normed = sem("normed")
        xn_stored = sem("xn_stored")
        xT_made = sem("xT_made")
        xT_kept = sem("xT_kept")
        logits_made = sem("logits_made")
        logits_kept = sem("logits_kept")
        gdiff = sem("gdiff")
        gexped = sem("gexped")
        tdiff = sem("tdiff")
        texped = sem("texped")
        hots = sem("hots")
        ranked = sem("ranked")
        placed = sem("placed")
        tabbed = sem("tabbed")
        table_ready = sem("table_ready")
        vchain = sem("vchain")
        cleared = sem("cleared")
        weights_in = m["weights_of"][layer]
        weights_used = [sem(f"{n}_products") for n in ("gate", "up", "down")]
        gate_made, up_made, y_made = weights_used
        gathered = sem("gathered")
        gx_T = sem("gx_T")
        gx_kept = sem("gx_kept")
        silued = sem("silued")
        hidden = sem("hidden")
        hid_T = sem("hid_T")
        hid_kept = sem("hid_kept")
        y_kept = sem("y_kept")
        scattered = sem("scattered")
        y_back = sem("y_back")
        scattered_all = sem("scattered_all")
        mean_made = sem("mean_made")
        ss_cleared = sem("ss_cleared")
        waits_held = sem("waits_held")
        in_copied = sem("in_copied")
        out_copied = sem("out_copied")
        xn_dram, y_dram = m["xn_dram"], m["y_dram"][layer]
        y_rows = y_dram.rearrange("(t k) d -> t k d", k=TOP_K)
        ring = m["ring"]
        W = m["expert_views"][layer]

        block = ctx.enter_context(nc.Block())

        @block.sync
        def _(sp):
            sp.dma_start(norm_b[:], m["norm_m"][layer:layer + 1, :].broadcast_to([128, D_MODEL])).then_inc(consts_in, 16)
            sp.dma_start(w_router[:, :, 0:N_GROUPS], m["w_rg"][layer].rearrange("(p t) n -> p t n", t=KT)).then_inc(consts_in, 16)
            sp.dma_start(w_router[:, :, N_GROUPS:], m["w_re"][layer].rearrange("(p t) n -> p t n", t=KT)).then_inc(consts_in, 16)
            sp.dma_start(b_router[:, 0:N_GROUPS], m["b_rg"][layer:layer + 1, :].broadcast_to([128, N_GROUPS])).then_inc(consts_in, 16)
            sp.dma_start(b_router[:, N_GROUPS:], m["b_re"][layer:layer + 1, :].broadcast_to([128, N_EXPERTS])).then_inc(consts_in, 16)
            sp.wait_ge(normed, NT)
            for t in range(NT):
                sp.dma_start(xn_dram[128 * t:128 * t + rows[t], :], xn[0:rows[t], t, :]).then_inc(xn_stored, 16)
            with sp.Fori(1, MAIN_GROUPS) as g:
                for n in range(3):
                    sp.wait_ge(weights_used[n], g)
                    for e in range(2):
                        sp.dma_start(ring[n][:, e:e + 1, :], W[n][:, bass.ds(2 * g + e, 1), :]).then_inc(weights_in[n][e], 16)
            sp.wait_ge(table_ready, 1)
            groups = sp.value_load(steer[0:1, 0:1], min_val=MAIN_GROUPS, max_val=MAIN_GROUPS + OVER_GROUPS)
            with sp.If(groups > MAIN_GROUPS):
                with sp.Fori(MAIN_GROUPS, groups) as g:
                    for e in range(2):
                        expert = sp.value_load(steer[0:1, bass.ds(2 * (g - MAIN_GROUPS) + 1 + e, 1)], min_val=0, max_val=N_EXPERTS - 1)
                        for n in range(3):
                            sp.wait_ge(weights_used[n], g)
                            sp.dma_start(ring[n][:, e:e + 1, :], W[n][:, bass.ds(expert, 1), :]).then_inc(weights_in[n][e], 16)
            sp.wait_ge(scattered_all, 1)
            for t in range(NT):
                sp.dma_start(ring[0][0:rows[t], :, :].rearrange("p a n -> p (a n)")[:, 2048 * t:2048 * t + 2048].rearrange("p (k d) -> p k d", k=2),
                             y_rows[128 * t:128 * t + rows[t], :, :]).then_inc(y_back, 16)
            sp.wait_ge(y_back, 16 * NT)


        @block.gpsimd
        def _(pool):
            nc.gpsimd.memset(xg[:], 0.0).then_inc(cleared, 1)
            pool.wait_ge(cleared, 1)
            pool.wait_ge(xn_stored, 16 * NT)
            pool.wait_ge(table_ready, 1)
            last_group = pool.value_load(steer[0:1, 2 * OVER_GROUPS + 1:2 * OVER_GROUPS + 2], min_val=MAIN_GROUPS - 1, max_val=N_COLS - 1)

            def gather(g):
                if not (isinstance(g, int) and g == 0):
                    pool.wait_ge(gathered, 16 * g)
                nc.gpsimd.tensor_copy(rows_in[:, :], table[:, 0, bass.ds(g, 1)]).then_inc(in_copied, 1)
                pool.wait_ge(in_copied, g + 1)
                if not (isinstance(g, int) and g == 0):
                    pool.wait_ge(gx_T, g)
                pool.sem_inc(waits_held, 1)
                pool.indirect_dma_start(xg[:, :], None, xn_dram[:, :], bass.IndirectOffsetOnAxis(rows_in[:, :], 0),
                                        bounds_check=T_ALL - 1, oob_is_err=False).then_inc(gathered, 16)

            def scatter(g, first=False):
                if not first:
                    pool.wait_ge(scattered, 16 * g)
                nc.gpsimd.tensor_copy(rows_out[:, :], table[:, 1, bass.ds(g, 1)]).then_inc(out_copied, 1)
                pool.wait_ge(out_copied, g + 1)
                pool.wait_ge(y_kept, 2 * g + 2)
                pool.sem_inc(waits_held, 1)
                pool.indirect_dma_start(y_dram[:, :], bass.IndirectOffsetOnAxis(rows_out[:, :], 0), y_sb[:, :], None,
                                        bounds_check=TOP_K * T_ALL - 1, oob_is_err=False).then_inc(scattered, 16)

            gather(0)
            with pool.Fori(0, last_group) as g:
                gather(g + 1)
                scatter(g)
            scatter(last_group)
            pool.wait_ge(scattered, 16 * last_group + 16)
            pool.sem_inc(scattered_all, 1)

        @block.scalar
        def _(act):
            act.wait_ge(ss_cleared, 1)
            for t in range(NT):
                r = rows[t]
                nc.scalar.activation(sq[0:r, :], resid[0:r, t, :], ACT.Square, accum_out=ss[0:r, t:t + 1]).then_inc(squares, 1)
                act.wait_ge(squares, t + 1)
            act.wait_ge(mean_made, 1)
            nc.scalar.activation(rstd[:, :], ss[:, :], ACT.Sqrt).then_inc(roots, 1)
            for t in range(NT):
                act.wait_ge(xT_made, 2 * t + 2)
                nc.scalar.copy(xnT[:, 4:8, :], ps_x[:, 1]).then_inc(xT_kept, 1)
            act.wait_ge(gdiff, 1)
            nc.scalar.activation(gexp[:], gexp[:], ACT.Exp).then_inc(gexped, 1)
            act.wait_ge(tdiff, 1)
            nc.scalar.activation(ratio[:], ratio[:], ACT.Exp).then_inc(texped, 1)
            act.wait_ge(table_ready, 1)
            groups = act.value_load(steer[0:1, 0:1], min_val=MAIN_GROUPS, max_val=MAIN_GROUPS + OVER_GROUPS)
            with act.Fori(0, groups) as g:
                act.wait_ge(gx_T, g + 1)
                act.wait_ge(up_made, g)
                nc.scalar.copy(xgT[:, 4:8, :], ps_x[:, 1]).then_inc(gx_kept, 1)
                act.wait_ge(gate_made, g + 1)
                act.wait_ge(hidden, g)
                nc.scalar.activation(silu[:], ps_gate[:], ACT.Silu).then_inc(silued, 1)
                act.wait_ge(y_made, g + 1)
                act.wait_ge(scattered, 16 * g)
                nc.scalar.copy(y_sb[:, 512:1024], ps_y[:, 1]).then_inc(y_kept, 1)


        @block.vector
        def _(dve):
            n = [0]

            def link(ins):
                n[0] += 1
                ins.then_inc(vchain, 1)
                dve.wait_ge(vchain, n[0])

            V = nc.vector
            link(V.memset(logits[:], 0.0))
            V.memset(ss[:], 1.0).then_inc(ss_cleared, 1)
            dve.wait_ge(squares, NT)
            V.tensor_scalar(ss[:, :], ss[:, :], 1.0 / D_MODEL, EPS, ALU.mult, ALU.add).then_inc(mean_made, 1)
            dve.wait_ge(roots, 1)
            link(V.reciprocal(rstd[:, :], rstd[:, :]))
            dve.wait_ge(consts_in, 16 * 5)
            for t in range(NT):
                r = rows[t]
                V.scalar_tensor_tensor(xn[0:r, t, :], resid[0:r, t, :], rstd[0:r, t:t + 1], norm_b[0:r, :], ALU.mult, ALU.mult).then_inc(normed, 1)
            for t in range(NT):
                r = rows[t]
                dve.wait_ge(xT_made, 2 * t + 1)
                if t:
                    dve.wait_ge(logits_made, t)
                V.tensor_copy(xnT[:, 0:4, :], ps_x[:, 0]).then_inc(xT_kept, 1)
                dve.wait_ge(logits_made, t + 1)
                V.tensor_tensor(logits[0:r, t, :], ps_log[0:r, :], b_router[0:r, :], ALU.add).then_inc(logits_kept, 1)
            dve.wait_ge(logits_kept, NT)
            lg, le = logits[:, :, 0:N_GROUPS], logits[:, :, N_GROUPS:]

            def bc(a, k):
                return a.unsqueeze(2).broadcast_to([128, NT, k])

            link(V.tensor_reduce(gmax[:], lg, AX.X, ALU.max))
            V.tensor_tensor(gexp[:], lg, bc(gmax[:], N_GROUPS), ALU.subtract).then_inc(gdiff, 1)
            link(V.tensor_tensor(gpick[:], lg, bc(gmax[:], N_GROUPS), ALU.is_equal))
            link(V.tensor_tensor(gpick[:], gpick[:], m["falling"][:, 0:N_GROUPS].unsqueeze(1).broadcast_to([128, NT, N_GROUPS]), ALU.mult))
            link(V.tensor_reduce(gbest[:], gpick[:], AX.X, ALU.max))
            link(V.tensor_tensor(gpick[:], gpick[:], bc(gbest[:], N_GROUPS), ALU.is_equal))
            link(V.tensor_scalar(gpick[:], gpick[:], 1.0, FAR, ALU.subtract, ALU.mult))
            for t in range(NT):
                link(V.tensor_tensor(masked[:, t, :].rearrange("p (g e) -> p g e", g=N_GROUPS),
                                     le[:, t, :].rearrange("p (g e) -> p g e", g=N_GROUPS),
                                     gpick[:, t, :].unsqueeze(2).broadcast_to([128, N_GROUPS, EXP_PER_GROUP]), ALU.add))
            for k in range(TOP_K):
                link(V.tensor_reduce(top[:, k, :], masked[:], AX.X, ALU.max))
                link(V.tensor_tensor(etmp[:], masked[:], bc(top[:, k, :], N_EXPERTS), ALU.is_equal))
                link(V.tensor_tensor(etmp[:], etmp[:], m["falling"][:, 0:N_EXPERTS].unsqueeze(1).broadcast_to([128, NT, N_EXPERTS]), ALU.mult))
                link(V.tensor_reduce(ebest[:], etmp[:], AX.X, ALU.max))
                link(V.tensor_tensor(oneh[:, k], etmp[:], bc(ebest[:], N_EXPERTS), ALU.is_equal))
                if k == 0:
                    link(V.scalar_tensor_tensor(masked[:], oneh[:, k], -3.0 * FAR, masked[:], ALU.mult, ALU.add))
            V.tensor_tensor(ratio[:], top[:, 1, :], top[:, 0, :], ALU.subtract).then_inc(tdiff, 1)
            for k in range(TOP_K):
                link(V.tensor_tensor(oneh[:, k], oneh[:, k], bc(m["valid"][:, :], N_EXPERTS), ALU.mult))
            V.tensor_tensor(both[:], oneh[:, 0], oneh[:, 1], ALU.add).then_inc(hots, 1)
            dve.wait_ge(gexped, 1)
            link(V.tensor_reduce(gsum[:], gexp[:], AX.X, ALU.add))
            link(V.reciprocal(gsum[:], gsum[:]))
            dve.wait_ge(texped, 1)
            link(V.tensor_scalar(ebest[:], ratio[:], 1.0, None, ALU.add))
            link(V.reciprocal(ebest[:], ebest[:]))
            link(V.tensor_tensor(gate[:, 0, :], gsum[:], ebest[:], ALU.mult))
            link(V.tensor_tensor(gate[:, 1, :], gate[:, 0, :], ratio[:], ALU.mult))
            dve.wait_ge(ranked, 1)
            link(V.tensor_copy(rank[:], ps_rank))
            link(V.tensor_copy(counts[:], ps_count))
            link(V.tensor_scalar(nover[:], counts[:], float(SLOTS), None, ALU.is_gt))
            for j in range(2, OVER_LEVELS + 1):
                link(V.scalar_tensor_tensor(nover[:], counts[:], float(SLOTS * j), nover[:], ALU.is_gt, ALU.add))
            link(V.tensor_tensor_scan(cend[:], nover[:], nover[:], 0.0, ALU.add, ALU.bypass))
            link(V.tensor_tensor(cstart[:], cend[:], nover[:], ALU.subtract))
            for k in range(TOP_K):
                link(V.tensor_tensor(etmp[:], oneh[:, k], rank[:], ALU.mult))
                link(V.tensor_reduce(rk[:, k, :], etmp[:], AX.X, ALU.add))
                link(V.tensor_tensor(etmp[:], oneh[:, k], m["odd_slots"][:, :].unsqueeze(1).broadcast_to([128, NT, N_EXPERTS]), ALU.mult))
                link(V.tensor_reduce(lmain[:, k, :], etmp[:], AX.X, ALU.add))
                link(V.tensor_tensor(etmp[:], oneh[:, k], cstart[:, :].unsqueeze(1).broadcast_to([128, NT, N_EXPERTS]), ALU.mult))
                link(V.tensor_reduce(opos[:, k, :], etmp[:], AX.X, ALU.add))
            link(V.tensor_tensor(lmain[:], lmain[:], rk[:], ALU.add))
            link(V.tensor_scalar(opos[:], opos[:], float(SLOTS), -float(SLOTS), ALU.mult, ALU.add))
            link(V.tensor_tensor(opos[:], opos[:], rk[:], ALU.add))
            link(V.tensor_scalar(inmain[:], rk[:], float(SLOTS), None, ALU.is_lt))
            for j in range(OVER_GROUPS + 1):
                link(V.tensor_scalar(oge[:, :, :, j], opos[:], 128.0 * j, None, ALU.is_ge))
            link(V.tensor_reduce(olow[:], oge[:, :, :, 1:OVER_GROUPS], AX.X, ALU.add))
            link(V.scalar_tensor_tensor(olow[:], olow[:], -128.0, opos[:], ALU.mult, ALU.add))
            link(V.tensor_tensor(lmain[:], lmain[:], olow[:], ALU.subtract))
            link(V.tensor_tensor(lmain[:], lmain[:], inmain[:], ALU.mult))
            link(V.tensor_tensor(lpos[:], lmain[:], olow[:], ALU.add))
            for k in range(TOP_K):
                for t in range(NT):
                    link(V.tensor_scalar(place[:, k, t, :], m["lanes"][:, :], lpos[:, k, t:t + 1], None, ALU.is_equal))
                link(V.tensor_reduce(colhot[:, k, :, 0:MAIN_GROUPS], oneh[:, k].rearrange("p a (g e) -> p a g e", e=2), AX.X, ALU.add))
                link(V.tensor_tensor(colhot[:, k, :, 0:MAIN_GROUPS], colhot[:, k, :, 0:MAIN_GROUPS], bc(inmain[:, k, :], MAIN_GROUPS), ALU.mult))
                link(V.tensor_tensor(colhot[:, k, :, MAIN_GROUPS:], oge[:, k, :, 0:OVER_GROUPS], oge[:, k, :, 1:OVER_GROUPS + 1], ALU.subtract))
                link(V.tensor_scalar(inmain[:, k, :], inmain[:, k, :], -1.0, 1.0, ALU.mult, ALU.add))
                link(V.tensor_tensor(inmain[:, k, :], inmain[:, k, :], m["valid"][:, :], ALU.mult))
                link(V.tensor_tensor(colhot[:, k, :, MAIN_GROUPS:], colhot[:, k, :, MAIN_GROUPS:], bc(inmain[:, k, :], OVER_GROUPS), ALU.mult))
                for j in range(2):
                    link(V.tensor_tensor(entry[:, k, :, j, :], colhot[:, k], bc(m["token_no"][:, k, j, :], N_COLS), ALU.mult))
            V.tensor_copy(etmp[:, 0, 0:1], m["lanes"][:, 0:1]).then_inc(placed, 1)
            link(V.tensor_reduce(ngf[:, 0:1], nover[0:1, :], AX.X, ALU.add))
            link(V.memset(ovalf[:], float(MAIN_GROUPS)))
            for j in range(OVER_GROUPS):
                link(V.scalar_tensor_tensor(ovalf[:, 0:1], ngf[:, 0:1], 2.0 * j, ovalf[:, 0:1], ALU.is_gt, ALU.add))
            for b in range(2 * OVER_GROUPS):
                link(V.tensor_scalar(obf[:, b, :], cend[0:1, :], float(b), None, ALU.is_le))
            link(V.tensor_reduce(ovalf[:, 1:2 * OVER_GROUPS + 1], obf[:], AX.X, ALU.add))
            link(V.tensor_scalar(ovalf[:, 1:2 * OVER_GROUPS + 1], ovalf[:, 1:2 * OVER_GROUPS + 1], float(N_EXPERTS - 1), None, ALU.min))
            link(V.tensor_scalar(ovalf[:, 2 * OVER_GROUPS + 1:], ovalf[:, 0:1], -1.0, None, ALU.add))
            link(V.tensor_copy(steer[:], ovalf[:]))
            dve.wait_ge(tabbed, 1)
            tf = tabf[:].rearrange("p a c -> p (a c)")
            tz = tabz[:].rearrange("p a c -> p (a c)")
            link(V.tensor_copy(tf, ps_tab))
            link(V.tensor_scalar(tz, tf, 0.0, NOWHERE, ALU.is_equal, ALU.mult))
            link(V.scalar_tensor_tensor(tf, tf, -1.0, tz, ALU.add, ALU.add))
            V.tensor_copy(table[:].rearrange("p a c -> p (a c)"), tf).then_inc(table_ready, 1)
            dve.wait_ge(table_ready, 1)
            groups = dve.value_load(steer[0:1, 0:1], min_val=MAIN_GROUPS, max_val=MAIN_GROUPS + OVER_GROUPS)
            with dve.Fori(0, groups) as g:
                dve.wait_ge(gx_T, g + 1)
                dve.wait_ge(up_made, g)
                V.tensor_copy(xgT[:, 0:4, :], ps_x[:, 0]).then_inc(gx_kept, 1)
                dve.wait_ge(up_made, g + 1)
                dve.wait_ge(silued, g + 1)
                dve.wait_ge(hid_T, g)
                V.tensor_tensor(hid[:], silu[:], ps_up[:], ALU.mult).then_inc(hidden, 1)
                dve.wait_ge(hid_T, g + 1)
                dve.wait_ge(y_made, g)
                V.tensor_copy(hidT[:], ps_hid[:]).then_inc(hid_kept, 1)
                dve.wait_ge(y_made, g + 1)
                dve.wait_ge(scattered, 16 * g)
                V.tensor_copy(y_sb[:, 0:512], ps_y[:, 0]).then_inc(y_kept, 1)
            dve.wait_ge(y_back, 16 * NT)
            back = ring[0][:].rearrange("p a n -> p (a n)")
            for k in range(TOP_K):
                for t in range(NT):
                    r = rows[t]
                    link(V.scalar_tensor_tensor(resid[0:r, t, :], back[0:r, 2048 * t + 1024 * k:2048 * t + 1024 * k + 1024], gate[0:r, k, t:t + 1],
                                                resid[0:r, t, :], ALU.mult, ALU.add))

        @block.tensor
        def _(pe):
            T = nc.tensor
            for t in range(NT):
                r = rows[t]
                pe.wait_ge(normed, t + 1)
                if t:
                    pe.wait_ge(xT_kept, 2 * t)
                xv = xn[0:r, t, :].rearrange("p (c k) -> p k c", k=KT)
                for k in range(KT):
                    last = T.transpose(ps_x[:, k // 4, k % 4, 0:r], xv[:, k, :], ident[0:r, 0:r])
                    if k % 4 == 3:
                        last.then_inc(xT_made, 1)
                pe.wait_ge(xT_kept, 2 * t + 2)
                if t:
                    pe.wait_ge(logits_kept, t)
                for k in range(KT):
                    last = T.matmul(ps_log[0:r, :], xnT[:, k, 0:r], w_router[:, k, :], start=(k == 0), stop=(k == KT - 1))
                last.then_inc(logits_made, 1)
            pe.wait_ge(hots, 1)
            for t in range(NT):
                for s in range(t):
                    T.matmul(ps_rank[:, t, :], m["ones"][:, :], both[:, s, :], start=(s == 0), stop=False)
                T.matmul(ps_rank[:, t, :], m["before"][:, :], both[:, t, :], start=(t == 0), stop=True)
            for s in range(NT):
                last = T.matmul(ps_count, m["ones"][:, :], both[:, s, :], start=(s == 0), stop=(s == NT - 1))
            last.then_inc(ranked, 1)
            pe.wait_ge(placed, 1)
            for k in range(TOP_K):
                for t in range(NT):
                    last = T.matmul(ps_tab, place[:, k, t, :], entry[:, k, t].rearrange("p a c -> p (a c)"),
                                    start=(k == 0 and t == 0), stop=(k == TOP_K - 1 and t == NT - 1))
            last.then_inc(tabbed, 1)
            pe.wait_ge(table_ready, 1)
            groups = pe.value_load(steer[0:1, 0:1], min_val=MAIN_GROUPS, max_val=MAIN_GROUPS + OVER_GROUPS)
            xgv = xg[:, :].rearrange("p (c k) -> p k c", k=KT)
            hidv = hid[:, :].rearrange("p (c k) -> p k c", k=FT)
            with pe.Fori(0, groups) as g:
                pe.wait_ge(gathered, 16 * g + 16)
                pe.wait_ge(gx_kept, 2 * g)
                for k in range(KT):
                    last = T.transpose(ps_x[:, k // 4, k % 4, :], xgv[:, k, :], ident[:, :])
                last.then_inc(gx_T, 1)
                pe.wait_ge(gx_kept, 2 * g + 2)
                pe.wait_ge(silued, g)
                for n, ps in ((0, ps_gate), (1, ps_up)):
                    if n == 1:
                        pe.wait_ge(hidden, g)
                    for e in range(2):
                        pe.wait_ge(weights_in[n][e], 16 * g + 16)
                    for k in range(KT):
                        for e in range(2):
                            last = T.matmul(ps[64 * e:64 * e + 64, :], xgT[:, k, 64 * e:64 * e + 64],
                                            ring[n][:, e, 512 * k:512 * k + 512], start=(k == 0), stop=(k == KT - 1))
                    last.then_inc(weights_used[n], 1)
                pe.wait_ge(hidden, g + 1)
                pe.wait_ge(hid_kept, g)
                for k in range(FT):
                    last = T.transpose(ps_hid[:, k, :], hidv[:, k, :], ident[:, :])
                last.then_inc(hid_T, 1)
                pe.wait_ge(hid_kept, g + 1)
                pe.wait_ge(y_kept, 2 * g)
                for e in range(2):
                    pe.wait_ge(weights_in[2][e], 16 * g + 16)
                for h in range(2):
                    for k in range(FT):
                        for e in range(2):
                            last = T.matmul(ps_y[64 * e:64 * e + 64, h, :], hidT[:, k, 64 * e:64 * e + 64],
                                            ring[2][:, e, 1024 * k + 512 * h:1024 * k + 512 * h + 512], start=(k == 0), stop=(k == FT - 1))
                last.then_inc(weights_used[2], 1)

    nc.clear_and_free_semaphores(sems)
    nc.all_engine_barrier(sem_only=True)


def final_phase(nc, m):
    ctx, sems = ExitStack(), []
    with ctx:
        def sem(name):
            sems.append(nc.alloc_semaphore(f"fin_{name}"))
            return sems[-1]

        NT, rows = TOK_TILES, TILE_ROWS
        norm_b = ctx.enter_context(nc.sbuf_tensor("fin_norm", [128, D_MODEL], F32))
        sq = ctx.enter_context(nc.sbuf_tensor("fin_sq", [128, D_MODEL], F32))
        ss = ctx.enter_context(nc.sbuf_tensor("fin_ss", [128, NT], F32))
        cleared, squares, mean_made, roots, inverse, norm_in, normed, stored = (sem(n) for n in (
            "cleared", "squares", "mean_made", "roots", "inverse", "norm_in", "normed", "stored"))
        block = ctx.enter_context(nc.Block())

        @block.sync
        def _(sp):
            sp.dma_start(norm_b[:], m["final_norm"].rearrange("(a d) -> a d", a=1).broadcast_to([128, D_MODEL])).then_inc(norm_in, 16)
            for t in range(NT):
                sp.wait_ge(normed, t + 1)
                dst = m["y_prompt"][0, 128 * t:128 * t + 128, :] if t < 2 else m["y_sample"].rearrange("b l d -> (b l) d")
                sp.dma_start(dst, m["resid"][0:rows[t], t, :]).then_inc(stored, 16)
            sp.wait_ge(stored, 16 * NT)

        @block.scalar
        def _(act):
            act.wait_ge(cleared, 1)
            for t in range(NT):
                r = rows[t]
                nc.scalar.activation(sq[0:r, :], m["resid"][0:r, t, :], ACT.Square, accum_out=ss[0:r, t:t + 1]).then_inc(squares, 1)
                act.wait_ge(squares, t + 1)
            act.wait_ge(mean_made, 1)
            nc.scalar.activation(ss[:, :], ss[:, :], ACT.Sqrt).then_inc(roots, 1)

        @block.vector
        def _(dve):
            nc.vector.memset(ss[:], 1.0).then_inc(cleared, 1)
            dve.wait_ge(squares, NT)
            nc.vector.tensor_scalar(ss[:, :], ss[:, :], 1.0 / D_MODEL, EPS, ALU.mult, ALU.add).then_inc(mean_made, 1)
            dve.wait_ge(roots, 1)
            nc.vector.reciprocal(ss[:, :], ss[:, :]).then_inc(inverse, 1)
            dve.wait_ge(inverse, 1)
            dve.wait_ge(norm_in, 16)
            for t in range(NT):
                r = rows[t]
                nc.vector.scalar_tensor_tensor(m["resid"][0:r, t, :], m["resid"][0:r, t, :], ss[0:r, t:t + 1], norm_b[0:r, :],
                                               ALU.mult, ALU.mult).then_inc(normed, 1)

    nc.clear_and_free_semaphores(sems)
    nc.all_engine_barrier(sem_only=True)

def decoder_step(nc, m, shapes):
    m["xn_dram"] = nc.dram_tensor("xn_rows", (T_ALL, D_MODEL), F32, kind="Internal").ap()
    m["y_dram"] = [nc.dram_tensor(f"expert_rows{i}", (TOP_K * T_ALL, D_MODEL), F32, kind="Internal").ap() for i in range(LAYERS)]
    with ExitStack() as ctx:
        def sb(name, shape):
            return ctx.enter_context(nc.sbuf_tensor(name, shape, F32))

        m["resid"] = sb("resid", [128, TOK_TILES, D_MODEL])
        m["consts"] = sb("consts", [128, sum(shapes.values())])
        start = 0
        for name, width in shapes.items():
            m[name] = m["consts"][:, start:start + width]
            start += width
        m["token_no"] = m["token_no"].rearrange("p (k j t) -> p k j t", k=TOP_K, j=2)
        m["levels"] = m["levels"].rearrange("p (n i) -> p n i", n=LEVELS)
        m["cos"] = m["cos"].rearrange("p (t d) -> p t d", t=TOK_TILES)
        m["sin"] = m["sin"].rearrange("p (t d) -> p t d", t=TOK_TILES)
        m["new_keys"] = m["new_keys"].rearrange("p (a k) -> p a k", k=T_DEC)
        m["ring"] = [sb(f"ring_{n}", [128, 2, KT * D_FF_EXPERT]) for n in ("gate", "up", "down")]
        m["expert_views"] = [[w[i].rearrange("e (p t) n -> p e (t n)", p=128) for w in (m["w_gate_e"], m["w_up_e"], m["w_down_e"])] for i in range(LAYERS)]
        m["weights_of"] = [[[ctx.enter_context(nc.semaphore(f"{n}{e}_in_{i}")) for e in range(2)] for n in ("gate", "up", "down")] for i in range(LAYERS)]

        def prefetch(eng, layer, kinds):
            for n in kinds:
                for e in range(2):
                    eng.dma_start(m["ring"][n][:, e:e + 1, :], m["expert_views"][layer][n][:, e:e + 1, :]).then_inc(m["weights_of"][layer][n][e], 16)

        m["prefetch"] = prefetch
        gdn_phase(nc, m)
        moe_phase(nc, m, 0)
        attn_phase(nc, m)
        moe_phase(nc, m, 1)
        final_phase(nc, m)


_OUTS = [("y_prompt", (1, SEQ, D_MODEL)), ("y_sample", (DEC_BATCH, DEC_SEQ, D_MODEL)),
         ("sd_prompt", (1, 1, HEADS, DK, DK)), ("sc_prompt", (1, 1, CONV_W - 1, CONV_CH)),
         ("k_prompt", (1, SEQ, HEADS, 2 * DH)), ("v_prompt", (1, SEQ, HEADS, 2 * DH)),
         ("sd_sample", (1, DEC_BATCH, HEADS, DK, DK)), ("sc_sample", (1, DEC_BATCH, CONV_W - 1, CONV_CH)),
         ("k_sample", (DEC_BATCH, DEC_SEQ, HEADS, 2 * DH)), ("v_sample", (DEC_BATCH, DEC_SEQ, HEADS, 2 * DH))]


def kernel(**inputs):
    import concourse.bacc as _bacc
    from concourse.bass_utils import run_bass_kernel_spmd as _run

    nc = _bacc.Bacc("TRN2", target_bir_lowering=False, num_devices=1)
    tables = shape_constants()
    arrays, aps = {}, {}

    def give(name, a):
        arrays[f"in_{name}_dram"] = a
        aps[name] = nc.dram_tensor(f"in_{name}_dram", a.shape, mybir.dt.from_np(a.dtype), kind="ExternalInput").ap()

    for name, a in inputs.items():
        give(name, np.ascontiguousarray(a))
    give("consts_dram", np.ascontiguousarray(np.concatenate(list(tables.values()), 1)))
    for name, shape in _OUTS:
        aps[name] = nc.dram_tensor(f"out_{name}_dram", shape, F32, kind="ExternalOutput").ap()
    decoder_step(nc, aps, {n: a.shape[1] for n, a in tables.items()})
    r = _run(nc, [arrays], core_ids=[0])
    return tuple(r.results[0][f"out_{name}_dram"] for name, _ in _OUTS)
```

```python
import math
from contextlib import ExitStack

import numpy as np

import concourse.bass as bass
from concourse import mybir

F32 = mybir.dt.float32
U32 = mybir.dt.uint32
I32 = mybir.dt.int32
ACT = mybir.ActivationFunctionType
ALU = mybir.AluOpType
AX = mybir.AxisListType

D_MODEL = 1024
SEQ = 256
DEC_BATCH = 8
DEC_SEQ = 4
PAST_LEN = 256
PAGE_SIZE = 128
N_PAGES = PAST_LEN // PAGE_SIZE
N_PHYS = DEC_BATCH * N_PAGES + max(1, DEC_BATCH * N_PAGES // 4)
HEADS = 8
DK = 128
CONV_CH = 3 * D_MODEL
GDN_IN = CONV_CH + D_MODEL + 2 * HEADS
CONV_W = 4
DH = 64
N_GROUPS = 4
EXP_PER_GROUP = 8
N_EXPERTS = 32
D_FF_EXPERT = 512
TOP_K = 2
EPS = 1e-6
LAYERS = 2

T_DEC = DEC_BATCH * DEC_SEQ
T_ALL = SEQ + T_DEC
TILE_ROWS = [128, 128, T_DEC]
TOK_TILES = len(TILE_ROWS)
KT = D_MODEL // 128
FT = D_FF_EXPERT // 128

SLOTS = 64
MAIN_GROUPS = N_EXPERTS // 2
OVER_LEVELS = -(-T_ALL // SLOTS) - 1
OVER_GROUPS = -(-((TOP_K * T_ALL) // SLOTS - 1) // 2)
N_COLS = MAIN_GROUPS + OVER_GROUPS
FAR = 1e30
NOWHERE = 16384.0


def shape_constants():
    p = np.arange(128)
    c = {}
    c["ident"] = np.eye(128)
    c["ones"] = np.ones((128, 128))
    c["before"] = (p[:, None] < p[None, :])
    c["lanes"] = np.tile(p, (128, 1))
    c["eps"] = np.full((128, 1), EPS)
    c["falling"] = np.tile(N_EXPERTS - np.arange(N_EXPERTS), (128, 1))
    c["odd_slots"] = np.tile(64 * (np.arange(N_EXPERTS) % 2), (128, 1))
    tok = p[:, None] + 128 * np.arange(TOK_TILES)[None, :]
    c["valid"] = tok < T_ALL
    c["token_no"] = np.stack([np.stack([tok + 1, TOP_K * tok + k + 1], 1) for k in range(TOP_K)], 1)
    c.update(mixer_constants())
    return {n: np.ascontiguousarray(a, np.float32).reshape(128, -1) for n, a in c.items()}


def mixer_constants():
    return {**gdn_constants(), **attn_constants()}


CW_COLS = SEQ + CONV_W - 1 + DEC_BATCH * (DEC_SEQ + CONV_W - 1)
DEC0 = SEQ + CONV_W - 1
DEC_STRIDE = DEC_SEQ + CONV_W - 1
ACC_COLS = CW_COLS - (CONV_W - 1)
CHUNK = 128
LEVELS = 7
V_STEPS = 12


def gdn_constants():
    c = {}
    p = np.arange(128)
    same = (p[:, None] // DEC_SEQ) == (p[None, :] // DEC_SEQ)
    upto = p[:, None] <= p[None, :]
    dec = np.zeros((128, T_DEC))
    dec[:T_DEC] = (same & upto)[:T_DEC, :T_DEC]
    c["upto"] = np.concatenate([upto, upto, dec], 1)
    c["floor"] = np.where(c["upto"] > 0, 0.0, -FAR)
    c["dec_same"] = np.where(np.arange(128)[:, None] < T_DEC, same[:, :T_DEC], 0)
    c["dec_seq"] = (p[:, None] // DEC_SEQ) == np.arange(DEC_BATCH)[None, :]
    lev = []
    for n in range(LEVELS):
        s = 1 << n
        lev.append((p[:, None] // (2 * s) == p[None, :] // (2 * s)) & ((p[:, None] // s) % 2 == 0) & ((p[None, :] // s) % 2 == 1))
    c["levels"] = np.stack(lev, 1)
    return c


def gdn_phase(nc, m):
    ctx, sems = ExitStack(), []
    with ctx:
        def sb(name, shape, dt=F32):
            return ctx.enter_context(nc.sbuf_tensor(f"gdn_{name}", shape, dt))

        def sem(name):
            sems.append(nc.alloc_semaphore(f"gdn_{name}"))
            return sems[-1]

        NT, rows, H = TOK_TILES, TILE_ROWS, HEADS
        at = [slice(128 * t, 128 * t + rows[t]) for t in range(NT)]
        resid, ident, ones = m["resid"], m["ident"], m["ones"]
        norm_b, sq, xn = (m["ring"][1][:, 1, D_MODEL * j:D_MODEL * (j + 1)] for j in range(3))
        oT = m["ring"][0][:, 0, 0:H * T_ALL].rearrange("p (h t) -> p h t", h=H)
        osum = m["ring"][1][:, 1, 0:H * T_ALL].rearrange("p (h t) -> p h t", h=H)
        ss = sb("ss", [128, NT])
        xT = sb("xT", [128, KT, T_ALL])
        w_ab = sb("w_ab", [128, KT, 2 * H])
        ab_bias = sb("ab_bias", [128, 2, H])
        ab = sb("ab", [128, NT, 2 * H])
        g = sb("g", [128, NT, H])
        gt = sb("gt", [128, NT, H])
        gt2 = sb("gt2", [128, NT, H])
        beta = sb("beta", [128, NT, H])
        G = sb("G", [128, NT, H])
        eG = sb("eG", [128, NT, H])
        beG = sb("beG", [128, NT, H])
        eL = sb("eL", [128, NT, H])
        decg = sb("decg", [T_DEC, DEC_BATCH, H])
        eLast = sb("eLast", [128, 2 + DEC_BATCH, H])
        w4 = m["ring"][1][:, 0, :].rearrange("p (j k c) -> p j k c", j=4, k=KT)
        st_in = sb("st_in", [28, 3, 128])
        cw = sb("cw", [128, 3, CONV_W])
        cin = sb("cin", [128, 3, CW_COLS])
        ends = sb("ends", [128, 3, 27])
        ends_tok = sb("ends_tok", [27, 3, 128])
        acc = sb("acc", [128, 3, CW_COLS])
        qkv = sb("qkv", [128, 3, T_ALL])
        qk2 = sb("qk2", [128, 2, T_ALL])
        rn = sb("rn", [128, 2, T_ALL])
        kbq = sb("kbq", [128, 2, T_ALL])
        kT = sb("kT", [128, T_ALL])
        eGB = sb("eGB", [128, T_ALL])
        gsrc = sb("gsrc", [128, T_ALL])
        bsrc = sb("bsrc", [128, T_ALL])
        D = sb("D", [128, T_ALL])
        KQD = sb("KQD", [128, 2, 2, 128])
        KQD2 = sb("KQD2", [T_DEC, 2, T_DEC])
        Mlev = sb("Mlev", [128, LEVELS, 2, 128])
        M2 = sb("M2", [T_DEC, 2, T_DEC])
        TU = sb("TU", [128, 2, 2, 128])
        TU2 = sb("TU2", [T_DEC, 2, T_DEC])
        Y = m["ring"][1][:, 1, H * T_ALL:H * T_ALL + LEVELS * 256].rearrange("p (n t i) -> p n t i", n=LEVELS, t=2)
        Y2 = sb("Y2", [T_DEC, T_DEC])
        vb = sb("vb", [128, NT, 128])
        kg = sb("kg", [128, NT, 128])
        kd = sb("kd", [128, NT, 128])
        WQ = sb("WQ", [128, 2, T_ALL])
        wsT = sb("wsT", [128, 2, T_DEC])
        u = sb("u", [128, NT, 128])
        uB = sb("uB", [T_DEC, DEC_BATCH, 128])
        S1 = sb("S1", [128, 128])
        S2 = sb("S2", [128, 128])
        Sd = sb("Sd", [128, DEC_BATCH, 128])
        Sn = sb("Sn", [128, DEC_BATCH, 128])
        o2 = sb("o2", [128, T_ALL])
        ozT = sb("ozT", [128, H, T_ALL])
        onorm = sb("onorm", [128, 1])
        w_out = m["ring"][2][:].rearrange("p a n -> p (a n)").rearrange("p (h n) -> p h n", h=H)

        B = [ctx.enter_context(nc.psum_tensor(f"gdn_bank{i}", [128, 512], F32)) for i in range(8)]

        s = {n: sem(n) for n in (
            "x_in0 x_in1 x_in2 consts_in squares mean_made roots normed xT_made xT_kept ab_made ab_kept exp_in exp_out soft_in soft_out gates_made sums_made "
            "decays_in decays_out "
            "q_in k_in v_in z_in st_loaded st_T proj proj_kept prior_kept ends_copied conv_done silued squares2 sums2 logs2 roots2 ends_T ends_kept ends_stored "
            "src_made bcast eGB_made D_in D_made T0_kept parts_clear kb_made kv_T kv_kept KQ_made lev_made T1_made TU_kept Y_made Y_kept TU_made "
            "W_made W_kept z_kept zs_made joined Sn_decayed rows_kept kT_made Y2_kept u0_made u_kept S1_made S1_kept ws_made ws_kept u2_made u1_made o_made oT_kept S2_made S2_kept Sd_in Sn_made uB_made Sn_kept "
            "S_stored o2_made osum_made osum_kept olog oroot oz_made wout_in out_made out_kept v").split()}

        w_in = m["w_in_a"][0].rearrange("(p t) n -> p t n", t=KT)
        heads_of = [w_in[:, :, j * D_MODEL:(j + 1) * D_MODEL] for j in range(4)]
        slot_in = [s["q_in"], s["k_in"], s["v_in"], s["z_in"]]
        st_conv = m["state_conv"][0].rearrange("b j c -> (b j) c").rearrange("r (s c) -> r s c", s=3)
        cv_w = m["conv_w_a"][0].rearrange("j (s c) -> j s c", s=3)
        st_delta = m["state_delta"][0].rearrange("b h k v -> k h b v")
        out_delta = m["sd_sample"][0].rearrange("b h k v -> k h b v")
        out_delta_p = m["sd_prompt"][0, 0].rearrange("h k v -> k h v")
        out_conv = m["sc_sample"][0].rearrange("b j c -> (b j) c").rearrange("r (s c) -> r s c", s=3)
        out_conv_p = m["sc_prompt"][0, 0].rearrange("j (s c) -> j s c", s=3)
        dec_cin = cin[:, :, DEC0:].rearrange("p s (b c) -> p s b c", c=DEC_STRIDE)
        dec_acc = acc[:, :, DEC0:].rearrange("p s (b c) -> p s b c", c=DEC_STRIDE)[:, :, :, 0:DEC_SEQ]

        def part(a, n, half):
            return a.rearrange("p t (b e c) -> p t b e c", e=2, c=1 << n)[:, :, :, half, :]

        def packed(a, n):
            return a.rearrange("p (t b c) -> p t b c", t=2, c=1 << n)

        block = ctx.enter_context(nc.Block())

        @block.sync
        def _(sp):
            for t in range(NT):
                src = m["x_prompt"][0, at[t], :] if t < 2 else m["x_sample"].rearrange("b l d -> (b l) d")
                sp.dma_start(resid[0:rows[t], t, :], src).then_inc((s["x_in0"], s["x_in1"], s["x_in2"])[t], 16)
            sp.dma_start(norm_b[:], m["norm_a"][0:1, :].broadcast_to([128, D_MODEL])).then_inc(s["consts_in"], 16)
            sp.dma_start(m["consts"][:], m["consts_dram"]).then_inc(s["consts_in"], 16)
            sp.dma_start(w_ab[:], w_in[:, :, CONV_CH + D_MODEL:GDN_IN]).then_inc(s["consts_in"], 16)
            sp.dma_start(ab_bias[:, 0, :], m["a_log"][0:1, :].broadcast_to([128, H])).then_inc(s["consts_in"], 16)
            sp.dma_start(ab_bias[:, 1, :], m["dt_bias"][0:1, :].broadcast_to([128, H])).then_inc(s["consts_in"], 16)
            sp.dma_start(onorm[:], m["onorm_a"].rearrange("a v -> v a")).then_inc(s["consts_in"], 16)

            def load_rows(h):
                if not (isinstance(h, int) and h == 0):
                    sp.wait_ge(s["st_T"], h)
                for r, src in ((slice(0, 24), st_conv), (slice(24, 28), cv_w)):
                    sp.dma_start(st_in[r, :, :], src[:, :, bass.ds(h * 128, 128)]).then_inc(s["st_loaded"], 16)

            def load(h, j):
                if not (isinstance(h, int) and h == 0):
                    sp.wait_ge(s["proj"], 4 * h - 3 + j)
                sp.dma_start(w4[:, j], heads_of[j][:, :, bass.ds(h * 128, 128)]).then_inc(slot_in[j], 16)

            def load_state(h):
                if not (isinstance(h, int) and h == 0):
                    sp.wait_ge(s["ws_made"], h)
                    sp.wait_ge(s["Sn_decayed"], h)
                sp.dma_start(Sd[:], st_delta[:, bass.ds(h, 1), :, :].rearrange("k h b v -> k (h b) v")).then_inc(s["Sd_in"], 16)

            def store_ends(h):
                sp.wait_ge(s["ends_kept"], h + 1)
                sp.dma_start(out_conv_p[:, :, bass.ds(h * 128, 128)], ends_tok[0:3, :, :]).then_inc(s["ends_stored"], 16)
                sp.dma_start(out_conv[:, :, bass.ds(h * 128, 128)], ends_tok[3:27, :, :]).then_inc(s["ends_stored"], 16)

            def store_states(h):
                sp.wait_ge(s["S2_kept"], h + 1)
                sp.dma_start(out_delta_p[:, bass.ds(h, 1), :].rearrange("k h v -> k (h v)"), S2[:]).then_inc(s["S_stored"], 16)
                sp.wait_ge(s["Sn_kept"], 2 * h + 2)
                sp.dma_start(out_delta[:, bass.ds(h, 1), :, :].rearrange("k h b v -> k (h b) v"), Sn[:]).then_inc(s["S_stored"], 16)

            def serve(h, ahead, following):
                store_ends(h)
                if ahead:
                    load(h + 3, 0)
                    load(h + 3, 1)
                    load_rows(h + 3)
                    load(h + 3, 2)
                if following:
                    load_state(h + 1)
                if ahead:
                    load(h + 3, 3)
                store_states(h)

            for h in range(3):
                if h < 2:
                    load_rows(h)
                for j in range(4):
                    load(h, j)
                if h == 0:
                    load_state(0)
            load_rows(2)
            serve(0, True, True)
            with sp.Fori(1, H - 3) as h:
                serve(h, True, True)
            serve(H - 3, False, True)
            serve(H - 2, False, True)
            sp.dma_start(w_out, m["w_out_a"][0].rearrange("(h p) n -> p h n", p=128)).then_inc(s["wout_in"], 16)
            serve(H - 1, False, False)
            sp.wait_ge(s["ends_stored"], 32 * H)
            sp.wait_ge(s["S_stored"], 32 * H)
            sp.wait_ge(s["oz_made"], H // 2)
            m["prefetch"](sp, 0, (0, 1))
            sp.wait_ge(s["out_made"], 2 * NT)
            m["prefetch"](sp, 0, (2,))

        @block.gpsimd
        def _(pool):
            nc.gpsimd.memset(cin[:, :, 0:CONV_W - 1], 0.0).then_inc(s["prior_kept"], 1)
            pool.wait_ge(s["xT_made"], 2 * NT)
            nc.gpsimd.memset(Y[:], 0.0).then_inc(s["parts_clear"], 1)
            nc.gpsimd.memset(Mlev[:], 0.0).then_inc(s["parts_clear"], 1)
            pool.wait_ge(s["gates_made"], 1)

            def head(h):
                if not (isinstance(h, int) and h == 0):
                    pool.wait_ge(s["bcast"], h)
                    pool.wait_ge(s["ends_T"], h)
                pool.wait_ge(s["proj_kept"], 6 * h + 6)
                for t in range(NT):
                    r = rows[t]
                    nc.gpsimd.tensor_tensor(gsrc[0:r, at[t]], m["upto"][0:r, at[t]], g[0:r, t, bass.ds(h, 1)].broadcast_to([r, r]), ALU.mult).then_inc(s["src_made"], 1)
                    nc.gpsimd.tensor_tensor(bsrc[0:r, at[t]], ident[0:r, 0:r], beta[0:r, t, bass.ds(h, 1)].broadcast_to([r, r]), ALU.mult).then_inc(s["src_made"], 1)
                nc.gpsimd.tensor_copy(ends[:, :, 0:3], cin[:, :, SEQ:SEQ + 3]).then_inc(s["ends_copied"], 1)
                for j in range(3):
                    nc.gpsimd.tensor_copy(ends[:, j, 3:27].rearrange("p (b c) -> p b c", c=3), dec_cin[:, j, :, DEC_SEQ:]).then_inc(s["ends_copied"], 1)

            def states(h):
                pool.wait_ge(s["Sd_in"], 16 * h + 16)
                if not (isinstance(h, int) and h == 0):
                    pool.wait_ge(s["S_stored"], 32 * h)
                nc.gpsimd.tensor_tensor(Sn[:], Sd[:], eLast[:, 2:, bass.ds(h, 1)].broadcast_to([128, DEC_BATCH, 128]), ALU.mult).then_inc(s["Sn_decayed"], 1)
                pool.wait_ge(s["u_kept"], 3 * h + 3)
                nc.gpsimd.tensor_tensor(uB[:], u[0:T_DEC, 2, :].unsqueeze(1).broadcast_to([T_DEC, DEC_BATCH, 128]),
                                        m["dec_seq"][0:T_DEC, :].unsqueeze(2).broadcast_to([T_DEC, DEC_BATCH, 128]), ALU.mult).then_inc(s["uB_made"], 1)

            head(0)
            head(1)
            pool.wait_ge(s["decays_out"], 3)
            states(0)
            with pool.Fori(1, H - 1) as h:
                head(h + 1)
                states(h)
            states(H - 1)

        @block.scalar
        def _(act):
            A = nc.scalar
            for t in range(NT):
                r = rows[t]
                act.wait_ge((s["x_in0"], s["x_in1"], s["x_in2"])[t], 16)
                if t == 0:
                    act.wait_ge(s["squares"], 1)
                A.activation(sq[0:r, :], resid[0:r, t, :], ACT.Square, accum_out=ss[0:r, t:t + 1]).then_inc(s["squares"], 1)
                act.wait_ge(s["squares"], t + 2)
            act.wait_ge(s["mean_made"], 1)
            A.activation(ss[:, :], ss[:, :], ACT.Sqrt).then_inc(s["roots"], 1)
            for t in range(NT):
                act.wait_ge(s["xT_made"], 2 * t + 2)
                A.copy(xT[:, 4:8, at[t]], B[1][:, :].rearrange("p (k r) -> p k r", k=4)[:, :, 0:rows[t]]).then_inc(s["xT_kept"], 1)
            act.wait_ge(s["exp_in"], 1)
            A.activation(gt[:], gt[:], ACT.Exp).then_inc(s["exp_out"], 1)
            A.activation(beta[:], beta[:], ACT.Exp).then_inc(s["exp_out"], 1)
            A.activation(ab_bias[:, 0, :], ab_bias[:, 0, :], ACT.Exp).then_inc(s["exp_out"], 1)
            act.wait_ge(s["exp_out"], 3)
            act.wait_ge(s["soft_in"], 1)
            A.activation(gt[:], gt[:], ACT.Ln).then_inc(s["soft_out"], 1)

            def evacuate(h, j):
                act.wait_ge(s["proj"], 4 * h + j + 1)
                if j == 0 and not (isinstance(h, int) and h == 0):
                    act.wait_ge(s["conv_done"], h)
                    act.wait_ge(s["ends_copied"], 4 * h)
                src = B[j % 2]
                if j < 3:
                    A.copy(cin[:, j, 3:3 + SEQ], src[:, 0:SEQ]).then_inc(s["proj_kept"], 1)
                    A.copy(dec_cin[:, j, :, 3:], src[:, SEQ:T_ALL].rearrange("p (b c) -> p b c", c=DEC_SEQ)).then_inc(s["proj_kept"], 1)
                else:
                    A.copy(ozT[:, bass.ds(h, 1), :].rearrange("p o t -> p (o t)"), src[:, 0:T_ALL]).then_inc(s["z_kept"], 1)

            def silu_z(h):
                z = ozT[:, bass.ds(h, 1), :].rearrange("p o t -> p (o t)")
                act.wait_ge(s["z_kept"], h + 1)
                A.activation(z, z, ACT.Silu).then_inc(s["zs_made"], 1)

            def silu_qkv(h):
                act.wait_ge(s["conv_done"], h + 1)
                A.activation(qkv[:, :, 0:SEQ], acc[:, :, 0:SEQ], ACT.Silu).then_inc(s["silued"], 1)
                A.activation(qkv[:, :, SEQ:].rearrange("p s (b c) -> p s b c", c=DEC_SEQ), dec_acc, ACT.Silu).then_inc(s["silued"], 1)

            def norms(h):
                act.wait_ge(s["sums2"], h + 1)
                for j in range(2):
                    A.activation(rn[:, j, :], B[2 + j][:, 0:T_ALL], ACT.Ln, bias=m["eps"][:, 0:1]).then_inc(s["logs2"], 1)
                act.wait_ge(s["logs2"], 2 * h + 2)
                A.activation(rn[:], rn[:], ACT.Exp, scale=-0.5).then_inc(s["roots2"], 1)

            def decays(h):
                act.wait_ge(s["bcast"], h + 1)
                A.activation(eGB[:, :], B[2][:, 0:T_ALL], ACT.Exp).then_inc(s["eGB_made"], 1)
                act.wait_ge(s["D_in"], h + 1)
                A.activation(D[:, 0:256], D[:, 0:256], ACT.Exp).then_inc(s["D_made"], 1)
                A.activation(D[0:T_DEC, 256:], D[0:T_DEC, 256:], ACT.Exp).then_inc(s["D_made"], 1)

            def chain(h, prepare, projected):
                act.wait_ge(s["kv_T"], h + 1)
                for t in range(2):
                    kt, vt = B[6][:, 256 * t:256 * t + 128], B[6][:, 256 * t + 128:256 * t + 256]
                    A.activation(vb[:, t, :], vt, ACT.Copy, scale=beta[:, t, bass.ds(h, 1)]).then_inc(s["kv_kept"], 1)
                    A.activation(kg[:, t, :], kt, ACT.Copy, scale=beG[:, t, bass.ds(h, 1)]).then_inc(s["kv_kept"], 1)
                    A.activation(kd[:, t, :], kt, ACT.Copy, scale=eL[:, t, bass.ds(h, 1)]).then_inc(s["kv_kept"], 1)
                kt, vt = B[7][0:T_DEC, 0:128], B[7][0:T_DEC, 128:256]
                A.activation(vb[0:T_DEC, 2, :], vt, ACT.Copy, scale=beta[0:T_DEC, 2, bass.ds(h, 1)]).then_inc(s["kv_kept"], 1)
                A.activation(kg[0:T_DEC, 2, :], kt, ACT.Copy, scale=beG[0:T_DEC, 2, bass.ds(h, 1)]).then_inc(s["kv_kept"], 1)
                A.activation(kd[0:T_DEC, 2, :], kt, ACT.Copy, scale=eL[0:T_DEC, 2, bass.ds(h, 1)]).then_inc(s["kv_kept"], 1)
                act.wait_ge(s["ends_T"], h + 1)
                if not (isinstance(h, int) and h == 0):
                    act.wait_ge(s["ends_stored"], 32 * h)
                A.copy(ends_tok[:, :, :], B[7][0:27, 0:384].rearrange("p (s c) -> p s c", s=3)).then_inc(s["ends_kept"], 1)
                silu_z(h)
                if prepare:
                    silu_qkv(h + 1)
                if projected:
                    evacuate(h + 2, 0)
                    evacuate(h + 2, 1)
                if prepare:
                    norms(h + 1)
                if projected:
                    evacuate(h + 2, 2)
                if prepare:
                    decays(h + 1)
                if projected:
                    evacuate(h + 2, 3)
                act.wait_ge(s["osum_made"], h + 1)
                A.copy(osum[:, bass.ds(h, 1), :].rearrange("p o t -> p (o t)"), B[7][:, 0:T_ALL]).then_inc(s["osum_kept"], 1)

            for j in range(4):
                evacuate(0, j)
            act.wait_ge(s["decays_in"], 1)
            A.activation(eG[:], G[:], ACT.Exp).then_inc(s["decays_out"], 1)
            A.activation(eL[:], eL[:], ACT.Exp).then_inc(s["decays_out"], 1)
            A.activation(eLast[:], eLast[:], ACT.Exp).then_inc(s["decays_out"], 1)
            silu_qkv(0)
            for j in range(4):
                evacuate(1, j)
            norms(0)
            decays(0)
            chain(0, True, True)
            with act.Fori(1, H - 2) as h:
                chain(h, True, True)
            chain(H - 2, True, False)
            chain(H - 1, False, False)
            act.wait_ge(s["osum_kept"], H)
            for j in range(H // 2):
                v = osum[:, 2 * j:2 * j + 2, :]
                A.activation(v, v, ACT.Ln, scale=1.0 / DK, bias=m["eps"][:, 0:1]).then_inc(s["olog"], 1)
            for j in range(H // 2):
                v = osum[:, 2 * j:2 * j + 2, :]
                act.wait_ge(s["olog"], j + 1)
                A.activation(v, v, ACT.Exp, scale=-0.5).then_inc(s["oroot"], 1)

        @block.vector
        def _(dve):
            V = nc.vector
            st = {"base": 0, "n": 0}

            def link(ins):
                st["n"] += 1
                ins.then_inc(s["v"], 1)
                dve.wait_ge(s["v"], st["base"] + st["n"])

            V.memset(ss[:], 1.0).then_inc(s["squares"], 1)
            link(V.memset(ab[:], 0.0))
            link(V.memset(G[:], 0.0))
            link(V.memset(eL[:], 0.0))
            dve.wait_ge(s["squares"], NT + 1)
            V.tensor_scalar(ss[:, :], ss[:, :], 1.0 / D_MODEL, EPS, ALU.mult, ALU.add).then_inc(s["mean_made"], 1)
            dve.wait_ge(s["roots"], 1)
            link(V.reciprocal(ss[:, :], ss[:, :]))
            dve.wait_ge(s["consts_in"], 16 * 6)
            for t in range(NT):
                r = rows[t]
                if t:
                    dve.wait_ge(s["xT_made"], 2 * t)
                V.scalar_tensor_tensor(xn[0:r, :], resid[0:r, t, :], ss[0:r, t:t + 1], norm_b[0:r, :], ALU.mult, ALU.mult).then_inc(s["normed"], 1)
                dve.wait_ge(s["xT_made"], 2 * t + 1)
                V.tensor_copy(xT[:, 0:4, at[t]], B[0][:, :].rearrange("p (k r) -> p k r", k=4)[:, :, 0:r]).then_inc(s["xT_kept"], 1)
            dve.wait_ge(s["ab_made"], 1)
            for t in range(NT):
                r = rows[t]
                link(V.tensor_copy(ab[0:r, t, :], B[2][0:r, 16 * t:16 * t + 16]))

            def all_tiles(a):
                return a.unsqueeze(1).broadcast_to([128, NT, H])

            link(V.tensor_scalar(beta[:], ab[:, :, 0:H], -1.0, None, ALU.mult))
            link(V.tensor_tensor(g[:], ab[:, :, H:], all_tiles(ab_bias[:, 1, :]), ALU.add))
            link(V.tensor_scalar(gt2[:], g[:], -1.0, None, ALU.mult))
            V.tensor_tensor(gt[:], gt2[:], g[:], ALU.min).then_inc(s["exp_in"], 1)
            link(V.tensor_scalar(g[:], g[:], 0.0, None, ALU.max))
            dve.wait_ge(s["exp_out"], 3)
            V.tensor_scalar(gt[:], gt[:], 1.0, None, ALU.add).then_inc(s["soft_in"], 1)
            link(V.tensor_scalar(beta[:], beta[:], 1.0, None, ALU.add))
            link(V.reciprocal(beta[:], beta[:]))
            dve.wait_ge(s["soft_out"], 1)
            link(V.tensor_tensor(g[:], g[:], gt[:], ALU.add))
            link(V.tensor_tensor(g[:], g[:], all_tiles(ab_bias[:, 0, :]), ALU.mult))
            link(V.tensor_scalar(g[:], g[:], -1.0, None, ALU.mult))
            V.tensor_tensor(decg[:], g[0:T_DEC, 2, :].unsqueeze(1).broadcast_to([T_DEC, DEC_BATCH, H]),
                            m["dec_seq"][0:T_DEC, :].unsqueeze(2).broadcast_to([T_DEC, DEC_BATCH, H]), ALU.mult).then_inc(s["gates_made"], 1)
            dve.wait_ge(s["sums_made"], 1)
            for t in range(NT):
                r = rows[t]
                link(V.tensor_copy(G[0:r, t, :], B[2][0:r, 8 * t:8 * t + 8]))
                link(V.tensor_tensor(eL[0:r, t, :], B[2][0:r, 24 + 8 * t:32 + 8 * t], G[0:r, t, :], ALU.subtract))
            link(V.tensor_copy(eLast[:, 0:2, :], B[2][:, 24:40].rearrange("p (t h) -> p t h", t=2)))
            V.tensor_copy(eLast[:, 2:, :], B[2][:, 64:128].rearrange("p (b h) -> p b h", h=H)).then_inc(s["decays_in"], 1)
            dve.wait_ge(s["decays_out"], 3)
            link(V.tensor_tensor(beG[:], beta[:], eG[:], ALU.mult))

            def conv_rows(h):
                dve.wait_ge(s["st_T"], h + 1)
                v = B[7][:, 0:84].rearrange("p (s c) -> p s c", s=3)
                V.tensor_copy(cw[:, :, :], v[:, :, 24:28]).then_inc(s["rows_kept"], 1)
                for j in range(3):
                    V.tensor_copy(dec_cin[:, j, :, 0:3], v[:, j, 0:24].rearrange("p (b c) -> p b c", c=3)).then_inc(s["rows_kept"], 1)

            def conv(h, lo, hi):
                if lo == 0:
                    dve.wait_ge(s["rows_kept"], 4 * h + 4)
                    dve.wait_ge(s["proj_kept"], 6 * h + 6)
                    if not (isinstance(h, int) and h == 0):
                        dve.wait_ge(s["silued"], 2 * h)
                for step in range(lo, hi):
                    tap, j = divmod(step, 3)
                    src = cin[:, j, tap:tap + ACC_COLS]
                    if tap == 0:
                        ins = V.tensor_scalar(acc[:, j, 0:ACC_COLS], src, cw[:, j, 0:1], None, ALU.mult)
                    else:
                        ins = V.scalar_tensor_tensor(acc[:, j, 0:ACC_COLS], src, cw[:, j, tap:tap + 1], acc[:, j, 0:ACC_COLS], ALU.mult, ALU.add)
                    if step == 11:
                        ins.then_inc(s["conv_done"], 1)
                    elif j == 2 or step == hi - 1:
                        link(ins)

            def squares(h):
                dve.wait_ge(s["silued"], 2 * h + 2)
                V.tensor_tensor(qk2[:], qkv[:, 0:2, :], qkv[:, 0:2, :], ALU.mult).then_inc(s["squares2"], 1)

            def normed(h):
                dve.wait_ge(s["roots2"], h + 1)
                link(V.scalar_tensor_tensor(kbq[:, 1, :], qkv[:, 0, :], DK ** -0.5, rn[:, 0, :], ALU.mult, ALU.mult))
                V.tensor_tensor(kT[:, :], qkv[:, 1, :], rn[:, 1, :], ALU.mult).then_inc(s["kT_made"], 1)
                dve.wait_ge(s["kT_made"], h + 1)

            def decays(h):
                dve.wait_ge(s["bcast"], h + 1)
                V.tensor_tensor(kbq[:, 0, :], kT[:, :], B[3][:, 0:T_ALL], ALU.mult).then_inc(s["kb_made"], 1)
                dve.wait_ge(s["eGB_made"], h + 1)
                for t in range(NT):
                    r = rows[t]
                    ins = V.scalar_tensor_tensor(D[0:r, at[t]], B[2][0:r, at[t]], G[0:r, t, bass.ds(h, 1)], m["floor"][0:r, at[t]], ALU.subtract, ALU.min)
                    if t == 2:
                        ins.then_inc(s["D_in"], 1)

            def chain(h, prepare, projected):
                first = isinstance(h, int) and h == 0
                link(V.tensor_tensor(WQ[:, 1, :], kbq[:, 1, :], eGB[:, :], ALU.mult))
                dve.wait_ge(s["D_made"], 2 * h + 2)
                dve.wait_ge(s["KQ_made"], h + 1)
                link(V.tensor_tensor(KQD[:].rearrange("p t a i -> p t a i"), B[4][:, :].rearrange("p (t a i) -> p t a i", t=2, a=2),
                                     D[:, 0:256].rearrange("p (t i) -> p t i", t=2).unsqueeze(2).broadcast_to([128, 2, 2, 128]), ALU.mult))
                link(V.tensor_tensor(KQD2[:], B[5][0:T_DEC, 0:2 * T_DEC].rearrange("p (a i) -> p a i", a=2),
                                     D[0:T_DEC, 256:].unsqueeze(1).broadcast_to([T_DEC, 2, T_DEC]), ALU.mult))

                def joins(n):
                    mask = m["levels"][:, n, :].unsqueeze(1).broadcast_to([128, 2, 128])
                    return V.tensor_tensor(part(Mlev[:, n], n, 1), part(KQD[:, :, 0, :], n, 1), part(mask, n, 1), ALU.mult)

                if first:
                    dve.wait_ge(s["parts_clear"], 2)
                joins(0)
                for n in range(2):
                    last = V.tensor_tensor(M2[:, n, :], KQD2[:, 0, :], m["levels"][0:T_DEC, n, 0:T_DEC], ALU.mult)
                link(last)
                V.tensor_tensor(TU[:, :, 1, :], ident[:, :].unsqueeze(1).broadcast_to([128, 2, 128]), Mlev[:, 0], ALU.subtract)
                V.tensor_tensor(TU2[:, 1, :], ident[0:T_DEC, 0:T_DEC], M2[:, 0, :], ALU.subtract).then_inc(s["lev_made"], 1)
                joins(1).then_inc(s["joined"], 1)
                dve.wait_ge(s["T1_made"], h + 1)
                V.tensor_copy(TU[:, :, 0, :], B[4][:, 0:256].rearrange("p (t i) -> p t i", t=2)).then_inc(s["TU_kept"], 1)
                V.tensor_copy(TU2[:, 0, :], B[4][0:T_DEC, 256:288]).then_inc(s["TU_kept"], 1)
                for n in range(1, LEVELS):
                    k = (LEVELS - 1) * h + n
                    if n + 1 < LEVELS:
                        joins(n + 1).then_inc(s["joined"], 1)
                    dve.wait_ge(s["Y_made"], k)
                    V.tensor_copy(part(Y[:, n], n, 0), packed(B[4][:, 0:128], n)).then_inc(s["Y_kept"], 1)
                    if n == 1:
                        V.tensor_copy(Y2[:], B[4][0:T_DEC, 256:288]).then_inc(s["Y2_kept"], 1)
                    if prepare:
                        if n <= 3:
                            conv(h + 1, 4 * n - 4, 4 * n - 2)
                    dve.wait_ge(s["TU_made"], k)
                    if n < LEVELS - 1:
                        V.tensor_tensor(part(TU[:, :, 0, :], n, 0), part(TU[:, :, 0, :], n, 0), packed(B[5][:, 0:128], n), ALU.subtract).then_inc(s["T0_kept"], 1)
                    V.tensor_tensor(part(TU[:, :, 1, :], n, 1), part(TU[:, :, 1, :], n, 1), packed(B[5][:, 128:256], n), ALU.subtract).then_inc(s["TU_kept"], 1)
                    if n == 1:
                        V.tensor_tensor(TU2[:], TU2[:], B[7][0:T_DEC, 0:64].rearrange("p (a i) -> p a i", a=2), ALU.subtract).then_inc(s["TU_kept"], 1)
                    if prepare:
                        if n <= 3:
                            conv(h + 1, 4 * n - 2, 4 * n)
                        elif n == 4:
                            squares(h + 1)
                        elif n == 5 and projected:
                            conv_rows(h + 2)
                dve.wait_ge(s["W_made"], h + 1)
                V.tensor_scalar(WQ[:, 0, :], B[6][:, 0:T_ALL], -1.0, None, ALU.mult).then_inc(s["W_kept"], 1)
                dve.wait_ge(s["u0_made"], h + 1)
                V.tensor_copy(u[:, 0, :], B[7][:, 0:128]).then_inc(s["u_kept"], 1)
                if prepare:
                    normed(h + 1)
                dve.wait_ge(s["ws_made"], h + 1)
                V.tensor_copy(wsT[:], B[5][:, 0:64].rearrange("p (b a c) -> p a b c", a=2, c=DEC_SEQ)).then_inc(s["ws_kept"], 1)
                dve.wait_ge(s["S1_made"], h + 1)
                V.tensor_copy(S1[:, :], B[4][:, 0:128]).then_inc(s["S1_kept"], 1)
                dve.wait_ge(s["u2_made"], h + 1)
                V.tensor_copy(u[:, 1, :], B[7][:, 0:128]).then_inc(s["u_kept"], 1)
                V.tensor_copy(u[0:T_DEC, 2, :], B[7][0:T_DEC, 128:256]).then_inc(s["u_kept"], 1)
                dve.wait_ge(s["o_made"], h + 1)
                o = oT[:, bass.ds(h, 1), :].rearrange("p o t -> p (o t)")
                V.tensor_copy(o, B[6][:, 0:T_ALL]).then_inc(s["oT_kept"], 1)
                dve.wait_ge(s["oT_kept"], h + 1)
                V.tensor_tensor(o2[:, :], o, o, ALU.mult).then_inc(s["o2_made"], 1)
                dve.wait_ge(s["S2_made"], h + 1)
                if not first:
                    dve.wait_ge(s["S_stored"], 32 * h)
                V.scalar_tensor_tensor(S2[:, :], S1[:, :], eLast[:, 1, bass.ds(h, 1)], B[5][:, 0:128], ALU.mult, ALU.add).then_inc(s["S2_kept"], 1)
                if prepare:
                    decays(h + 1)
                dve.wait_ge(s["Sn_decayed"], h + 1)
                dve.wait_ge(s["Sn_made"], h + 1)
                for j in range(2):
                    V.tensor_tensor(Sn[:, 4 * j:4 * j + 4, :], Sn[:, 4 * j:4 * j + 4, :], B[4 + j][:, :].rearrange("p (b v) -> p b v", b=4), ALU.add).then_inc(s["Sn_kept"], 1)

            dve.wait_ge(s["prior_kept"], 1)
            conv_rows(0)
            conv(0, 0, 12)
            conv_rows(1)
            squares(0)
            normed(0)
            decays(0)
            chain(0, True, True)
            pre = st["n"]
            with dve.Fori(1, H - 2) as h:
                st["base"], st["n"] = (h - 1) * V_STEPS + pre, 0
                chain(h, True, True)
                assert st["n"] == V_STEPS, st["n"]
            st["base"], st["n"] = (H - 3) * V_STEPS + pre, 0
            chain(H - 2, True, False)
            chain(H - 1, False, False)
            for j in range(H // 2):
                v, o, z = (x[:, 2 * j:2 * j + 2, :] for x in (osum, oT, ozT))
                dve.wait_ge(s["oroot"], j + 1)
                link(V.tensor_tensor(v, v, o, ALU.mult))
                if j == 0:
                    dve.wait_ge(s["zs_made"], H)
                V.scalar_tensor_tensor(z, v, onorm[:, 0:1], z, ALU.mult, ALU.mult).then_inc(s["oz_made"], 1)
            for t in range(NT):
                r = rows[t]
                for j in range(2):
                    dve.wait_ge(s["out_made"], 2 * t + j + 1)
                    out = B[2 * t + j] if t < 2 else B[4 + j]
                    V.tensor_tensor(resid[0:r, t, 512 * j:512 * j + 512], resid[0:r, t, 512 * j:512 * j + 512], out[0:r, :], ALU.add).then_inc(s["out_kept"], 1)
            dve.wait_ge(s["out_kept"], 2 * NT)

        @block.tensor
        def _(pe):
            T = nc.tensor
            xv = xn[:, :].rearrange("p (c k) -> p k c", k=KT)
            for t in range(NT):
                r = rows[t]
                pe.wait_ge(s["normed"], t + 1)
                if t:
                    pe.wait_ge(s["xT_kept"], 2 * t)
                for k in range(KT):
                    last = T.transpose(B[k // 4][:, 128 * (k % 4):128 * (k % 4) + r], xv[0:r, k, :], ident[0:r, 0:r])
                    if k % 4 == 3:
                        last.then_inc(s["xT_made"], 1)
            pe.wait_ge(s["xT_kept"], 2 * NT)
            for t in range(NT):
                for k in range(KT):
                    last = T.matmul(B[2][0:rows[t], 16 * t:16 * t + 16], xT[:, k, at[t]], w_ab[:, k, :], start=(k == 0), stop=(k == KT - 1))
            last.then_inc(s["ab_made"], 1)

            def project(h, j, lo=0, hi=KT):
                if lo == 0:
                    first = isinstance(h, int) and h == 0
                    pe.wait_ge(slot_in[j], 16 * h + 16)
                    if j == 0 and not first:
                        pe.wait_ge(s["proj_kept"], 6 * h)
                    elif j == 1 and not first:
                        pe.wait_ge(s["z_kept"], h)
                    elif j == 2:
                        pe.wait_ge(s["proj_kept"], 6 * h + 2)
                    elif j == 3:
                        pe.wait_ge(s["proj_kept"], 6 * h + 4)
                for k in range(lo, hi):
                    last = T.matmul(B[j % 2][:, 0:T_ALL], w4[:, j, k, :], xT[:, k, :], start=(k == 0), stop=(k == KT - 1))
                if hi == KT:
                    last.then_inc(s["proj"], 1)

            def conv_rows():
                for j in range(3):
                    last = T.transpose(B[7][:, 28 * j:28 * j + 28], st_in[:, j, :], ident[0:28, 0:28])
                last.then_inc(s["st_T"], 1)

            def norm_sums(h):
                pe.wait_ge(s["squares2"], h + 1)
                for j in range(2):
                    last = T.matmul(B[2 + j][:, 0:T_ALL], ones[:, :], qk2[:, j, :], start=True, stop=True)
                last.then_inc(s["sums2"], 1)

            def broadcasts(h):
                pe.wait_ge(s["src_made"], 6 * h + 6)
                pe.wait_ge(s["roots2"], h + 1)
                for src, bank in ((gsrc, 2), (bsrc, 3)):
                    for t in range(NT):
                        last = T.matmul(B[bank][:, at[t]], ones[0:rows[t], :], src[0:rows[t], at[t]], start=True, stop=True)
                last.then_inc(s["bcast"], 1)

            def chain(h, prepare, projected):
                first = isinstance(h, int) and h == 0
                pe.wait_ge(s["kT_made"], h + 1)
                if not first:
                    pe.wait_ge(s["oT_kept"], h)
                    pe.wait_ge(s["osum_kept"], h)
                for t in range(2):
                    T.transpose(B[6][:, 256 * t:256 * t + 128], kT[:, at[t]], ident[:, :])
                    T.transpose(B[6][:, 256 * t + 128:256 * t + 256], qkv[:, 2, at[t]], ident[:, :])
                T.transpose(B[7][0:T_DEC, 0:128], kT[:, at[2]], ident[:, :])
                T.transpose(B[7][0:T_DEC, 128:256], qkv[:, 2, at[2]], ident[:, :]).then_inc(s["kv_T"], 1)
                pe.wait_ge(s["kb_made"], h + 1)
                if not first:
                    pe.wait_ge(s["Sn_kept"], 2 * h)
                for t in range(2):
                    T.matmul(B[4][:, 256 * t:256 * t + 256].rearrange("p (a i) -> p a i", a=2), kT[:, at[t]], kbq[:, :, at[t]], start=True, stop=True)
                T.matmul(B[5][0:T_DEC, 0:64].rearrange("p (a i) -> p a i", a=2), kT[:, at[2]], kbq[:, :, at[2]], start=True, stop=True).then_inc(s["KQ_made"], 1)
                if projected:
                    project(h + 2, 0, 0, 3)
                pe.wait_ge(s["ends_copied"], 4 * h + 4)
                pe.wait_ge(s["kv_kept"], 9 * h + 9)
                for j in range(3):
                    last = T.transpose(B[7][0:27, 128 * j:128 * j + 128], ends[:, j, :], ident[:, :])
                last.then_inc(s["ends_T"], 1)
                pe.wait_ge(s["lev_made"], h + 1)
                for t in range(2):
                    T.transpose(B[4][:, 128 * t:128 * t + 128], TU[:, t, 1, :], ident[:, :])
                T.transpose(B[4][0:T_DEC, 256:288], TU2[:, 1, :], ident[0:T_DEC, 0:T_DEC]).then_inc(s["T1_made"], 1)
                if projected:
                    project(h + 2, 0, 3, 5)
                fill = {1: ((0, 5, 6), (0, 6, 8)), 2: ((1, 0, 2), (1, 2, 4)), 3: ((1, 4, 6), (1, 6, 8)), 5: ((2, 0, 2), (2, 2, 4)), 6: ((2, 4, 6), (2, 6, 8))}
                for n in range(1, LEVELS):
                    k = (LEVELS - 1) * h + n
                    kept = (LEVELS + 2) * h + n + (1 if n == 1 else 2)
                    pe.wait_ge(s["TU_kept"], kept)
                    pe.wait_ge(s["joined"], (LEVELS - 1) * h + n)
                    if n == 4 and projected:
                        pe.wait_ge(s["st_loaded"], 32 * h + 96)
                    for t in range(2):
                        last = T.matmul(packed(B[4][:, 0:128], n)[:, t], Mlev[:, n, t, :], part(TU[:, :, 0, :], n, 0)[:, t], start=True, stop=True)
                    if n == 1:
                        last = T.matmul(B[4][0:T_DEC, 256:288], M2[:, 1, :], TU2[:, 0, :], start=True, stop=True)
                    last.then_inc(s["Y_made"], 1)
                    if projected and n in fill:
                        project(h + 2, *fill[n][0])
                    pe.wait_ge(s["Y_kept"], k)
                    if n == 1:
                        pe.wait_ge(s["Y2_kept"], h + 1)
                        pe.wait_ge(s["ends_kept"], h + 1)
                    for t in range(2):
                        if n < LEVELS - 1:
                            T.matmul(packed(B[5][:, 0:128], n)[:, t], TU[:, t, 1, :], part(Y[:, n], n, 0)[:, t], start=True, stop=True)
                        last = T.matmul(packed(B[5][:, 128:256], n)[:, t], Y[:, n, t, :], part(TU[:, :, 1, :], n, 1)[:, t], start=True, stop=True)
                    if n == 1:
                        T.matmul(B[7][0:T_DEC, 0:32], TU2[:, 1, :], Y2[:, :], start=True, stop=True)
                        last = T.matmul(B[7][0:T_DEC, 32:64], Y2[:, :], TU2[:, 1, :], start=True, stop=True)
                    last.then_inc(s["TU_made"], 1)
                    if n == 4 and projected:
                        conv_rows()
                    if n == 5 and prepare:
                        norm_sums(h + 1)
                    if projected and n in fill:
                        project(h + 2, *fill[n][1])
                pe.wait_ge(s["TU_kept"], (LEVELS + 2) * h + LEVELS + 2)
                for t in range(NT):
                    r = rows[t]
                    inv = TU[:, t, 1, :] if t < 2 else TU2[:, 1, :]
                    last = T.matmul(B[6][:, at[t]], kg[0:r, t, :], inv, start=True, stop=True)
                last.then_inc(s["W_made"], 1)
                if projected:
                    pe.wait_ge(s["rows_kept"], 4 * h + 12)
                T.matmul(B[7][:, 0:128], TU[:, 0, 1, :], vb[:, 0, :], start=True, stop=True).then_inc(s["u0_made"], 1)
                if prepare:
                    broadcasts(h + 1)
                pe.wait_ge(s["W_kept"], h + 1)
                pe.wait_ge(s["Sd_in"], 16 * h + 16)
                for b in range(DEC_BATCH):
                    c = SEQ + DEC_SEQ * b
                    last = T.matmul(B[5][:, 8 * b:8 * b + 8].rearrange("p (a c) -> p a c", a=2), Sd[:, b, :], WQ[:, :, c:c + DEC_SEQ], start=True, stop=True)
                last.then_inc(s["ws_made"], 1)
                pe.wait_ge(s["u_kept"], 3 * h + 1)
                T.matmul(B[4][:, 0:128], kd[:, 0, :], u[:, 0, :], start=True, stop=True).then_inc(s["S1_made"], 1)
                if projected:
                    project(h + 2, 3, 0, 3)
                pe.wait_ge(s["S1_kept"], h + 1)
                pe.wait_ge(s["ws_kept"], h + 1)
                T.matmul(B[7][:, 0:128], TU[:, 1, 1, :], vb[:, 1, :], start=True, stop=False)
                T.matmul(B[7][:, 0:128], WQ[:, 0, at[1]], S1[:, :], start=False, stop=True)
                T.matmul(B[7][0:T_DEC, 128:256], TU2[:, 1, :], vb[0:T_DEC, 2, :], start=True, stop=False)
                T.matmul(B[7][0:T_DEC, 128:256], wsT[:, 0, :], ident[:, :], start=False, stop=True).then_inc(s["u2_made"], 1)
                T.matmul(B[6][:, at[0]], u[:, 0, :], KQD[:, 0, 1, :], start=True, stop=True)
                if projected:
                    project(h + 2, 3, 3, 6)
                pe.wait_ge(s["u_kept"], 3 * h + 3)
                T.matmul(B[6][:, at[1]], u[:, 1, :], KQD[:, 1, 1, :], start=True, stop=False)
                T.matmul(B[6][:, at[1]], S1[:, :], WQ[:, 1, at[1]], start=False, stop=True)
                T.matmul(B[6][:, at[2]], u[0:T_DEC, 2, :], KQD2[:, 1, :], start=True, stop=False)
                T.matmul(B[6][:, at[2]], ident[:, :], wsT[:, 1, :], start=False, stop=True).then_inc(s["o_made"], 1)
                T.matmul(B[5][:, 0:128], kd[:, 1, :], u[:, 1, :], start=True, stop=True).then_inc(s["S2_made"], 1)
                if projected:
                    project(h + 2, 3, 6, 8)
                pe.wait_ge(s["o2_made"], h + 1)
                T.matmul(B[7][:, 0:T_ALL], ones[:, :], o2[:, :], start=True, stop=True).then_inc(s["osum_made"], 1)
                pe.wait_ge(s["uB_made"], h + 1)
                pe.wait_ge(s["S2_kept"], h + 1)
                for j in range(2):
                    last = T.matmul(B[4 + j][:, :], kd[0:T_DEC, 2, :], uB[:, 4 * j:4 * j + 4, :], start=True, stop=True)
                last.then_inc(s["Sn_made"], 1)

            for j in range(4):
                project(0, j)
            pe.wait_ge(s["st_loaded"], 32)
            conv_rows()
            pe.wait_ge(s["gates_made"], 1)
            for t in range(NT):
                r = rows[t]
                T.matmul(B[2][0:r, 8 * t:8 * t + 8], m["upto"][0:r, at[t]], g[0:r, t, :], start=True, stop=True)
                T.matmul(B[2][0:r, 24 + 8 * t:32 + 8 * t], ones[:, :] if t < 2 else m["dec_same"][0:r, :], g[0:r, t, :], start=True, stop=True)
            T.matmul(B[2][:, 64:128], ones[0:T_DEC, :], decg[:, :, :].rearrange("p b h -> p (b h)"), start=True, stop=True).then_inc(s["sums_made"], 1)
            for j in range(4):
                project(1, j)
            pe.wait_ge(s["rows_kept"], 4)
            pe.wait_ge(s["st_loaded"], 64)
            conv_rows()
            norm_sums(0)
            broadcasts(0)
            chain(0, True, True)
            with pe.Fori(1, H - 2) as h:
                chain(h, True, True)
            chain(H - 2, True, False)
            chain(H - 1, False, False)
            pe.wait_ge(s["wout_in"], 16)
            for t in range(NT):
                for j in range(2):
                    for h in range(H):
                        if t == 0 and j == 0 and h % 2 == 0:
                            pe.wait_ge(s["oz_made"], h // 2 + 1)
                        last = T.matmul((B[2 * t + j] if t < 2 else B[4 + j])[0:rows[t], :], ozT[:, h, at[t]], w_out[:, h, 512 * j:512 * j + 512], start=(h == 0), stop=(h == H - 1))
                    last.then_inc(s["out_made"], 1)

    nc.clear_and_free_semaphores(sems)
    nc.all_engine_barrier(sem_only=True)


LAM_INIT = 0.8 - 0.6 * math.exp(-0.3 * 1)
ROPE_THETA = 10000.0
SCORES = 128 + 256
S_STEPS = 5
P_STEPS = 8


def attn_constants():
    c = {}
    half = DH // 2
    p = np.arange(128)
    pos = np.stack([p, 128 + p, PAST_LEN + p % DEC_SEQ], 1).astype(np.float32)
    inv = (np.float32(ROPE_THETA) ** (-np.arange(half, dtype=np.float32) / np.float32(half))).astype(np.float32)
    ang = pos[:, :, None] * inv
    c["cos"] = np.cos(ang)
    c["sin"] = np.sin(ang)
    causal = np.where(p[None, :] <= p[:, None], 0.0, -FAR)
    c["causal"] = np.concatenate([causal, np.zeros((128, 128)), causal], 1)
    rb, rc, rh, rq = p // 64, (p // 32) % 2, (p // 4) % 8, p % 4
    kb, kq = np.arange(T_DEC) // DEC_SEQ, np.arange(T_DEC) % DEC_SEQ
    pair = np.arange(DEC_BATCH // 2)
    seen = (kb[None, None, :] == 2 * pair[None, :, None] + rb[:, None, None]) & (kq[None, None, :] <= rq[:, None, None])
    c["new_keys"] = np.where(seen, 0.0, -FAR)
    col = np.arange(64)
    c["halves"] = (rb[:, None] == col // 32) & (rh[:, None] == (col // 4) % 8) & (rq[:, None] == col % 4)
    c["first_half"] = rc[:, None] == 0
    c["second_half"] = rc[:, None] == 1
    return c


def attn_phase(nc, m):
    ctx, sems = ExitStack(), []
    with ctx:
        def sb(name, shape, dt=F32):
            return ctx.enter_context(nc.sbuf_tensor(f"at_{name}", shape, dt))

        def sem(name):
            sems.append(nc.alloc_semaphore(f"at_{name}"))
            return sems[-1]

        NT, rows, H = TOK_TILES, TILE_ROWS, HEADS
        at = [slice(128 * t, 128 * t + rows[t]) for t in range(NT)]
        resid, ident, ones = m["resid"], m["ident"], m["ones"]
        ss = sb("ss", [128, NT])
        gains = sb("gains", [128, 2, KT])
        XK = sb("XK", [128, 2, KT, T_ALL])
        kvq = [sb(n, [128, NT, D_MODEL]) for n in ("k", "v", "q")]
        k_t, v_t, q_t = kvq
        rot = sb("rot", [128, 512])
        rot2 = sb("rot2", [128, 512])
        lam_in = sb("lam_in", [128, 4, DH])
        lam = sb("lam", [128, 4])
        coef = sb("coef", [128, 1])
        pages = sb("pages", [1, DEC_BATCH * N_PAGES], I32)
        subln = sb("subln", [128, 1])
        qTd = sb("qTd", [128, H, T_DEC])
        QBs = sb("QBs", [128, 2, H, 64])
        P = sb("P", [128, SCORES * 2])
        aT = sb("aT", [128, 3, 128])
        mx = sb("mx", [128, 4])
        sm = sb("sm", [128, 4])
        o_ss = sb("o_ss", [128, 2, H])
        oT = sb("oT", [128, H, T_ALL])
        qk_h = sb("qk_h", [128, 2, 2, 128])
        qkT = sb("qkT", [128, 2, 256])
        o_t = q_t
        flat = [m["ring"][n][:].rearrange("p a n -> p (a n)") for n in range(3)]
        wslot = [flat[0][:, 0:4096], flat[0][:, 4096:], flat[1][:, 0:4096]]
        wslot = [w.rearrange("p (k n) -> p k n", k=KT) for w in wslot]
        xh = flat[2][:, 0:1024]
        sq = flat[2][:, 1024:2048]
        QB = flat[1][:, 4096:].rearrange("p (b h r) -> p b h r", b=DEC_BATCH, h=H)
        Kc = flat[2][:, 0:4096].rearrange("p (b i n) -> p b i n", b=2, i=N_PAGES)
        Vc = flat[2][:, 4096:].rearrange("p (b i n) -> p b i n", b=2, i=N_PAGES)
        w_out = flat[0].rearrange("p (h n) -> p h n", h=H)
        o_sq = P[:, 0:512]

        B = [ctx.enter_context(nc.psum_tensor(f"at_bank{i}", [128, 512], F32)) for i in range(2)]
        BB = ctx.enter_context(nc.psum_tensor("at_pair", [128, 2, 512], F32))
        B += [None, None] + [ctx.enter_context(nc.psum_tensor(f"at_bank{i}", [128, 512], F32)) for i in range(4, 8)]
        B[2], B[3] = BB[:, 0, :], BB[:, 1, :]

        s = {n: sem(n) for n in (
            "consts_in w0_in w1_in w2_in squares mean_made roots xh_made xT_made xT_kept lam_in lam_out kv_made kv_kept rotated q_rotated stored "
            "dT_made dT_kept QB_clear QB_made K0_in V0_in KT_made KT_kept QBs_made S_made S_kept S_exp a_made aT_made aT_kept od_made od_kept "
            "rows_kept od_T od_sq od_sum od_root od_done sliced qk_T qkT_kept sc_made sc_kept sc_exp pa_made paT_made paT_kept o_made o_kept on_sq on_root on_made onT_made onT_kept "
            "wout_in out_made out_kept v").split()}
        w_kv = m["w_kv"].rearrange("(p t) n -> p t n", t=KT)
        w_q = m["w_q_b"][0].rearrange("(p t) n -> p t n", t=KT)
        w_src = [w_kv[:, :, 0:D_MODEL], w_kv[:, :, D_MODEL:], w_q]
        slot_in = [s["w0_in"], s["w1_in"], s["w2_in"]]
        outs = [(m["k_prompt"][0].rearrange("l h e -> l (h e)"), m["k_sample"].rearrange("b l h e -> (b l) (h e)")),
                (m["v_prompt"][0].rearrange("l h e -> l (h e)"), m["v_sample"].rearrange("b l h e -> (b l) (h e)"))]
        caches = [m["cache_k"].rearrange("n s h e -> s n (h e)"), m["cache_v"].rearrange("n s h e -> s n (h e)")]
        PAIRS = DEC_BATCH // 2

        def kbank(t):
            return (B[0], B[1], B[2])[t]

        def vbank(t):
            return (B[3], B[4], B[5])[t]

        def qbank(t):
            return (B[6], B[7], B[0])[t]

        def later(step):
            return not (isinstance(step, int) and step == 0)

        block = ctx.enter_context(nc.Block())

        @block.sync
        def _(sp):
            sp.dma_start(gains[:, 0, :], m["kv_norm"].rearrange("(p t) -> p t", t=KT)).then_inc(s["consts_in"], 16)
            sp.dma_start(gains[:, 1, :], m["norm_b"][0].rearrange("(p t) -> p t", t=KT)).then_inc(s["consts_in"], 16)
            sp.dma_start(lam_in[:].rearrange("p a d -> p (a d)"), m["lam_b"].rearrange("a l d -> a (l d)").broadcast_to([128, 4 * DH])).then_inc(s["consts_in"], 16)
            sp.dma_start(subln[:], m["subln_b"].rearrange("a v -> v a")).then_inc(s["consts_in"], 16)
            sp.dma_start(pages[:], m["page_table"].rearrange("(a b) i -> a (b i)", a=1)).then_inc(s["consts_in"], 16)

            def weights(half, first=False):
                for j in range(3):
                    if not first:
                        sp.wait_ge(s["kv_made"], 9 * half - 6 + 3 * j)
                    sp.dma_start(wslot[j], w_src[j][:, :, 512 * half:512 * half + 512]).then_inc(slot_in[j], 16)

            weights(0, True)
            weights(1)
            for j in range(2):
                for t in range(NT):
                    sp.wait_ge((s["rotated"], s["kv_kept"])[j], 6)
                    dst = outs[j][0][at[t], :] if t < 2 else outs[j][1]
                    sp.dma_start(dst, kvq[j][0:rows[t], t, :]).then_inc(s["stored"], 16)

            def cache(j, pair, later):
                for b in range(2):
                    for i in range(N_PAGES):
                        page = sp.value_load(pages[0:1, bass.ds(4 * pair + 2 * b + i, 1)], min_val=0, max_val=N_PHYS - 1)
                        if later and b == 0 and i == 0:
                            if j == 0:
                                sp.wait_ge(s["KT_made"], 8 * pair)
                            else:
                                sp.wait_ge(s["od_made"], pair)
                        dst = (Kc, Vc)[j][:, b, i, :]
                        sp.dma_start(dst, caches[j][:, bass.ds(page, 1), :].rearrange("s o n -> s (o n)")).then_inc((s["K0_in"], s["V0_in"])[j], 16)

            sp.wait_ge(s["consts_in"], 16 * 5)
            sp.wait_ge(s["xT_made"], 2 * NT)
            cache(0, 0, False)
            cache(1, 0, False)
            with sp.Fori(1, PAIRS) as pair:
                cache(0, pair, True)
                cache(1, pair, True)
            sp.wait_ge(s["kv_made"], 18)
            sp.dma_start(w_out, m["w_out_b"][0].rearrange("(h p) n -> p h n", p=128)).then_inc(s["wout_in"], 16)
            sp.wait_ge(s["QBs_made"], PAIRS)
            m["prefetch"](sp, 1, (1,))
            sp.wait_ge(s["od_made"], PAIRS)
            m["prefetch"](sp, 1, (2,))
            sp.wait_ge(s["stored"], 16 * 2 * NT)
            sp.wait_ge(s["out_made"], 2 * NT)
            m["prefetch"](sp, 1, (0,))

        @block.gpsimd
        def _(pool):
            nc.gpsimd.memset(QB[:, :, :, :], 0.0).then_inc(s["QB_clear"], 1)
            pool.wait_ge(s["QB_made"], 2 * H)

            def queries(pair):
                if later(pair):
                    pool.wait_ge(s["S_made"], pair)
                nc.gpsimd.tensor_copy(QBs[:, :, :, :], QB[:, bass.ds(2 * pair, 2), :, :]).then_inc(s["QBs_made"], 1)

            queries(0)
            with pool.Fori(1, PAIRS) as pair:
                queries(pair)

            def cut(h):
                if later(h):
                    pool.wait_ge(s["qk_T"], h)
                nc.gpsimd.tensor_copy(qk_h[:, 0, :, :], q_t[:, 0:2, bass.ds(128 * h, 128)]).then_inc(s["sliced"], 1)
                nc.gpsimd.tensor_copy(qk_h[:, 1, :, :], k_t[:, 0:2, bass.ds(128 * h, 128)]).then_inc(s["sliced"], 1)

            cut(0)
            with pool.Fori(1, H) as h:
                cut(h)

        @block.scalar
        def _(act):
            A = nc.scalar
            act.wait_ge(s["squares"], 1)
            for t in range(NT):
                r = rows[t]
                A.activation(sq[0:r, :], resid[0:r, t, :], ACT.Square, accum_out=ss[0:r, t:t + 1]).then_inc(s["squares"], 1)
                act.wait_ge(s["squares"], t + 2)
            act.wait_ge(s["mean_made"], 1)
            A.activation(ss[:, :], ss[:, :], ACT.Sqrt).then_inc(s["roots"], 1)
            act.wait_ge(s["lam_in"], 1)
            A.activation(lam[:, 0:2], lam[:, 0:2], ACT.Exp).then_inc(s["lam_out"], 1)
            for half in range(2):
                for t in range(NT):
                    act.wait_ge(s["kv_made"], 9 * half + 3 + t + 1)
                    A.copy(v_t[0:rows[t], t, 512 * half:512 * half + 512], vbank(t)[0:rows[t], :]).then_inc(s["kv_kept"], 1)
            act.wait_ge(s["dT_made"], 1)
            A.copy(qTd[:, :, :], B[4][:, 0:256].rearrange("p (h r) -> p h r", h=H)).then_inc(s["dT_kept"], 1)
            for b in range(2):
                A.copy(XK[:, b, :, PAST_LEN:], B[5][:, 0:256].rearrange("p (h r) -> p h r", h=H)).then_inc(s["dT_kept"], 1)
            def samples(pair):
                for b in range(2):
                    for j in (1, 3):
                        act.wait_ge(s["KT_made"], 8 * pair + 4 * b + j + 1)
                        if later(pair) and b == 0 and j == 1:
                            act.wait_ge(s["S_made"], pair)
                        A.copy(XK[:, b, 2 * j:2 * j + 2, 0:PAST_LEN], B[4 + j][:, :].rearrange("p (h r) -> p h r", h=2)).then_inc(s["KT_kept"], 1)
                act.wait_ge(s["S_kept"], pair + 1)
                A.activation(P[:, 0:T_ALL], P[:, 0:T_ALL], ACT.Exp, bias=mx[:, 1:2], scale=DH ** -0.5, accum_out=sm[:, 0:1]).then_inc(s["S_exp"], 1)

            samples(0)
            with act.Fori(1, PAIRS) as pair:
                samples(pair)
            act.wait_ge(s["od_sum"], 1)
            A.activation(rot[:, 0:256], B[0][:, 0:256], ACT.Sqrt, scale=1.0 / DK, bias=m["eps"][:, 0:1]).then_inc(s["od_root"], 1)

            def turned(h):
                act.wait_ge(s["qk_T"], h + 1)
                A.copy(qkT[:, 0, :], B[4][:, 0:256]).then_inc(s["qkT_kept"], 1)
                A.copy(qkT[:, 1, :], B[4][:, 256:512]).then_inc(s["qkT_kept"], 1)

            def head(h, more):
                act.wait_ge(s["sc_kept"], h + 1)
                for t in range(2):
                    for c in range(2):
                        lo = SCORES * c + 128 * t
                        n = 128 * (t + 1)
                        A.activation(P[:, lo:lo + n], P[:, lo:lo + n], ACT.Exp, bias=mx[:, 2 * t + c:2 * t + c + 1],
                                     scale=DH ** -0.5, accum_out=sm[:, 2 * t + c:2 * t + c + 1]).then_inc(s["sc_exp"], 1)
                if more:
                    turned(h + 1)
                act.wait_ge(s["paT_made"], h + 1)
                A.copy(aT[:, :, :], B[6][:, 0:384].rearrange("p (j r) -> p j r", j=3)).then_inc(s["paT_kept"], 1)
                act.wait_ge(s["o_made"], h + 1)
                A.copy(o_t[:, 0:2, bass.ds(128 * h, 128)], B[7][:, 0:256].rearrange("p (t e) -> p t e", t=2)).then_inc(s["o_kept"], 1)

            turned(0)
            head(0, True)
            with act.Fori(1, H - 1) as h:
                head(h, True)
            head(H - 1, False)
            act.wait_ge(s["on_sq"], 1)
            A.activation(o_ss[:, :, :], o_ss[:, :, :], ACT.Sqrt, scale=1.0 / DK, bias=m["eps"][:, 0:1]).then_inc(s["on_root"], 1)
            for t in range(2):
                for j in range(2):
                    act.wait_ge(s["onT_made"], 2 * t + j + 1)
                    A.activation(oT[:, 4 * j:4 * j + 4, at[t]], B[2 * t + j][:, :].rearrange("p (h r) -> p h r", h=4), ACT.Copy, scale=subln[:, 0:1]).then_inc(s["onT_kept"], 1)

        @block.vector
        def _(dve):
            V = nc.vector
            st = {"base": 0, "n": 0}

            def link(ins):
                st["n"] += 1
                ins.then_inc(s["v"], 1)
                dve.wait_ge(s["v"], st["base"] + st["n"])

            V.memset(ss[:], 1.0).then_inc(s["squares"], 1)
            dve.wait_ge(s["consts_in"], 16 * 5)
            for j in range(2):
                link(V.tensor_tensor(lam_in[:, 2 * j, :], lam_in[:, 2 * j, :], lam_in[:, 2 * j + 1, :], ALU.mult))
                ins = V.tensor_reduce(lam[:, j:j + 1], lam_in[:, 2 * j, :], AX.X, ALU.add)
                ins.then_inc(s["lam_in"], 1) if j else link(ins)
            dve.wait_ge(s["squares"], NT + 1)
            V.tensor_scalar(ss[:, :], ss[:, :], 1.0 / D_MODEL, EPS, ALU.mult, ALU.add).then_inc(s["mean_made"], 1)
            dve.wait_ge(s["roots"], 1)
            link(V.reciprocal(ss[:, :], ss[:, :]))
            for t in range(NT):
                r = rows[t]
                if t:
                    dve.wait_ge(s["xT_made"], 2 * t)
                V.tensor_scalar(xh[0:r, :], resid[0:r, t, :], ss[0:r, t:t + 1], None, ALU.mult).then_inc(s["xh_made"], 1)
                for j in range(2):
                    dve.wait_ge(s["xT_made"], 2 * t + j + 1)
                    for x in range(2):
                        V.tensor_tensor(XK[:, x, 4 * j:4 * j + 4, at[t]], B[j][:, :].rearrange("p (k r) -> p k r", k=4)[:, :, 0:r],
                                        gains[:, x, 4 * j:4 * j + 4].unsqueeze(2).broadcast_to([128, 4, r]), ALU.mult).then_inc(s["xT_kept"], 1)
            dve.wait_ge(s["lam_out"], 1)
            link(V.tensor_tensor(lam[:, 2:3], lam[:, 1:2], lam[:, 0:1], ALU.subtract))
            link(V.tensor_scalar(lam[:, 2:3], lam[:, 2:3], -LAM_INIT, None, ALU.add))
            link(V.scalar_tensor_tensor(coef[:, :], m["second_half"][:, :], lam[:, 2:3], m["first_half"][:, :], ALU.mult, ALU.add))
            link(V.tensor_scalar(subln[:, :], subln[:, :], 1.0 - LAM_INIT, None, ALU.mult))

            def rotate(half, dst, bank, t):
                r = rows[t]
                G = 512 // DH
                x = bank[0:r, :].rearrange("p (g a d) -> p g a d", g=G, a=2)
                c, sn = (a[0:r, t, :].unsqueeze(1).broadcast_to([r, G, DH // 2]) for a in (m["cos"], m["sin"]))
                y = rot[0:r, :].rearrange("p (g a d) -> p g a d", g=G, a=2)
                z = rot2[0:r, :].rearrange("p (g a d) -> p g a d", g=G, a=2)
                o = dst[0:r, t, 512 * half:512 * half + 512].rearrange("p (g a d) -> p g a d", g=G, a=2)
                for a in range(2):
                    V.tensor_tensor(y[:, :, a, :], x[:, :, a, :], c, ALU.mult)
                    last = V.tensor_tensor(z[:, :, a, :], x[:, :, 1 - a, :], sn, ALU.mult)
                    if a:
                        link(last)
                V.tensor_tensor(o[:, :, 0, :], y[:, :, 0, :], z[:, :, 0, :], ALU.subtract)
                V.tensor_tensor(o[:, :, 1, :], y[:, :, 1, :], z[:, :, 1, :], ALU.add).then_inc(s["rotated"] if dst is k_t else s["q_rotated"], 1)

            for half in range(2):
                for j, (dst, bank, done) in enumerate(((k_t, kbank, s["rotated"]), (q_t, qbank, s["q_rotated"]))):
                    for t in range(NT):
                        dve.wait_ge(s["kv_made"], 9 * half + 6 * j + t + 1)
                        rotate(half, dst, bank(t), t)
                        dve.wait_ge(done, 3 * half + t + 1)
            dve.wait_ge(s["dT_kept"], 3)
            dve.wait_ge(s["QB_clear"], 1)
            for c in range(2):
                for h in range(H):
                    V.tensor_copy(QB[64 * c:64 * c + 64, :, h, 32 * c + 4 * h:32 * c + 4 * h + 4],
                                  qTd[64 * c:64 * c + 64, h, :].rearrange("p (b q) -> p b q", q=DEC_SEQ)).then_inc(s["QB_made"], 1)
            pre = st["n"]

            def samples(pair):
                for b in range(2):
                    for j in (0, 2):
                        dve.wait_ge(s["KT_made"], 8 * pair + 4 * b + j + 1)
                        if later(pair) and b == 0 and j == 0:
                            dve.wait_ge(s["S_made"], pair)
                        V.tensor_copy(XK[:, b, 2 * j:2 * j + 2, 0:PAST_LEN], B[4 + j][:, :].rearrange("p (h r) -> p h r", h=2)).then_inc(s["KT_kept"], 1)
                dve.wait_ge(s["S_made"], pair + 1)
                if later(pair):
                    dve.wait_ge(s["aT_made"], pair)
                link(V.tensor_copy(P[:, 0:PAST_LEN], B[0][:, 0:PAST_LEN]))
                link(V.tensor_tensor(P[:, PAST_LEN:T_ALL], B[0][:, PAST_LEN:T_ALL], m["new_keys"][:, bass.ds(pair, 1), :].rearrange("p o k -> p (o k)"), ALU.add))
                link(V.tensor_reduce(mx[:, 0:1], P[:, 0:T_ALL], AX.X, ALU.max))
                V.tensor_scalar(mx[:, 1:2], mx[:, 0:1], -(DH ** -0.5), None, ALU.mult).then_inc(s["S_kept"], 1)
                dve.wait_ge(s["S_exp"], pair + 1)
                link(V.reciprocal(sm[:, 1:2], sm[:, 0:1]))
                link(V.tensor_tensor(sm[:, 1:2], sm[:, 1:2], coef[:, :], ALU.mult))
                V.tensor_scalar(P[:, 0:T_ALL], P[:, 0:T_ALL], sm[:, 1:2], None, ALU.mult).then_inc(s["a_made"], 1)
                dve.wait_ge(s["aT_made"], pair + 1)
                if later(pair):
                    dve.wait_ge(s["od_made"], pair)
                V.tensor_copy(aT[:, 0:2, 0:64], B[1][:, 0:128].rearrange("p (i r) -> p i r", i=2)).then_inc(s["aT_kept"], 1)
                V.tensor_copy(aT[0:T_DEC, 2, 0:64], B[1][0:T_DEC, 128:192]).then_inc(s["aT_kept"], 1)
                dve.wait_ge(s["od_made"], pair + 1)
                V.tensor_copy(rot[:, :], B[2][:, :]).then_inc(s["rows_kept"], 1)
                dve.wait_ge(s["od_T"], pair + 1)
                for b in range(2):
                    own = (B[3][:, 0:36 * H], B[3][:, 512 - 36 * H:])[b].rearrange("p (h r) -> p h r", h=H)[:, :, (0, 32)[b]:(0, 32)[b] + DEC_SEQ]
                    V.tensor_copy(oT[:, :, bass.ds(8 * pair + (SEQ + DEC_SEQ * b), DEC_SEQ)], own).then_inc(s["od_kept"], 1)

            samples(0)
            assert st["n"] == pre + S_STEPS, st["n"]
            with dve.Fori(1, PAIRS) as pair:
                st["base"], st["n"] = pair * S_STEPS + pre, 0
                samples(pair)
                assert st["n"] == S_STEPS, st["n"]
            st["base"], st["n"] = PAIRS * S_STEPS + pre, 0
            dve.wait_ge(s["od_kept"], 2 * PAIRS)
            V.tensor_tensor(rot2[:, 0:256].rearrange("p (h r) -> p h r", h=H), oT[:, :, SEQ:], oT[:, :, SEQ:], ALU.mult).then_inc(s["od_sq"], 1)
            dve.wait_ge(s["od_root"], 1)
            link(V.reciprocal(rot[:, 0:256], rot[:, 0:256]))
            link(V.scalar_tensor_tensor(oT[:, :, SEQ:], rot[:, 0:256].rearrange("p (h r) -> p h r", h=H), subln[:, 0:1], oT[:, :, SEQ:], ALU.mult, ALU.mult))
            pre = PAIRS * S_STEPS + pre + st["n"]

            def head(h, more):
                dve.wait_ge(s["sc_made"], h + 1)
                if later(h):
                    dve.wait_ge(s["paT_made"], h)
                link(V.tensor_tensor(P[:, :].rearrange("p (c n) -> p c n", c=2), BB[:, :, 0:SCORES], m["causal"][:, :].unsqueeze(1).broadcast_to([128, 2, SCORES]), ALU.add))
                for t in range(2):
                    v = P[:, :].rearrange("p (c n) -> p c n", c=2)[:, :, 128 * t:128 * t + 128 * (t + 1)]
                    link(V.tensor_reduce(mx[:, 2 * t:2 * t + 2], v, AX.X, ALU.max))
                V.tensor_scalar(mx[:, :], mx[:, :], -(DH ** -0.5), None, ALU.mult).then_inc(s["sc_kept"], 1)
                dve.wait_ge(s["sc_exp"], 4 * h + 4)
                link(V.reciprocal(sm[:, :], sm[:, :]))
                link(V.tensor_scalar(sm[:, 1:2], sm[:, 1:2], lam[:, 2:3], None, ALU.mult))
                link(V.tensor_scalar(sm[:, 3:4], sm[:, 3:4], lam[:, 2:3], None, ALU.mult))
                for t in range(2):
                    lo, n = 128 * t, 128 * (t + 1)
                    p0, p1 = P[:, lo:lo + n], P[:, SCORES + lo:SCORES + lo + n]
                    link(V.tensor_scalar(p1, p1, sm[:, 2 * t + 1:2 * t + 2], None, ALU.mult))
                    ins = V.scalar_tensor_tensor(p0, p0, sm[:, 2 * t:2 * t + 1], p1, ALU.mult, ALU.add)
                    ins.then_inc(s["pa_made"], 1)

            st["base"], st["n"] = pre, 0
            head(0, True)
            with dve.Fori(1, H - 1) as h:
                st["base"], st["n"] = h * P_STEPS + pre, 0
                head(h, True)
                assert st["n"] == P_STEPS, st["n"]
            st["base"], st["n"] = (H - 1) * P_STEPS + pre, 0
            head(H - 1, False)
            dve.wait_ge(s["o_kept"], H)
            for t in range(2):
                for j in range(2):
                    v = o_t[:, t, 512 * j:512 * j + 512]
                    link(V.tensor_tensor(o_sq, v, v, ALU.mult))
                    ins = V.tensor_reduce(o_ss[:, t, 4 * j:4 * j + 4], o_sq.rearrange("p (h e) -> p h e", h=4), AX.X, ALU.add)
                    ins.then_inc(s["on_sq"], 1) if t and j else link(ins)
            dve.wait_ge(s["on_root"], 1)
            link(V.reciprocal(o_ss[:], o_ss[:]))
            for t in range(2):
                v = o_t[:, t, :].rearrange("p (h e) -> p h e", h=H)
                V.tensor_tensor(v, v, o_ss[:, t, :].unsqueeze(2).broadcast_to([128, H, 128]), ALU.mult).then_inc(s["on_made"], 1)
            for t in range(NT):
                r = rows[t]
                for j in range(2):
                    dve.wait_ge(s["out_made"], 2 * t + j + 1)
                    V.tensor_tensor(resid[0:r, t, 512 * j:512 * j + 512], resid[0:r, t, 512 * j:512 * j + 512], B[4 + j][0:r, :], ALU.add).then_inc(s["out_kept"], 1)
            dve.wait_ge(s["out_kept"], 2 * NT)

        @block.tensor
        def _(pe):
            T = nc.tensor
            xv = xh.rearrange("p (c k) -> p k c", k=KT)
            for t in range(NT):
                r = rows[t]
                pe.wait_ge(s["xh_made"], t + 1)
                if t:
                    pe.wait_ge(s["xT_kept"], 4 * t)
                for k in range(KT):
                    last = T.transpose(B[k // 4][:, 128 * (k % 4):128 * (k % 4) + r], xv[0:r, k, :], ident[0:r, 0:r])
                    if k % 4 == 3:
                        last.then_inc(s["xT_made"], 1)
            pe.wait_ge(s["xT_kept"], 4 * NT)
            for half in range(2):
                for j in range(3):
                    pe.wait_ge(slot_in[j], 16 * half + 16)
                    for t in range(NT):
                        if half:
                            if j == 0:
                                pe.wait_ge(s["q_rotated"] if t == 0 else s["rotated"], 3)
                            elif j == 1:
                                pe.wait_ge(s["kv_kept"], t + 1)
                            else:
                                pe.wait_ge(s["q_rotated"], 3)
                        if j == 2 and t == 2:
                            pe.wait_ge(s["rotated"], 3 * half + 1)
                        bank = (kbank, vbank, qbank)[j](t)
                        for k in range(KT):
                            last = T.matmul(bank[0:rows[t], :], XK[:, 0 if j < 2 else 1, k, at[t]], wslot[j][:, k, :], start=(k == 0), stop=(k == KT - 1))
                        last.then_inc(s["kv_made"], 1)
            pe.wait_ge(s["q_rotated"], 6)
            pe.wait_ge(s["rotated"], 6)
            pe.wait_ge(s["kv_kept"], 6)
            for j, src in ((4, q_t), (5, k_t)):
                for h in range(H):
                    last = T.transpose(B[j][:, 32 * h:32 * h + 32], src[0:T_DEC, 2, 128 * h:128 * h + 128], ident[0:T_DEC, 0:T_DEC])
            last.then_inc(s["dT_made"], 1)
            pe.wait_ge(s["dT_kept"], 3)

            def samples(pair):
                pe.wait_ge(s["K0_in"], 64 * pair + 64)
                for b in range(2):
                    for j in range(4):
                        if b == 0 and later(pair):
                            pe.wait_ge(s["KT_kept"], 8 * pair)
                        elif b and j == 0:
                            pe.wait_ge(s["KT_kept"], 8 * pair + 4)
                        for h in range(2):
                            for i in range(N_PAGES):
                                last = T.transpose(B[4 + j][:, 256 * h + 128 * i:256 * h + 128 * i + 128],
                                                   Kc[:, b, i, 128 * (2 * j + h):128 * (2 * j + h) + 128], ident[:, :])
                        last.then_inc(s["KT_made"], 1)
                pe.wait_ge(s["KT_kept"], 8 * pair + 8)
                if later(pair):
                    pe.wait_ge(s["S_kept"], pair)
                pe.wait_ge(s["QBs_made"], pair + 1)
                for h in range(H):
                    for b in range(2):
                        last = T.matmul(B[0][64 * b:64 * b + 64, 0:T_ALL], QBs[:, b, h, :], XK[:, b, h, :], start=(h == 0), stop=(h == H - 1))
                last.then_inc(s["S_made"], 1)
                pe.wait_ge(s["a_made"], pair + 1)
                T.matmul(B[1][:, 0:64], P[:, 0:128], m["halves"][:, :], start=True, stop=True)
                T.matmul(B[1][:, 64:128], P[:, 128:256], m["halves"][:, :], start=True, stop=True)
                T.matmul(B[1][0:T_DEC, 128:192], P[:, 256:T_ALL], m["halves"][:, :], start=True, stop=True).then_inc(s["aT_made"], 1)
                pe.wait_ge(s["aT_kept"], 2 * pair + 2)
                pe.wait_ge(s["V0_in"], 64 * pair + 64)
                for b in range(2):
                    for f in range(2):
                        for i in range(N_PAGES + 1):
                            for h in range(4 * f, 4 * f + 4):
                                values = Vc[:, b, i, 128 * h:128 * h + 128] if i < N_PAGES else v_t[0:T_DEC, 2, 128 * h:128 * h + 128]
                                weights = aT[:, i, 32 * b:32 * b + 32] if i < N_PAGES else aT[0:T_DEC, 2, 32 * b:32 * b + 32]
                                lane = 32 * (h % 4)
                                last = T.matmul(B[2][lane:lane + 32, 256 * b + 128 * f:256 * b + 128 * f + 128], weights, values,
                                                start=(i == 0), stop=(i == N_PAGES), tile_position=(0, lane))
                last.then_inc(s["od_made"], 1)
                pe.wait_ge(s["rows_kept"], pair + 1)
                if later(pair):
                    pe.wait_ge(s["od_kept"], 2 * pair)
                for j in range(4):
                    last = T.transpose(B[3][:, 128 * j:128 * j + 128], rot[:, 128 * j:128 * j + 128], ident[:, :])
                last.then_inc(s["od_T"], 1)

            samples(0)
            with pe.Fori(1, PAIRS) as pair:
                samples(pair)
            pe.wait_ge(s["od_sq"], 1)
            T.matmul(B[0][:, 0:256], ones[:, :], rot2[:, 0:256], start=True, stop=True).then_inc(s["od_sum"], 1)

            def turn(h):
                pe.wait_ge(s["sliced"], 2 * h + 2)
                if later(h):
                    pe.wait_ge(s["qkT_kept"], 2 * h)
                for j in range(2):
                    for t in range(2):
                        last = T.transpose(B[4][:, 256 * j + 128 * t:256 * j + 128 * t + 128], qk_h[:, j, t, :], ident[:, :])
                last.then_inc(s["qk_T"], 1)

            def head(h, more):
                pe.wait_ge(s["qkT_kept"], 2 * h + 2)
                if later(h):
                    pe.wait_ge(s["sc_kept"], h)
                for t in range(2):
                    for c in range(2):
                        lane = slice(64 * c, 64 * c + 64)
                        last = T.matmul(BB[:, c, 128 * t:128 * t + 128 * (t + 1)], qkT[lane, 0, 128 * t:128 * t + 128], qkT[lane, 1, 0:128 * (t + 1)],
                                        start=True, stop=True)
                last.then_inc(s["sc_made"], 1)
                if more:
                    turn(h + 1)
                pe.wait_ge(s["pa_made"], 2 * h + 2)
                if later(h):
                    pe.wait_ge(s["paT_kept"], h)
                for j, lo in enumerate((0, 128, 256)):
                    last = T.transpose(B[6][:, 128 * j:128 * j + 128], P[:, lo:lo + 128], ident[:, :])
                last.then_inc(s["paT_made"], 1)
                pe.wait_ge(s["paT_kept"], h + 1)
                if later(h):
                    pe.wait_ge(s["o_kept"], h)
                e = bass.ds(128 * h, 128)
                T.matmul(B[7][:, 0:128], aT[:, 0, :], v_t[:, 0, e], start=True, stop=True)
                T.matmul(B[7][:, 128:256], aT[:, 1, :], v_t[:, 0, e], start=True, stop=False)
                T.matmul(B[7][:, 128:256], aT[:, 2, :], v_t[:, 1, e], start=False, stop=True).then_inc(s["o_made"], 1)

            turn(0)
            head(0, True)
            with pe.Fori(1, H - 1) as h:
                head(h, True)
            head(H - 1, False)
            for t in range(2):
                pe.wait_ge(s["on_made"], t + 1)
                for j in range(2):
                    for h in range(4):
                        last = T.transpose(B[2 * t + j][:, 128 * h:128 * h + 128], o_t[:, t, 128 * (4 * j + h):128 * (4 * j + h) + 128], ident[:, :])
                    last.then_inc(s["onT_made"], 1)
            pe.wait_ge(s["onT_kept"], 4)
            pe.wait_ge(s["wout_in"], 16)
            for t in range(NT):
                if t:
                    pe.wait_ge(s["out_kept"], 2 * t)
                for j in range(2):
                    for h in range(H):
                        last = T.matmul(B[4 + j][0:rows[t], :], oT[:, h, at[t]], w_out[:, h, 512 * j:512 * j + 512], start=(h == 0), stop=(h == H - 1))
                    last.then_inc(s["out_made"], 1)

    nc.clear_and_free_semaphores(sems)
    nc.all_engine_barrier(sem_only=True)


def moe_phase(nc, m, layer):
    ctx, sems = ExitStack(), []
    with ctx:
        def sb(name, shape, dt=F32):
            return ctx.enter_context(nc.sbuf_tensor(f"moe{layer}_{name}", shape, dt))

        def pb(name, shape, dt=F32):
            return ctx.enter_context(nc.psum_tensor(f"moe{layer}_{name}", shape, dt))

        def sem(name):
            sems.append(nc.alloc_semaphore(f"moe{layer}_{name}"))
            return sems[-1]

        NT = TOK_TILES
        rows = TILE_ROWS
        resid, ident = m["resid"], m["ident"]
        norm_b = sb("norm_b", [128, D_MODEL])
        w_router = sb("w_router", [128, KT, N_GROUPS + N_EXPERTS])
        b_router = sb("b_router", [128, N_GROUPS + N_EXPERTS])
        xn = sb("xn", [128, NT, D_MODEL])
        xnT = sb("xnT", [128, KT, 128])
        logits = sb("logits", [128, NT, N_GROUPS + N_EXPERTS])
        sq = sb("sq", [128, D_MODEL])
        ss = sb("ss", [128, NT])
        rstd = sb("rstd", [128, NT])
        gmax = sb("gmax", [128, NT])
        gexp = sb("gexp", [128, NT, N_GROUPS])
        gsum = sb("gsum", [128, NT])
        gpick = sb("gpick", [128, NT, N_GROUPS])
        gbest = sb("gbest", [128, NT])
        masked = sb("masked", [128, NT, N_EXPERTS])
        etmp = sb("etmp", [128, NT, N_EXPERTS])
        ebest = sb("ebest", [128, NT])
        top = sb("top", [128, TOP_K, NT])
        oneh = sb("oneh", [128, TOP_K, NT, N_EXPERTS])
        both = sb("both", [128, NT, N_EXPERTS])
        gate = sb("gate", [128, TOP_K, NT])
        ratio = sb("ratio", [128, NT])
        rank = sb("rank", [128, NT, N_EXPERTS])
        counts = sb("counts", [128, N_EXPERTS])
        nover = sb("nover", [128, N_EXPERTS])
        cend = sb("cend", [128, N_EXPERTS])
        cstart = sb("cstart", [128, N_EXPERTS])
        rk = sb("rk", [128, TOP_K, NT])
        inmain = sb("inmain", [128, TOP_K, NT])
        lmain = sb("lmain", [128, TOP_K, NT])
        opos = sb("opos", [128, TOP_K, NT])
        oge = sb("oge", [128, TOP_K, NT, OVER_GROUPS + 1])
        olow = sb("olow", [128, TOP_K, NT])
        lpos = sb("lpos", [128, TOP_K, NT])
        colhot = sb("colhot", [128, TOP_K, NT, N_COLS])
        entry = sb("entry", [128, TOP_K, NT, 2, N_COLS])
        place = sb("place", [128, TOP_K, NT, 128])
        tabf = sb("tabf", [128, 2, N_COLS])
        tabz = sb("tabz", [128, 2, N_COLS])
        table = sb("table", [128, 2, N_COLS], U32)
        obf = sb("obf", [1, 2 * OVER_GROUPS, N_EXPERTS])
        obf2 = sb("obf2", [1, 2 * OVER_GROUPS, N_EXPERTS])
        ovalf = sb("ovalf", [1, 2 * OVER_GROUPS + 2])
        ngf = sb("ngf", [1, 4])
        steer = sb("steer", [1, 2 * OVER_GROUPS + 2], I32)
        xg = sb("xg", [128, D_MODEL])
        xgT = sb("xgT", [128, KT, 128])
        silu = sb("silu", [128, D_FF_EXPERT])
        hid = sb("hid", [128, D_FF_EXPERT])
        hidT = sb("hidT", [128, FT, 128])
        y_sb = sb("y_sb", [128, D_MODEL])
        rows_in = sb("rows_in", [128, 1], U32)
        rows_out = sb("rows_out", [128, 1], U32)

        ps_x = pb("ps_x", [128, 2, 4, 128])
        ps_gate = pb("ps_gate", [128, D_FF_EXPERT])
        ps_up = pb("ps_up", [128, D_FF_EXPERT])
        ps_hid = pb("ps_hid", [128, FT, 128])
        ps_y = pb("ps_y", [128, 2, 512])
        ps_rank = ps_gate[:, 0:NT * N_EXPERTS].rearrange("p (a e) -> p a e", a=NT)
        ps_count = ps_gate[:, NT * N_EXPERTS:NT * N_EXPERTS + N_EXPERTS]
        ps_tab = ps_up[:, 0:2 * N_COLS]
        ps_log = ps_hid[:, 0, 0:N_GROUPS + N_EXPERTS]

        consts_in = sem("consts_in")
        squares = sem("squares")
        roots = sem("roots")
        normed = sem("normed")
        xn_stored = sem("xn_stored")
        xT_made = sem("xT_made")
        xT_kept = sem("xT_kept")
        logits_made = sem("logits_made")
        logits_kept = sem("logits_kept")
        gdiff = sem("gdiff")
        gexped = sem("gexped")
        tdiff = sem("tdiff")
        texped = sem("texped")
        hots = sem("hots")
        ranked = sem("ranked")
        placed = sem("placed")
        tabbed = sem("tabbed")
        table_ready = sem("table_ready")
        vchain = sem("vchain")
        cleared = sem("cleared")
        weights_in = m["weights_of"][layer]
        weights_used = [sem(f"{n}_products") for n in ("gate", "up", "down")]
        gate_made, up_made, y_made = weights_used
        gathered = sem("gathered")
        gx_T = sem("gx_T")
        gx_kept = sem("gx_kept")
        silued = sem("silued")
        hidden = sem("hidden")
        hid_T = sem("hid_T")
        hid_kept = sem("hid_kept")
        y_kept = sem("y_kept")
        scattered = sem("scattered")
        y_back = sem("y_back")
        scattered_all = sem("scattered_all")
        mean_made = sem("mean_made")
        ss_cleared = sem("ss_cleared")
        waits_held = sem("waits_held")
        in_copied = sem("in_copied")
        out_copied = sem("out_copied")
        xn_dram, y_dram = m["xn_dram"], m["y_dram"][layer]
        y_rows = y_dram.rearrange("(t k) d -> t k d", k=TOP_K)
        ring = m["ring"]
        W = m["expert_views"][layer]

        block = ctx.enter_context(nc.Block())

        @block.sync
        def _(sp):
            sp.dma_start(norm_b[:], m["norm_m"][layer:layer + 1, :].broadcast_to([128, D_MODEL])).then_inc(consts_in, 16)
            sp.dma_start(w_router[:, :, 0:N_GROUPS], m["w_rg"][layer].rearrange("(p t) n -> p t n", t=KT)).then_inc(consts_in, 16)
            sp.dma_start(w_router[:, :, N_GROUPS:], m["w_re"][layer].rearrange("(p t) n -> p t n", t=KT)).then_inc(consts_in, 16)
            sp.dma_start(b_router[:, 0:N_GROUPS], m["b_rg"][layer:layer + 1, :].broadcast_to([128, N_GROUPS])).then_inc(consts_in, 16)
            sp.dma_start(b_router[:, N_GROUPS:], m["b_re"][layer:layer + 1, :].broadcast_to([128, N_EXPERTS])).then_inc(consts_in, 16)
            sp.wait_ge(normed, NT)
            for t in range(NT):
                sp.dma_start(xn_dram[128 * t:128 * t + rows[t], :], xn[0:rows[t], t, :]).then_inc(xn_stored, 16)
            with sp.Fori(1, MAIN_GROUPS) as g:
                for n in range(3):
                    sp.wait_ge(weights_used[n], g)
                    for e in range(2):
                        sp.dma_start(ring[n][:, e:e + 1, :], W[n][:, bass.ds(2 * g + e, 1), :]).then_inc(weights_in[n][e], 16)
            sp.wait_ge(table_ready, 1)
            groups = sp.value_load(steer[0:1, 0:1], min_val=MAIN_GROUPS, max_val=MAIN_GROUPS + OVER_GROUPS)
            with sp.If(groups > MAIN_GROUPS):
                with sp.Fori(MAIN_GROUPS, groups) as g:
                    for e in range(2):
                        expert = sp.value_load(steer[0:1, bass.ds(2 * (g - MAIN_GROUPS) + 1 + e, 1)], min_val=0, max_val=N_EXPERTS - 1)
                        for n in range(3):
                            sp.wait_ge(weights_used[n], g)
                            sp.dma_start(ring[n][:, e:e + 1, :], W[n][:, bass.ds(expert, 1), :]).then_inc(weights_in[n][e], 16)
            sp.wait_ge(scattered_all, 1)
            for t in range(NT):
                sp.dma_start(ring[0][0:rows[t], :, :].rearrange("p a n -> p (a n)")[:, 2048 * t:2048 * t + 2048].rearrange("p (k d) -> p k d", k=2),
                             y_rows[128 * t:128 * t + rows[t], :, :]).then_inc(y_back, 16)
            sp.wait_ge(y_back, 16 * NT)


        @block.gpsimd
        def _(pool):
            nc.gpsimd.memset(xg[:], 0.0).then_inc(cleared, 1)
            pool.wait_ge(cleared, 1)
            pool.wait_ge(xn_stored, 16 * NT)
            pool.wait_ge(table_ready, 1)
            last_group = pool.value_load(steer[0:1, 2 * OVER_GROUPS + 1:2 * OVER_GROUPS + 2], min_val=MAIN_GROUPS - 1, max_val=N_COLS - 1)

            def gather(g):
                if not (isinstance(g, int) and g == 0):
                    pool.wait_ge(gathered, 16 * g)
                nc.gpsimd.tensor_copy(rows_in[:, :], table[:, 0, bass.ds(g, 1)]).then_inc(in_copied, 1)
                pool.wait_ge(in_copied, g + 1)
                if not (isinstance(g, int) and g == 0):
                    pool.wait_ge(gx_T, g)
                pool.sem_inc(waits_held, 1)
                pool.indirect_dma_start(xg[:, :], None, xn_dram[:, :], bass.IndirectOffsetOnAxis(rows_in[:, :], 0),
                                        bounds_check=T_ALL - 1, oob_is_err=False).then_inc(gathered, 16)

            def scatter(g, first=False):
                if not first:
                    pool.wait_ge(scattered, 16 * g)
                nc.gpsimd.tensor_copy(rows_out[:, :], table[:, 1, bass.ds(g, 1)]).then_inc(out_copied, 1)
                pool.wait_ge(out_copied, g + 1)
                pool.wait_ge(y_kept, 2 * g + 2)
                pool.sem_inc(waits_held, 1)
                pool.indirect_dma_start(y_dram[:, :], bass.IndirectOffsetOnAxis(rows_out[:, :], 0), y_sb[:, :], None,
                                        bounds_check=TOP_K * T_ALL - 1, oob_is_err=False).then_inc(scattered, 16)

            gather(0)
            with pool.Fori(0, last_group) as g:
                gather(g + 1)
                scatter(g)
            scatter(last_group)
            pool.wait_ge(scattered, 16 * last_group + 16)
            pool.sem_inc(scattered_all, 1)

        @block.scalar
        def _(act):
            act.wait_ge(ss_cleared, 1)
            for t in range(NT):
                r = rows[t]
                nc.scalar.activation(sq[0:r, :], resid[0:r, t, :], ACT.Square, accum_out=ss[0:r, t:t + 1]).then_inc(squares, 1)
                act.wait_ge(squares, t + 1)
            act.wait_ge(mean_made, 1)
            nc.scalar.activation(rstd[:, :], ss[:, :], ACT.Sqrt).then_inc(roots, 1)
            for t in range(NT):
                act.wait_ge(xT_made, 2 * t + 2)
                nc.scalar.copy(xnT[:, 4:8, :], ps_x[:, 1]).then_inc(xT_kept, 1)
            act.wait_ge(gdiff, 1)
            nc.scalar.activation(gexp[:], gexp[:], ACT.Exp).then_inc(gexped, 1)
            act.wait_ge(tdiff, 1)
            nc.scalar.activation(ratio[:], ratio[:], ACT.Exp).then_inc(texped, 1)
            act.wait_ge(table_ready, 1)
            groups = act.value_load(steer[0:1, 0:1], min_val=MAIN_GROUPS, max_val=MAIN_GROUPS + OVER_GROUPS)
            with act.Fori(0, groups) as g:
                act.wait_ge(gx_T, g + 1)
                act.wait_ge(up_made, g)
                nc.scalar.copy(xgT[:, 4:8, :], ps_x[:, 1]).then_inc(gx_kept, 1)
                act.wait_ge(gate_made, g + 1)
                act.wait_ge(hidden, g)
                nc.scalar.activation(silu[:], ps_gate[:], ACT.Silu).then_inc(silued, 1)
                act.wait_ge(y_made, g + 1)
                act.wait_ge(scattered, 16 * g)
                nc.scalar.copy(y_sb[:, 512:1024], ps_y[:, 1]).then_inc(y_kept, 1)


        @block.vector
        def _(dve):
            n = [0]

            def link(ins):
                n[0] += 1
                ins.then_inc(vchain, 1)
                dve.wait_ge(vchain, n[0])

            V = nc.vector
            link(V.memset(logits[:], 0.0))
            V.memset(ss[:], 1.0).then_inc(ss_cleared, 1)
            dve.wait_ge(squares, NT)
            V.tensor_scalar(ss[:, :], ss[:, :], 1.0 / D_MODEL, EPS, ALU.mult, ALU.add).then_inc(mean_made, 1)
            dve.wait_ge(roots, 1)
            link(V.reciprocal(rstd[:, :], rstd[:, :]))
            dve.wait_ge(consts_in, 16 * 5)
            for t in range(NT):
                r = rows[t]
                V.scalar_tensor_tensor(xn[0:r, t, :], resid[0:r, t, :], rstd[0:r, t:t + 1], norm_b[0:r, :], ALU.mult, ALU.mult).then_inc(normed, 1)
            for t in range(NT):
                r = rows[t]
                dve.wait_ge(xT_made, 2 * t + 1)
                if t:
                    dve.wait_ge(logits_made, t)
                V.tensor_copy(xnT[:, 0:4, :], ps_x[:, 0]).then_inc(xT_kept, 1)
                dve.wait_ge(logits_made, t + 1)
                V.tensor_tensor(logits[0:r, t, :], ps_log[0:r, :], b_router[0:r, :], ALU.add).then_inc(logits_kept, 1)
            dve.wait_ge(logits_kept, NT)
            lg, le = logits[:, :, 0:N_GROUPS], logits[:, :, N_GROUPS:]

            def bc(a, k):
                return a.unsqueeze(2).broadcast_to([128, NT, k])

            link(V.tensor_reduce(gmax[:], lg, AX.X, ALU.max))
            V.tensor_tensor(gexp[:], lg, bc(gmax[:], N_GROUPS), ALU.subtract).then_inc(gdiff, 1)
            link(V.tensor_tensor(gpick[:], lg, bc(gmax[:], N_GROUPS), ALU.is_equal))
            link(V.tensor_tensor(gpick[:], gpick[:], m["falling"][:, 0:N_GROUPS].unsqueeze(1).broadcast_to([128, NT, N_GROUPS]), ALU.mult))
            link(V.tensor_reduce(gbest[:], gpick[:], AX.X, ALU.max))
            link(V.tensor_tensor(gpick[:], gpick[:], bc(gbest[:], N_GROUPS), ALU.is_equal))
            link(V.tensor_scalar(gpick[:], gpick[:], 1.0, FAR, ALU.subtract, ALU.mult))
            for t in range(NT):
                link(V.tensor_tensor(masked[:, t, :].rearrange("p (g e) -> p g e", g=N_GROUPS),
                                     le[:, t, :].rearrange("p (g e) -> p g e", g=N_GROUPS),
                                     gpick[:, t, :].unsqueeze(2).broadcast_to([128, N_GROUPS, EXP_PER_GROUP]), ALU.add))
            for k in range(TOP_K):
                link(V.tensor_reduce(top[:, k, :], masked[:], AX.X, ALU.max))
                link(V.tensor_tensor(etmp[:], masked[:], bc(top[:, k, :], N_EXPERTS), ALU.is_equal))
                link(V.tensor_tensor(etmp[:], etmp[:], m["falling"][:, 0:N_EXPERTS].unsqueeze(1).broadcast_to([128, NT, N_EXPERTS]), ALU.mult))
                link(V.tensor_reduce(ebest[:], etmp[:], AX.X, ALU.max))
                link(V.tensor_tensor(oneh[:, k], etmp[:], bc(ebest[:], N_EXPERTS), ALU.is_equal))
                if k == 0:
                    link(V.scalar_tensor_tensor(masked[:], oneh[:, k], -3.0 * FAR, masked[:], ALU.mult, ALU.add))
            V.tensor_tensor(ratio[:], top[:, 1, :], top[:, 0, :], ALU.subtract).then_inc(tdiff, 1)
            for k in range(TOP_K):
                link(V.tensor_tensor(oneh[:, k], oneh[:, k], bc(m["valid"][:, :], N_EXPERTS), ALU.mult))
            V.tensor_tensor(both[:], oneh[:, 0], oneh[:, 1], ALU.add).then_inc(hots, 1)
            dve.wait_ge(gexped, 1)
            link(V.tensor_reduce(gsum[:], gexp[:], AX.X, ALU.add))
            link(V.reciprocal(gsum[:], gsum[:]))
            dve.wait_ge(texped, 1)
            link(V.tensor_scalar(ebest[:], ratio[:], 1.0, None, ALU.add))
            link(V.reciprocal(ebest[:], ebest[:]))
            link(V.tensor_tensor(gate[:, 0, :], gsum[:], ebest[:], ALU.mult))
            link(V.tensor_tensor(gate[:, 1, :], gate[:, 0, :], ratio[:], ALU.mult))
            dve.wait_ge(ranked, 1)
            link(V.tensor_copy(rank[:], ps_rank))
            link(V.tensor_copy(counts[:], ps_count))
            link(V.tensor_scalar(nover[:], counts[:], float(SLOTS), None, ALU.is_gt))
            for j in range(2, OVER_LEVELS + 1):
                link(V.scalar_tensor_tensor(nover[:], counts[:], float(SLOTS * j), nover[:], ALU.is_gt, ALU.add))
            link(V.tensor_tensor_scan(cend[:], nover[:], nover[:], 0.0, ALU.add, ALU.bypass))
            link(V.tensor_tensor(cstart[:], cend[:], nover[:], ALU.subtract))
            for k in range(TOP_K):
                link(V.tensor_tensor(etmp[:], oneh[:, k], rank[:], ALU.mult))
                link(V.tensor_reduce(rk[:, k, :], etmp[:], AX.X, ALU.add))
                link(V.tensor_tensor(etmp[:], oneh[:, k], m["odd_slots"][:, :].unsqueeze(1).broadcast_to([128, NT, N_EXPERTS]), ALU.mult))
                link(V.tensor_reduce(lmain[:, k, :], etmp[:], AX.X, ALU.add))
                link(V.tensor_tensor(etmp[:], oneh[:, k], cstart[:, :].unsqueeze(1).broadcast_to([128, NT, N_EXPERTS]), ALU.mult))
                link(V.tensor_reduce(opos[:, k, :], etmp[:], AX.X, ALU.add))
            link(V.tensor_tensor(lmain[:], lmain[:], rk[:], ALU.add))
            link(V.tensor_scalar(opos[:], opos[:], float(SLOTS), -float(SLOTS), ALU.mult, ALU.add))
            link(V.tensor_tensor(opos[:], opos[:], rk[:], ALU.add))
            link(V.tensor_scalar(inmain[:], rk[:], float(SLOTS), None, ALU.is_lt))
            for j in range(OVER_GROUPS + 1):
                link(V.tensor_scalar(oge[:, :, :, j], opos[:], 128.0 * j, None, ALU.is_ge))
            link(V.tensor_reduce(olow[:], oge[:, :, :, 1:OVER_GROUPS], AX.X, ALU.add))
            link(V.scalar_tensor_tensor(olow[:], olow[:], -128.0, opos[:], ALU.mult, ALU.add))
            link(V.tensor_tensor(lmain[:], lmain[:], olow[:], ALU.subtract))
            link(V.tensor_tensor(lmain[:], lmain[:], inmain[:], ALU.mult))
            link(V.tensor_tensor(lpos[:], lmain[:], olow[:], ALU.add))
            for k in range(TOP_K):
                for t in range(NT):
                    link(V.tensor_scalar(place[:, k, t, :], m["lanes"][:, :], lpos[:, k, t:t + 1], None, ALU.is_equal))
                link(V.tensor_reduce(colhot[:, k, :, 0:MAIN_GROUPS], oneh[:, k].rearrange("p a (g e) -> p a g e", e=2), AX.X, ALU.add))
                link(V.tensor_tensor(colhot[:, k, :, 0:MAIN_GROUPS], colhot[:, k, :, 0:MAIN_GROUPS], bc(inmain[:, k, :], MAIN_GROUPS), ALU.mult))
                link(V.tensor_tensor(colhot[:, k, :, MAIN_GROUPS:], oge[:, k, :, 0:OVER_GROUPS], oge[:, k, :, 1:OVER_GROUPS + 1], ALU.subtract))
                link(V.tensor_scalar(inmain[:, k, :], inmain[:, k, :], -1.0, 1.0, ALU.mult, ALU.add))
                link(V.tensor_tensor(inmain[:, k, :], inmain[:, k, :], m["valid"][:, :], ALU.mult))
                link(V.tensor_tensor(colhot[:, k, :, MAIN_GROUPS:], colhot[:, k, :, MAIN_GROUPS:], bc(inmain[:, k, :], OVER_GROUPS), ALU.mult))
                for j in range(2):
                    link(V.tensor_tensor(entry[:, k, :, j, :], colhot[:, k], bc(m["token_no"][:, k, j, :], N_COLS), ALU.mult))
            V.tensor_copy(etmp[:, 0, 0:1], m["lanes"][:, 0:1]).then_inc(placed, 1)
            link(V.tensor_reduce(ngf[:, 0:1], nover[0:1, :], AX.X, ALU.add))
            link(V.memset(ovalf[:], float(MAIN_GROUPS)))
            for j in range(OVER_GROUPS):
                link(V.scalar_tensor_tensor(ovalf[:, 0:1], ngf[:, 0:1], 2.0 * j, ovalf[:, 0:1], ALU.is_gt, ALU.add))
            for b in range(2 * OVER_GROUPS):
                link(V.tensor_scalar(obf[:, b, :], cend[0:1, :], float(b), None, ALU.is_le))
            link(V.tensor_reduce(ovalf[:, 1:2 * OVER_GROUPS + 1], obf[:], AX.X, ALU.add))
            link(V.tensor_scalar(ovalf[:, 1:2 * OVER_GROUPS + 1], ovalf[:, 1:2 * OVER_GROUPS + 1], float(N_EXPERTS - 1), None, ALU.min))
            link(V.tensor_scalar(ovalf[:, 2 * OVER_GROUPS + 1:], ovalf[:, 0:1], -1.0, None, ALU.add))
            link(V.tensor_copy(steer[:], ovalf[:]))
            dve.wait_ge(tabbed, 1)
            tf = tabf[:].rearrange("p a c -> p (a c)")
            tz = tabz[:].rearrange("p a c -> p (a c)")
            link(V.tensor_copy(tf, ps_tab))
            link(V.tensor_scalar(tz, tf, 0.0, NOWHERE, ALU.is_equal, ALU.mult))
            link(V.scalar_tensor_tensor(tf, tf, -1.0, tz, ALU.add, ALU.add))
            V.tensor_copy(table[:].rearrange("p a c -> p (a c)"), tf).then_inc(table_ready, 1)
            dve.wait_ge(table_ready, 1)
            groups = dve.value_load(steer[0:1, 0:1], min_val=MAIN_GROUPS, max_val=MAIN_GROUPS + OVER_GROUPS)
            with dve.Fori(0, groups) as g:
                dve.wait_ge(gx_T, g + 1)
                dve.wait_ge(up_made, g)
                V.tensor_copy(xgT[:, 0:4, :], ps_x[:, 0]).then_inc(gx_kept, 1)
                dve.wait_ge(up_made, g + 1)
                dve.wait_ge(silued, g + 1)
                dve.wait_ge(hid_T, g)
                V.tensor_tensor(hid[:], silu[:], ps_up[:], ALU.mult).then_inc(hidden, 1)
                dve.wait_ge(hid_T, g + 1)
                dve.wait_ge(y_made, g)
                V.tensor_copy(hidT[:], ps_hid[:]).then_inc(hid_kept, 1)
                dve.wait_ge(y_made, g + 1)
                dve.wait_ge(scattered, 16 * g)
                V.tensor_copy(y_sb[:, 0:512], ps_y[:, 0]).then_inc(y_kept, 1)
            dve.wait_ge(y_back, 16 * NT)
            back = ring[0][:].rearrange("p a n -> p (a n)")
            for k in range(TOP_K):
                for t in range(NT):
                    r = rows[t]
                    link(V.scalar_tensor_tensor(resid[0:r, t, :], back[0:r, 2048 * t + 1024 * k:2048 * t + 1024 * k + 1024], gate[0:r, k, t:t + 1],
                                                resid[0:r, t, :], ALU.mult, ALU.add))

        @block.tensor
        def _(pe):
            T = nc.tensor
            for t in range(NT):
                r = rows[t]
                pe.wait_ge(normed, t + 1)
                if t:
                    pe.wait_ge(xT_kept, 2 * t)
                xv = xn[0:r, t, :].rearrange("p (c k) -> p k c", k=KT)
                for k in range(KT):
                    last = T.transpose(ps_x[:, k // 4, k % 4, 0:r], xv[:, k, :], ident[0:r, 0:r])
                    if k % 4 == 3:
                        last.then_inc(xT_made, 1)
                pe.wait_ge(xT_kept, 2 * t + 2)
                if t:
                    pe.wait_ge(logits_kept, t)
                for k in range(KT):
                    last = T.matmul(ps_log[0:r, :], xnT[:, k, 0:r], w_router[:, k, :], start=(k == 0), stop=(k == KT - 1))
                last.then_inc(logits_made, 1)
            pe.wait_ge(hots, 1)
            for t in range(NT):
                for s in range(t):
                    T.matmul(ps_rank[:, t, :], m["ones"][:, :], both[:, s, :], start=(s == 0), stop=False)
                T.matmul(ps_rank[:, t, :], m["before"][:, :], both[:, t, :], start=(t == 0), stop=True)
            for s in range(NT):
                last = T.matmul(ps_count, m["ones"][:, :], both[:, s, :], start=(s == 0), stop=(s == NT - 1))
            last.then_inc(ranked, 1)
            pe.wait_ge(placed, 1)
            for k in range(TOP_K):
                for t in range(NT):
                    last = T.matmul(ps_tab, place[:, k, t, :], entry[:, k, t].rearrange("p a c -> p (a c)"),
                                    start=(k == 0 and t == 0), stop=(k == TOP_K - 1 and t == NT - 1))
            last.then_inc(tabbed, 1)
            pe.wait_ge(table_ready, 1)
            groups = pe.value_load(steer[0:1, 0:1], min_val=MAIN_GROUPS, max_val=MAIN_GROUPS + OVER_GROUPS)
            xgv = xg[:, :].rearrange("p (c k) -> p k c", k=KT)
            hidv = hid[:, :].rearrange("p (c k) -> p k c", k=FT)
            with pe.Fori(0, groups) as g:
                pe.wait_ge(gathered, 16 * g + 16)
                pe.wait_ge(gx_kept, 2 * g)
                for k in range(KT):
                    last = T.transpose(ps_x[:, k // 4, k % 4, :], xgv[:, k, :], ident[:, :])
                last.then_inc(gx_T, 1)
                pe.wait_ge(gx_kept, 2 * g + 2)
                pe.wait_ge(silued, g)
                for n, ps in ((0, ps_gate), (1, ps_up)):
                    if n == 1:
                        pe.wait_ge(hidden, g)
                    for e in range(2):
                        pe.wait_ge(weights_in[n][e], 16 * g + 16)
                    for k in range(KT):
                        for e in range(2):
                            last = T.matmul(ps[64 * e:64 * e + 64, :], xgT[:, k, 64 * e:64 * e + 64],
                                            ring[n][:, e, 512 * k:512 * k + 512], start=(k == 0), stop=(k == KT - 1))
                    last.then_inc(weights_used[n], 1)
                pe.wait_ge(hidden, g + 1)
                pe.wait_ge(hid_kept, g)
                for k in range(FT):
                    last = T.transpose(ps_hid[:, k, :], hidv[:, k, :], ident[:, :])
                last.then_inc(hid_T, 1)
                pe.wait_ge(hid_kept, g + 1)
                pe.wait_ge(y_kept, 2 * g)
                for e in range(2):
                    pe.wait_ge(weights_in[2][e], 16 * g + 16)
                for h in range(2):
                    for k in range(FT):
                        for e in range(2):
                            last = T.matmul(ps_y[64 * e:64 * e + 64, h, :], hidT[:, k, 64 * e:64 * e + 64],
                                            ring[2][:, e, 1024 * k + 512 * h:1024 * k + 512 * h + 512], start=(k == 0), stop=(k == FT - 1))
                last.then_inc(weights_used[2], 1)

    nc.clear_and_free_semaphores(sems)
    nc.all_engine_barrier(sem_only=True)


def final_phase(nc, m):
    ctx, sems = ExitStack(), []
    with ctx:
        def sem(name):
            sems.append(nc.alloc_semaphore(f"fin_{name}"))
            return sems[-1]

        NT, rows = TOK_TILES, TILE_ROWS
        norm_b = ctx.enter_context(nc.sbuf_tensor("fin_norm", [128, D_MODEL], F32))
        sq = ctx.enter_context(nc.sbuf_tensor("fin_sq", [128, D_MODEL], F32))
        ss = ctx.enter_context(nc.sbuf_tensor("fin_ss", [128, NT], F32))
        cleared, squares, mean_made, roots, inverse, norm_in, normed, stored = (sem(n) for n in (
            "cleared", "squares", "mean_made", "roots", "inverse", "norm_in", "normed", "stored"))
        block = ctx.enter_context(nc.Block())

        @block.sync
        def _(sp):
            sp.dma_start(norm_b[:], m["final_norm"].rearrange("(a d) -> a d", a=1).broadcast_to([128, D_MODEL])).then_inc(norm_in, 16)
            for t in range(NT):
                sp.wait_ge(normed, t + 1)
                dst = m["y_prompt"][0, 128 * t:128 * t + 128, :] if t < 2 else m["y_sample"].rearrange("b l d -> (b l) d")
                sp.dma_start(dst, m["resid"][0:rows[t], t, :]).then_inc(stored, 16)
            sp.wait_ge(stored, 16 * NT)

        @block.scalar
        def _(act):
            act.wait_ge(cleared, 1)
            for t in range(NT):
                r = rows[t]
                nc.scalar.activation(sq[0:r, :], m["resid"][0:r, t, :], ACT.Square, accum_out=ss[0:r, t:t + 1]).then_inc(squares, 1)
                act.wait_ge(squares, t + 1)
            act.wait_ge(mean_made, 1)
            nc.scalar.activation(ss[:, :], ss[:, :], ACT.Sqrt).then_inc(roots, 1)

        @block.vector
        def _(dve):
            nc.vector.memset(ss[:], 1.0).then_inc(cleared, 1)
            dve.wait_ge(squares, NT)
            nc.vector.tensor_scalar(ss[:, :], ss[:, :], 1.0 / D_MODEL, EPS, ALU.mult, ALU.add).then_inc(mean_made, 1)
            dve.wait_ge(roots, 1)
            nc.vector.reciprocal(ss[:, :], ss[:, :]).then_inc(inverse, 1)
            dve.wait_ge(inverse, 1)
            dve.wait_ge(norm_in, 16)
            for t in range(NT):
                r = rows[t]
                nc.vector.scalar_tensor_tensor(m["resid"][0:r, t, :], m["resid"][0:r, t, :], ss[0:r, t:t + 1], norm_b[0:r, :],
                                               ALU.mult, ALU.mult).then_inc(normed, 1)

    nc.clear_and_free_semaphores(sems)
    nc.all_engine_barrier(sem_only=True)

def decoder_step(nc, m, shapes):
    m["xn_dram"] = nc.dram_tensor("xn_rows", (T_ALL, D_MODEL), F32, kind="Internal").ap()
    m["y_dram"] = [nc.dram_tensor(f"expert_rows{i}", (TOP_K * T_ALL, D_MODEL), F32, kind="Internal").ap() for i in range(LAYERS)]
    with ExitStack() as ctx:
        def sb(name, shape):
            return ctx.enter_context(nc.sbuf_tensor(name, shape, F32))

        m["resid"] = sb("resid", [128, TOK_TILES, D_MODEL])
        m["consts"] = sb("consts", [128, sum(shapes.values())])
        start = 0
        for name, width in shapes.items():
            m[name] = m["consts"][:, start:start + width]
            start += width
        m["token_no"] = m["token_no"].rearrange("p (k j t) -> p k j t", k=TOP_K, j=2)
        m["levels"] = m["levels"].rearrange("p (n i) -> p n i", n=LEVELS)
        m["cos"] = m["cos"].rearrange("p (t d) -> p t d", t=TOK_TILES)
        m["sin"] = m["sin"].rearrange("p (t d) -> p t d", t=TOK_TILES)
        m["new_keys"] = m["new_keys"].rearrange("p (a k) -> p a k", k=T_DEC)
        m["ring"] = [sb(f"ring_{n}", [128, 2, KT * D_FF_EXPERT]) for n in ("gate", "up", "down")]
        m["expert_views"] = [[w[i].rearrange("e (p t) n -> p e (t n)", p=128) for w in (m["w_gate_e"], m["w_up_e"], m["w_down_e"])] for i in range(LAYERS)]
        m["weights_of"] = [[[ctx.enter_context(nc.semaphore(f"{n}{e}_in_{i}")) for e in range(2)] for n in ("gate", "up", "down")] for i in range(LAYERS)]

        def prefetch(eng, layer, kinds):
            for n in kinds:
                for e in range(2):
                    eng.dma_start(m["ring"][n][:, e:e + 1, :], m["expert_views"][layer][n][:, e:e + 1, :]).then_inc(m["weights_of"][layer][n][e], 16)

        m["prefetch"] = prefetch
        gdn_phase(nc, m)
        moe_phase(nc, m, 0)
        attn_phase(nc, m)
        moe_phase(nc, m, 1)
        final_phase(nc, m)


_OUTS = [("y_prompt", (1, SEQ, D_MODEL)), ("y_sample", (DEC_BATCH, DEC_SEQ, D_MODEL)),
         ("sd_prompt", (1, 1, HEADS, DK, DK)), ("sc_prompt", (1, 1, CONV_W - 1, CONV_CH)),
         ("k_prompt", (1, SEQ, HEADS, 2 * DH)), ("v_prompt", (1, SEQ, HEADS, 2 * DH)),
         ("sd_sample", (1, DEC_BATCH, HEADS, DK, DK)), ("sc_sample", (1, DEC_BATCH, CONV_W - 1, CONV_CH)),
         ("k_sample", (DEC_BATCH, DEC_SEQ, HEADS, 2 * DH)), ("v_sample", (DEC_BATCH, DEC_SEQ, HEADS, 2 * DH))]


def kernel(**inputs):
    import concourse.bacc as _bacc
    from concourse.bass_utils import run_bass_kernel_spmd as _run

    nc = _bacc.Bacc("TRN2", target_bir_lowering=False, num_devices=1)
    tables = shape_constants()
    arrays, aps = {}, {}

    def give(name, a):
        arrays[f"in_{name}_dram"] = a
        aps[name] = nc.dram_tensor(f"in_{name}_dram", a.shape, mybir.dt.from_np(a.dtype), kind="ExternalInput").ap()

    for name, a in inputs.items():
        give(name, np.ascontiguousarray(a))
    give("consts_dram", np.ascontiguousarray(np.concatenate(list(tables.values()), 1)))
    for name, shape in _OUTS:
        aps[name] = nc.dram_tensor(f"out_{name}_dram", shape, F32, kind="ExternalOutput").ap()
    decoder_step(nc, aps, {n: a.shape[1] for n, a in tables.items()})
    r = _run(nc, [arrays], core_ids=[0])
    return tuple(r.results[0][f"out_{name}_dram"] for name, _ in _OUTS)
```

```python
import math
from contextlib import ExitStack

import numpy as np

import concourse.bass as bass
from concourse import mybir

F32 = mybir.dt.float32
U32 = mybir.dt.uint32
I32 = mybir.dt.int32
ACT = mybir.ActivationFunctionType
ALU = mybir.AluOpType
AX = mybir.AxisListType

D_MODEL = 1024
SEQ = 256
DEC_BATCH = 8
DEC_SEQ = 4
PAST_LEN = 256
PAGE_SIZE = 128
N_PAGES = PAST_LEN // PAGE_SIZE
N_PHYS = DEC_BATCH * N_PAGES + max(1, DEC_BATCH * N_PAGES // 4)
HEADS = 8
DK = 128
CONV_CH = 3 * D_MODEL
GDN_IN = CONV_CH + D_MODEL + 2 * HEADS
CONV_W = 4
DH = 64
N_GROUPS = 4
EXP_PER_GROUP = 8
N_EXPERTS = 32
D_FF_EXPERT = 512
TOP_K = 2
EPS = 1e-6
LAYERS = 2

T_DEC = DEC_BATCH * DEC_SEQ
T_ALL = SEQ + T_DEC
TILE_ROWS = [128, 128, T_DEC]
TOK_TILES = len(TILE_ROWS)
KT = D_MODEL // 128
FT = D_FF_EXPERT // 128

SLOTS = 64
MAIN_GROUPS = N_EXPERTS // 2
OVER_LEVELS = -(-T_ALL // SLOTS) - 1
OVER_GROUPS = -(-((TOP_K * T_ALL) // SLOTS - 1) // 2)
N_COLS = MAIN_GROUPS + OVER_GROUPS
FAR = 1e30
NOWHERE = 16384.0


def shape_constants():
    p = np.arange(128)
    c = {}
    c["ident"] = np.eye(128)
    c["ones"] = np.ones((128, 128))
    c["before"] = (p[:, None] < p[None, :])
    c["block_starts"] = np.tile(128.0 * np.arange(OVER_GROUPS + 1), (128, 1))
    c["block_no"] = np.tile(np.arange(2 * OVER_GROUPS), (128, 1))
    c["lanes"] = np.tile(p, (128, 1))
    c["eps"] = np.full((128, 1), EPS)
    c["falling"] = np.tile(N_EXPERTS - np.arange(N_EXPERTS), (128, 1))
    c["odd_slots"] = np.tile(64 * (np.arange(N_EXPERTS) % 2), (128, 1))
    tok = p[:, None] + 128 * np.arange(TOK_TILES)[None, :]
    c["valid"] = tok < T_ALL
    c["token_no"] = np.stack([np.stack([tok + 1, TOP_K * tok + k + 1], 1) for k in range(TOP_K)], 1)
    c.update(mixer_constants())
    return {n: np.ascontiguousarray(a, np.float32).reshape(128, -1) for n, a in c.items()}


def mixer_constants():
    return {**gdn_constants(), **attn_constants()}


CW_COLS = SEQ + CONV_W - 1 + DEC_BATCH * (DEC_SEQ + CONV_W - 1)
DEC0 = SEQ + CONV_W - 1
DEC_STRIDE = DEC_SEQ + CONV_W - 1
ACC_COLS = CW_COLS - (CONV_W - 1)
CHUNK = 128
LEVELS = 7
V_STEPS = 12


def gdn_constants():
    c = {}
    p = np.arange(128)
    same = (p[:, None] // DEC_SEQ) == (p[None, :] // DEC_SEQ)
    upto = p[:, None] <= p[None, :]
    dec = np.zeros((128, T_DEC))
    dec[:T_DEC] = (same & upto)[:T_DEC, :T_DEC]
    c["upto"] = np.concatenate([upto, upto, dec], 1)
    c["floor"] = np.where(c["upto"] > 0, 0.0, -FAR)
    c["dec_same"] = np.where(np.arange(128)[:, None] < T_DEC, same[:, :T_DEC], 0)
    c["dec_seq"] = (p[:, None] // DEC_SEQ) == np.arange(DEC_BATCH)[None, :]
    lev = []
    for n in range(LEVELS):
        s = 1 << n
        lev.append((p[:, None] // (2 * s) == p[None, :] // (2 * s)) & ((p[:, None] // s) % 2 == 0) & ((p[None, :] // s) % 2 == 1))
    c["levels"] = np.stack(lev, 1)
    return c


def gdn_phase(nc, m):
    ctx, sems = ExitStack(), []
    with ctx:
        def sb(name, shape, dt=F32):
            return ctx.enter_context(nc.sbuf_tensor(f"gdn_{name}", shape, dt))

        def sem(name):
            sems.append(nc.alloc_semaphore(f"gdn_{name}"))
            return sems[-1]

        NT, rows, H = TOK_TILES, TILE_ROWS, HEADS
        at = [slice(128 * t, 128 * t + rows[t]) for t in range(NT)]
        resid, ident, ones = m["resid"], m["ident"], m["ones"]
        norm_b, sq, xn = (m["ring"][1][:, 1, D_MODEL * j:D_MODEL * (j + 1)] for j in range(3))
        oT = m["ring"][0][:, 0, 0:H * T_ALL].rearrange("p (h t) -> p h t", h=H)
        osum = m["ring"][1][:, 1, 0:H * T_ALL].rearrange("p (h t) -> p h t", h=H)
        ss = sb("ss", [128, NT])
        xT = sb("xT", [128, KT, T_ALL])
        w_ab = sb("w_ab", [128, KT, 2 * H])
        ab_bias = sb("ab_bias", [128, 2, H])
        ab = sb("ab", [128, NT, 2 * H])
        g = sb("g", [128, NT, H])
        gt = sb("gt", [128, NT, H])
        gt2 = sb("gt2", [128, NT, H])
        beta = sb("beta", [128, NT, H])
        G = sb("G", [128, NT, H])
        eG = sb("eG", [128, NT, H])
        beG = sb("beG", [128, NT, H])
        eL = sb("eL", [128, NT, H])
        decg = sb("decg", [T_DEC, DEC_BATCH, H])
        eLast = sb("eLast", [128, 2 + DEC_BATCH, H])
        w4 = m["ring"][1][:, 0, :].rearrange("p (j k c) -> p j k c", j=4, k=KT)
        st_in = sb("st_in", [28, 3, 128])
        cw = sb("cw", [128, 3, CONV_W])
        cin = sb("cin", [128, 3, CW_COLS])
        ends = sb("ends", [128, 3, 27])
        ends_tok = sb("ends_tok", [27, 3, 128])
        acc = sb("acc", [128, 3, CW_COLS])
        qkv = sb("qkv", [128, 3, T_ALL])
        qk2 = sb("qk2", [128, 2, T_ALL])
        rn = sb("rn", [128, 2, T_ALL])
        kbq = sb("kbq", [128, 2, T_ALL])
        kT = sb("kT", [128, T_ALL])
        eGB = sb("eGB", [128, T_ALL])
        gsrc = sb("gsrc", [128, T_ALL])
        bsrc = sb("bsrc", [128, T_ALL])
        D = sb("D", [128, T_ALL])
        KQD = sb("KQD", [128, 2, 2, 128])
        KQD2 = sb("KQD2", [T_DEC, 2, T_DEC])
        Mlev = sb("Mlev", [128, LEVELS, 2, 128])
        M2 = sb("M2", [T_DEC, 2, T_DEC])
        TU = sb("TU", [128, 2, 2, 128])
        TU2 = sb("TU2", [T_DEC, 2, T_DEC])
        Y = m["ring"][1][:, 1, H * T_ALL:H * T_ALL + LEVELS * 256].rearrange("p (n t i) -> p n t i", n=LEVELS, t=2)
        Y2 = sb("Y2", [T_DEC, T_DEC])
        vb = sb("vb", [128, NT, 128])
        kg = sb("kg", [128, NT, 128])
        kd = sb("kd", [128, NT, 128])
        WQ = sb("WQ", [128, 2, T_ALL])
        wsT = sb("wsT", [128, 2, T_DEC])
        u = sb("u", [128, NT, 128])
        uB = sb("uB", [T_DEC, DEC_BATCH, 128])
        S1 = sb("S1", [128, 128])
        S2 = sb("S2", [128, 128])
        Sd = sb("Sd", [128, DEC_BATCH, 128])
        Sn = sb("Sn", [128, DEC_BATCH, 128])
        o2 = sb("o2", [128, T_ALL])
        ozT = sb("ozT", [128, H, T_ALL])
        onorm = sb("onorm", [128, 1])
        w_out = m["ring"][2][:].rearrange("p a n -> p (a n)").rearrange("p (h n) -> p h n", h=H)

        B = [ctx.enter_context(nc.psum_tensor(f"gdn_bank{i}", [128, 512], F32)) for i in range(8)]

        s = {n: sem(n) for n in (
            "x_in0 x_in1 x_in2 consts_in squares mean_made roots normed xT_made xT_kept ab_made ab_kept exp_in exp_out soft_in soft_out gates_made sums_made "
            "decays_in decays_out "
            "q_in k_in v_in z_in st_loaded st_T proj proj_kept prior_kept ends_copied conv_done silued squares2 sums2 logs2 roots2 ends_T ends_kept ends_stored "
            "src_made bcast eGB_made D_in D_made T0_kept parts_clear kb_made kv_T kv_kept KQ_made lev_made T1_made TU_kept Y_made Y_kept TU_made "
            "W_made W_kept z_kept zs_made joined Sn_decayed rows_kept kT_made Y2_kept u0_made u_kept S1_made S1_kept ws_made ws_kept u2_made u1_made o_made oT_kept S2_made S2_kept Sd_in Sn_made uB_made Sn_kept "
            "S_stored o2_made osum_made osum_kept olog oroot oz_made wout_in out_made out_kept v").split()}

        w_in = m["w_in_a"][0].rearrange("(p t) n -> p t n", t=KT)
        heads_of = [w_in[:, :, j * D_MODEL:(j + 1) * D_MODEL] for j in range(4)]
        slot_in = [s["q_in"], s["k_in"], s["v_in"], s["z_in"]]
        st_conv = m["state_conv"][0].rearrange("b j c -> (b j) c").rearrange("r (s c) -> r s c", s=3)
        cv_w = m["conv_w_a"][0].rearrange("j (s c) -> j s c", s=3)
        st_delta = m["state_delta"][0].rearrange("b h k v -> k h b v")
        out_delta = m["sd_sample"][0].rearrange("b h k v -> k h b v")
        out_delta_p = m["sd_prompt"][0, 0].rearrange("h k v -> k h v")
        out_conv = m["sc_sample"][0].rearrange("b j c -> (b j) c").rearrange("r (s c) -> r s c", s=3)
        out_conv_p = m["sc_prompt"][0, 0].rearrange("j (s c) -> j s c", s=3)
        dec_cin = cin[:, :, DEC0:].rearrange("p s (b c) -> p s b c", c=DEC_STRIDE)
        dec_acc = acc[:, :, DEC0:].rearrange("p s (b c) -> p s b c", c=DEC_STRIDE)[:, :, :, 0:DEC_SEQ]

        def part(a, n, half):
            return a.rearrange("p t (b e c) -> p t b e c", e=2, c=1 << n)[:, :, :, half, :]

        def packed(a, n):
            return a.rearrange("p (t b c) -> p t b c", t=2, c=1 << n)

        block = ctx.enter_context(nc.Block())

        @block.sync
        def _(sp):
            for t in range(NT):
                src = m["x_prompt"][0, at[t], :] if t < 2 else m["x_sample"].rearrange("b l d -> (b l) d")
                sp.dma_start(resid[0:rows[t], t, :], src).then_inc((s["x_in0"], s["x_in1"], s["x_in2"])[t], 16)
            sp.dma_start(norm_b[:], m["norm_a"][0:1, :].broadcast_to([128, D_MODEL])).then_inc(s["consts_in"], 16)
            sp.dma_start(m["consts"][:], m["consts_dram"]).then_inc(s["consts_in"], 16)
            sp.dma_start(w_ab[:], w_in[:, :, CONV_CH + D_MODEL:GDN_IN]).then_inc(s["consts_in"], 16)
            sp.dma_start(ab_bias[:, 0, :], m["a_log"][0:1, :].broadcast_to([128, H])).then_inc(s["consts_in"], 16)
            sp.dma_start(ab_bias[:, 1, :], m["dt_bias"][0:1, :].broadcast_to([128, H])).then_inc(s["consts_in"], 16)
            sp.dma_start(onorm[:], m["onorm_a"].rearrange("a v -> v a")).then_inc(s["consts_in"], 16)

            def load_rows(h):
                if not (isinstance(h, int) and h == 0):
                    sp.wait_ge(s["st_T"], h)
                for r, src in ((slice(0, 24), st_conv), (slice(24, 28), cv_w)):
                    sp.dma_start(st_in[r, :, :], src[:, :, bass.ds(h * 128, 128)]).then_inc(s["st_loaded"], 16)

            def load(h, j):
                if not (isinstance(h, int) and h == 0):
                    sp.wait_ge(s["proj"], 4 * h - 3 + j)
                sp.dma_start(w4[:, j], heads_of[j][:, :, bass.ds(h * 128, 128)]).then_inc(slot_in[j], 16)

            def load_state(h):
                if not (isinstance(h, int) and h == 0):
                    sp.wait_ge(s["ws_made"], h)
                    sp.wait_ge(s["Sn_decayed"], h)
                sp.dma_start(Sd[:], st_delta[:, bass.ds(h, 1), :, :].rearrange("k h b v -> k (h b) v")).then_inc(s["Sd_in"], 16)

            def store_ends(h):
                sp.wait_ge(s["ends_kept"], h + 1)
                sp.dma_start(out_conv_p[:, :, bass.ds(h * 128, 128)], ends_tok[0:3, :, :]).then_inc(s["ends_stored"], 16)
                sp.dma_start(out_conv[:, :, bass.ds(h * 128, 128)], ends_tok[3:27, :, :]).then_inc(s["ends_stored"], 16)

            def store_states(h):
                sp.wait_ge(s["S2_kept"], h + 1)
                sp.dma_start(out_delta_p[:, bass.ds(h, 1), :].rearrange("k h v -> k (h v)"), S2[:]).then_inc(s["S_stored"], 16)
                sp.wait_ge(s["Sn_kept"], 2 * h + 2)
                sp.dma_start(out_delta[:, bass.ds(h, 1), :, :].rearrange("k h b v -> k (h b) v"), Sn[:]).then_inc(s["S_stored"], 16)

            def serve(h, ahead, following):
                store_ends(h)
                if ahead:
                    load(h + 3, 0)
                    load(h + 3, 1)
                    load_rows(h + 3)
                    load(h + 3, 2)
                if following:
                    load_state(h + 1)
                if ahead:
                    load(h + 3, 3)
                store_states(h)

            for h in range(3):
                if h < 2:
                    load_rows(h)
                for j in range(4):
                    load(h, j)
                if h == 0:
                    load_state(0)
            load_rows(2)
            serve(0, True, True)
            with sp.Fori(1, H - 3) as h:
                serve(h, True, True)
            serve(H - 3, False, True)
            serve(H - 2, False, True)
            sp.dma_start(w_out, m["w_out_a"][0].rearrange("(h p) n -> p h n", p=128)).then_inc(s["wout_in"], 16)
            serve(H - 1, False, False)
            sp.wait_ge(s["ends_stored"], 32 * H)
            sp.wait_ge(s["S_stored"], 32 * H)
            sp.wait_ge(s["oz_made"], H // 2)
            m["prefetch"](sp, 0, (0, 1))
            sp.wait_ge(s["out_made"], 2 * NT)
            m["prefetch"](sp, 0, (2,))

        @block.gpsimd
        def _(pool):
            nc.gpsimd.memset(cin[:, :, 0:CONV_W - 1], 0.0).then_inc(s["prior_kept"], 1)
            pool.wait_ge(s["xT_made"], 2 * NT)
            nc.gpsimd.memset(Y[:], 0.0).then_inc(s["parts_clear"], 1)
            nc.gpsimd.memset(Mlev[:], 0.0).then_inc(s["parts_clear"], 1)
            pool.wait_ge(s["gates_made"], 1)

            def head(h):
                if not (isinstance(h, int) and h == 0):
                    pool.wait_ge(s["bcast"], h)
                    pool.wait_ge(s["ends_T"], h)
                pool.wait_ge(s["proj_kept"], 6 * h + 6)
                for t in range(NT):
                    r = rows[t]
                    nc.gpsimd.tensor_tensor(gsrc[0:r, at[t]], m["upto"][0:r, at[t]], g[0:r, t, bass.ds(h, 1)].broadcast_to([r, r]), ALU.mult).then_inc(s["src_made"], 1)
                    nc.gpsimd.tensor_tensor(bsrc[0:r, at[t]], ident[0:r, 0:r], beta[0:r, t, bass.ds(h, 1)].broadcast_to([r, r]), ALU.mult).then_inc(s["src_made"], 1)
                nc.gpsimd.tensor_copy(ends[:, :, 0:3], cin[:, :, SEQ:SEQ + 3]).then_inc(s["ends_copied"], 1)
                for j in range(3):
                    nc.gpsimd.tensor_copy(ends[:, j, 3:27].rearrange("p (b c) -> p b c", c=3), dec_cin[:, j, :, DEC_SEQ:]).then_inc(s["ends_copied"], 1)

            def states(h):
                pool.wait_ge(s["Sd_in"], 16 * h + 16)
                if not (isinstance(h, int) and h == 0):
                    pool.wait_ge(s["S_stored"], 32 * h)
                nc.gpsimd.tensor_tensor(Sn[:], Sd[:], eLast[:, 2:, bass.ds(h, 1)].broadcast_to([128, DEC_BATCH, 128]), ALU.mult).then_inc(s["Sn_decayed"], 1)
                pool.wait_ge(s["u_kept"], 3 * h + 3)
                nc.gpsimd.tensor_tensor(uB[:], u[0:T_DEC, 2, :].unsqueeze(1).broadcast_to([T_DEC, DEC_BATCH, 128]),
                                        m["dec_seq"][0:T_DEC, :].unsqueeze(2).broadcast_to([T_DEC, DEC_BATCH, 128]), ALU.mult).then_inc(s["uB_made"], 1)

            head(0)
            head(1)
            pool.wait_ge(s["decays_out"], 3)
            states(0)
            with pool.Fori(1, H - 1) as h:
                head(h + 1)
                states(h)
            states(H - 1)

        @block.scalar
        def _(act):
            A = nc.scalar
            for t in range(NT):
                r = rows[t]
                act.wait_ge((s["x_in0"], s["x_in1"], s["x_in2"])[t], 16)
                if t == 0:
                    act.wait_ge(s["squares"], 1)
                A.activation(sq[0:r, :], resid[0:r, t, :], ACT.Square, accum_out=ss[0:r, t:t + 1]).then_inc(s["squares"], 1)
                act.wait_ge(s["squares"], t + 2)
            act.wait_ge(s["mean_made"], 1)
            A.activation(ss[:, :], ss[:, :], ACT.Sqrt).then_inc(s["roots"], 1)
            for t in range(NT):
                act.wait_ge(s["xT_made"], 2 * t + 2)
                A.copy(xT[:, 4:8, at[t]], B[1][:, :].rearrange("p (k r) -> p k r", k=4)[:, :, 0:rows[t]]).then_inc(s["xT_kept"], 1)
            act.wait_ge(s["exp_in"], 1)
            A.activation(gt[:], gt[:], ACT.Exp).then_inc(s["exp_out"], 1)
            A.activation(beta[:], beta[:], ACT.Exp).then_inc(s["exp_out"], 1)
            A.activation(ab_bias[:, 0, :], ab_bias[:, 0, :], ACT.Exp).then_inc(s["exp_out"], 1)
            act.wait_ge(s["exp_out"], 3)
            act.wait_ge(s["soft_in"], 1)
            A.activation(gt[:], gt[:], ACT.Ln).then_inc(s["soft_out"], 1)

            def evacuate(h, j):
                act.wait_ge(s["proj"], 4 * h + j + 1)
                if j == 0 and not (isinstance(h, int) and h == 0):
                    act.wait_ge(s["conv_done"], h)
                    act.wait_ge(s["ends_copied"], 4 * h)
                src = B[j % 2]
                if j < 3:
                    A.copy(cin[:, j, 3:3 + SEQ], src[:, 0:SEQ]).then_inc(s["proj_kept"], 1)
                    A.copy(dec_cin[:, j, :, 3:], src[:, SEQ:T_ALL].rearrange("p (b c) -> p b c", c=DEC_SEQ)).then_inc(s["proj_kept"], 1)
                else:
                    A.copy(ozT[:, bass.ds(h, 1), :].rearrange("p o t -> p (o t)"), src[:, 0:T_ALL]).then_inc(s["z_kept"], 1)

            def silu_z(h):
                z = ozT[:, bass.ds(h, 1), :].rearrange("p o t -> p (o t)")
                act.wait_ge(s["z_kept"], h + 1)
                A.activation(z, z, ACT.Silu).then_inc(s["zs_made"], 1)

            def silu_qkv(h):
                act.wait_ge(s["conv_done"], h + 1)
                A.activation(qkv[:, :, 0:SEQ], acc[:, :, 0:SEQ], ACT.Silu).then_inc(s["silued"], 1)
                A.activation(qkv[:, :, SEQ:].rearrange("p s (b c) -> p s b c", c=DEC_SEQ), dec_acc, ACT.Silu).then_inc(s["silued"], 1)

            def norms(h):
                act.wait_ge(s["sums2"], h + 1)
                for j in range(2):
                    A.activation(rn[:, j, :], B[2 + j][:, 0:T_ALL], ACT.Ln, bias=m["eps"][:, 0:1]).then_inc(s["logs2"], 1)
                act.wait_ge(s["logs2"], 2 * h + 2)
                A.activation(rn[:], rn[:], ACT.Exp, scale=-0.5).then_inc(s["roots2"], 1)

            def decays(h):
                act.wait_ge(s["bcast"], h + 1)
                A.activation(eGB[:, :], B[2][:, 0:T_ALL], ACT.Exp).then_inc(s["eGB_made"], 1)
                act.wait_ge(s["D_in"], h + 1)
                A.activation(D[:, 0:256], D[:, 0:256], ACT.Exp).then_inc(s["D_made"], 1)
                A.activation(D[0:T_DEC, 256:], D[0:T_DEC, 256:], ACT.Exp).then_inc(s["D_made"], 1)

            def chain(h, prepare, projected):
                act.wait_ge(s["kv_T"], h + 1)
                for t in range(2):
                    kt, vt = B[6][:, 256 * t:256 * t + 128], B[6][:, 256 * t + 128:256 * t + 256]
                    A.activation(vb[:, t, :], vt, ACT.Copy, scale=beta[:, t, bass.ds(h, 1)]).then_inc(s["kv_kept"], 1)
                    A.activation(kg[:, t, :], kt, ACT.Copy, scale=beG[:, t, bass.ds(h, 1)]).then_inc(s["kv_kept"], 1)
                    A.activation(kd[:, t, :], kt, ACT.Copy, scale=eL[:, t, bass.ds(h, 1)]).then_inc(s["kv_kept"], 1)
                kt, vt = B[7][0:T_DEC, 0:128], B[7][0:T_DEC, 128:256]
                A.activation(vb[0:T_DEC, 2, :], vt, ACT.Copy, scale=beta[0:T_DEC, 2, bass.ds(h, 1)]).then_inc(s["kv_kept"], 1)
                A.activation(kg[0:T_DEC, 2, :], kt, ACT.Copy, scale=beG[0:T_DEC, 2, bass.ds(h, 1)]).then_inc(s["kv_kept"], 1)
                A.activation(kd[0:T_DEC, 2, :], kt, ACT.Copy, scale=eL[0:T_DEC, 2, bass.ds(h, 1)]).then_inc(s["kv_kept"], 1)
                act.wait_ge(s["ends_T"], h + 1)
                if not (isinstance(h, int) and h == 0):
                    act.wait_ge(s["ends_stored"], 32 * h)
                A.copy(ends_tok[:, :, :], B[7][0:27, 0:384].rearrange("p (s c) -> p s c", s=3)).then_inc(s["ends_kept"], 1)
                silu_z(h)
                if prepare:
                    silu_qkv(h + 1)
                if projected:
                    evacuate(h + 2, 0)
                    evacuate(h + 2, 1)
                if prepare:
                    norms(h + 1)
                if projected:
                    evacuate(h + 2, 2)
                if prepare:
                    decays(h + 1)
                if projected:
                    evacuate(h + 2, 3)
                act.wait_ge(s["osum_made"], h + 1)
                A.copy(osum[:, bass.ds(h, 1), :].rearrange("p o t -> p (o t)"), B[7][:, 0:T_ALL]).then_inc(s["osum_kept"], 1)

            for j in range(4):
                evacuate(0, j)
            act.wait_ge(s["decays_in"], 1)
            A.activation(eG[:], G[:], ACT.Exp).then_inc(s["decays_out"], 1)
            A.activation(eL[:], eL[:], ACT.Exp).then_inc(s["decays_out"], 1)
            A.activation(eLast[:], eLast[:], ACT.Exp).then_inc(s["decays_out"], 1)
            silu_qkv(0)
            for j in range(4):
                evacuate(1, j)
            norms(0)
            decays(0)
            chain(0, True, True)
            with act.Fori(1, H - 2) as h:
                chain(h, True, True)
            chain(H - 2, True, False)
            chain(H - 1, False, False)
            act.wait_ge(s["osum_kept"], H)
            for j in range(H // 2):
                v = osum[:, 2 * j:2 * j + 2, :]
                A.activation(v, v, ACT.Ln, scale=1.0 / DK, bias=m["eps"][:, 0:1]).then_inc(s["olog"], 1)
            for j in range(H // 2):
                v = osum[:, 2 * j:2 * j + 2, :]
                act.wait_ge(s["olog"], j + 1)
                A.activation(v, v, ACT.Exp, scale=-0.5).then_inc(s["oroot"], 1)

        @block.vector
        def _(dve):
            V = nc.vector
            st = {"base": 0, "n": 0}

            def link(ins):
                st["n"] += 1
                ins.then_inc(s["v"], 1)
                dve.wait_ge(s["v"], st["base"] + st["n"])

            V.memset(ss[:], 1.0).then_inc(s["squares"], 1)
            link(V.memset(ab[:], 0.0))
            link(V.memset(G[:], 0.0))
            link(V.memset(eL[:], 0.0))
            dve.wait_ge(s["squares"], NT + 1)
            V.tensor_scalar(ss[:, :], ss[:, :], 1.0 / D_MODEL, EPS, ALU.mult, ALU.add).then_inc(s["mean_made"], 1)
            dve.wait_ge(s["roots"], 1)
            link(V.reciprocal(ss[:, :], ss[:, :]))
            dve.wait_ge(s["consts_in"], 16 * 6)
            for t in range(NT):
                r = rows[t]
                if t:
                    dve.wait_ge(s["xT_made"], 2 * t)
                V.scalar_tensor_tensor(xn[0:r, :], resid[0:r, t, :], ss[0:r, t:t + 1], norm_b[0:r, :], ALU.mult, ALU.mult).then_inc(s["normed"], 1)
                dve.wait_ge(s["xT_made"], 2 * t + 1)
                V.tensor_copy(xT[:, 0:4, at[t]], B[0][:, :].rearrange("p (k r) -> p k r", k=4)[:, :, 0:r]).then_inc(s["xT_kept"], 1)
            dve.wait_ge(s["ab_made"], 1)
            for t in range(NT):
                r = rows[t]
                link(V.tensor_copy(ab[0:r, t, :], B[2][0:r, 16 * t:16 * t + 16]))

            def all_tiles(a):
                return a.unsqueeze(1).broadcast_to([128, NT, H])

            link(V.tensor_scalar(beta[:], ab[:, :, 0:H], -1.0, None, ALU.mult))
            link(V.tensor_tensor(g[:], ab[:, :, H:], all_tiles(ab_bias[:, 1, :]), ALU.add))
            link(V.tensor_scalar(gt2[:], g[:], -1.0, None, ALU.mult))
            V.tensor_tensor(gt[:], gt2[:], g[:], ALU.min).then_inc(s["exp_in"], 1)
            link(V.tensor_scalar(g[:], g[:], 0.0, None, ALU.max))
            dve.wait_ge(s["exp_out"], 3)
            V.tensor_scalar(gt[:], gt[:], 1.0, None, ALU.add).then_inc(s["soft_in"], 1)
            link(V.tensor_scalar(beta[:], beta[:], 1.0, None, ALU.add))
            link(V.reciprocal(beta[:], beta[:]))
            dve.wait_ge(s["soft_out"], 1)
            link(V.tensor_tensor(g[:], g[:], gt[:], ALU.add))
            link(V.tensor_tensor(g[:], g[:], all_tiles(ab_bias[:, 0, :]), ALU.mult))
            link(V.tensor_scalar(g[:], g[:], -1.0, None, ALU.mult))
            V.tensor_tensor(decg[:], g[0:T_DEC, 2, :].unsqueeze(1).broadcast_to([T_DEC, DEC_BATCH, H]),
                            m["dec_seq"][0:T_DEC, :].unsqueeze(2).broadcast_to([T_DEC, DEC_BATCH, H]), ALU.mult).then_inc(s["gates_made"], 1)
            dve.wait_ge(s["sums_made"], 1)
            for t in range(NT):
                r = rows[t]
                link(V.tensor_copy(G[0:r, t, :], B[2][0:r, 8 * t:8 * t + 8]))
                link(V.tensor_tensor(eL[0:r, t, :], B[2][0:r, 24 + 8 * t:32 + 8 * t], G[0:r, t, :], ALU.subtract))
            link(V.tensor_copy(eLast[:, 0:2, :], B[2][:, 24:40].rearrange("p (t h) -> p t h", t=2)))
            V.tensor_copy(eLast[:, 2:, :], B[2][:, 64:128].rearrange("p (b h) -> p b h", h=H)).then_inc(s["decays_in"], 1)
            dve.wait_ge(s["decays_out"], 3)
            link(V.tensor_tensor(beG[:], beta[:], eG[:], ALU.mult))

            def conv_rows(h):
                dve.wait_ge(s["st_T"], h + 1)
                v = B[7][:, 0:84].rearrange("p (s c) -> p s c", s=3)
                V.tensor_copy(cw[:, :, :], v[:, :, 24:28]).then_inc(s["rows_kept"], 1)
                for j in range(3):
                    V.tensor_copy(dec_cin[:, j, :, 0:3], v[:, j, 0:24].rearrange("p (b c) -> p b c", c=3)).then_inc(s["rows_kept"], 1)

            def conv(h, lo, hi):
                if lo == 0:
                    dve.wait_ge(s["rows_kept"], 4 * h + 4)
                    dve.wait_ge(s["proj_kept"], 6 * h + 6)
                    if not (isinstance(h, int) and h == 0):
                        dve.wait_ge(s["silued"], 2 * h)
                for step in range(lo, hi):
                    tap, j = divmod(step, 3)
                    src = cin[:, j, tap:tap + ACC_COLS]
                    if tap == 0:
                        ins = V.tensor_scalar(acc[:, j, 0:ACC_COLS], src, cw[:, j, 0:1], None, ALU.mult)
                    else:
                        ins = V.scalar_tensor_tensor(acc[:, j, 0:ACC_COLS], src, cw[:, j, tap:tap + 1], acc[:, j, 0:ACC_COLS], ALU.mult, ALU.add)
                    if step == 11:
                        ins.then_inc(s["conv_done"], 1)
                    elif j == 2 or step == hi - 1:
                        link(ins)

            def squares(h):
                dve.wait_ge(s["silued"], 2 * h + 2)
                V.tensor_tensor(qk2[:], qkv[:, 0:2, :], qkv[:, 0:2, :], ALU.mult).then_inc(s["squares2"], 1)

            def normed(h):
                dve.wait_ge(s["roots2"], h + 1)
                link(V.scalar_tensor_tensor(kbq[:, 1, :], qkv[:, 0, :], DK ** -0.5, rn[:, 0, :], ALU.mult, ALU.mult))
                V.tensor_tensor(kT[:, :], qkv[:, 1, :], rn[:, 1, :], ALU.mult).then_inc(s["kT_made"], 1)
                dve.wait_ge(s["kT_made"], h + 1)

            def decays(h):
                dve.wait_ge(s["bcast"], h + 1)
                V.tensor_tensor(kbq[:, 0, :], kT[:, :], B[3][:, 0:T_ALL], ALU.mult).then_inc(s["kb_made"], 1)
                dve.wait_ge(s["eGB_made"], h + 1)
                for t in range(NT):
                    r = rows[t]
                    ins = V.scalar_tensor_tensor(D[0:r, at[t]], B[2][0:r, at[t]], G[0:r, t, bass.ds(h, 1)], m["floor"][0:r, at[t]], ALU.subtract, ALU.min)
                    if t == 2:
                        ins.then_inc(s["D_in"], 1)

            def chain(h, prepare, projected):
                first = isinstance(h, int) and h == 0
                link(V.tensor_tensor(WQ[:, 1, :], kbq[:, 1, :], eGB[:, :], ALU.mult))
                dve.wait_ge(s["D_made"], 2 * h + 2)
                dve.wait_ge(s["KQ_made"], h + 1)
                link(V.tensor_tensor(KQD[:].rearrange("p t a i -> p t a i"), B[4][:, :].rearrange("p (t a i) -> p t a i", t=2, a=2),
                                     D[:, 0:256].rearrange("p (t i) -> p t i", t=2).unsqueeze(2).broadcast_to([128, 2, 2, 128]), ALU.mult))
                link(V.tensor_tensor(KQD2[:], B[5][0:T_DEC, 0:2 * T_DEC].rearrange("p (a i) -> p a i", a=2),
                                     D[0:T_DEC, 256:].unsqueeze(1).broadcast_to([T_DEC, 2, T_DEC]), ALU.mult))

                def joins(n):
                    mask = m["levels"][:, n, :].unsqueeze(1).broadcast_to([128, 2, 128])
                    return V.tensor_tensor(part(Mlev[:, n], n, 1), part(KQD[:, :, 0, :], n, 1), part(mask, n, 1), ALU.mult)

                if first:
                    dve.wait_ge(s["parts_clear"], 2)
                joins(0)
                for n in range(2):
                    last = V.tensor_tensor(M2[:, n, :], KQD2[:, 0, :], m["levels"][0:T_DEC, n, 0:T_DEC], ALU.mult)
                link(last)
                V.tensor_tensor(TU[:, :, 1, :], ident[:, :].unsqueeze(1).broadcast_to([128, 2, 128]), Mlev[:, 0], ALU.subtract)
                V.tensor_tensor(TU2[:, 1, :], ident[0:T_DEC, 0:T_DEC], M2[:, 0, :], ALU.subtract).then_inc(s["lev_made"], 1)
                joins(1).then_inc(s["joined"], 1)
                dve.wait_ge(s["T1_made"], h + 1)
                V.tensor_copy(TU[:, :, 0, :], B[4][:, 0:256].rearrange("p (t i) -> p t i", t=2)).then_inc(s["TU_kept"], 1)
                V.tensor_copy(TU2[:, 0, :], B[4][0:T_DEC, 256:288]).then_inc(s["TU_kept"], 1)
                for n in range(1, LEVELS):
                    k = (LEVELS - 1) * h + n
                    if n + 1 < LEVELS:
                        joins(n + 1).then_inc(s["joined"], 1)
                    dve.wait_ge(s["Y_made"], k)
                    V.tensor_copy(part(Y[:, n], n, 0), packed(B[4][:, 0:128], n)).then_inc(s["Y_kept"], 1)
                    if n == 1:
                        V.tensor_copy(Y2[:], B[4][0:T_DEC, 256:288]).then_inc(s["Y2_kept"], 1)
                    if prepare:
                        if n <= 3:
                            conv(h + 1, 4 * n - 4, 4 * n - 2)
                    dve.wait_ge(s["TU_made"], k)
                    if n < LEVELS - 1:
                        V.tensor_tensor(part(TU[:, :, 0, :], n, 0), part(TU[:, :, 0, :], n, 0), packed(B[5][:, 0:128], n), ALU.subtract).then_inc(s["T0_kept"], 1)
                    V.tensor_tensor(part(TU[:, :, 1, :], n, 1), part(TU[:, :, 1, :], n, 1), packed(B[5][:, 128:256], n), ALU.subtract).then_inc(s["TU_kept"], 1)
                    if n == 1:
                        V.tensor_tensor(TU2[:], TU2[:], B[7][0:T_DEC, 0:64].rearrange("p (a i) -> p a i", a=2), ALU.subtract).then_inc(s["TU_kept"], 1)
                    if prepare:
                        if n <= 3:
                            conv(h + 1, 4 * n - 2, 4 * n)
                        elif n == 4:
                            squares(h + 1)
                        elif n == 5 and projected:
                            conv_rows(h + 2)
                dve.wait_ge(s["W_made"], h + 1)
                V.tensor_scalar(WQ[:, 0, :], B[6][:, 0:T_ALL], -1.0, None, ALU.mult).then_inc(s["W_kept"], 1)
                dve.wait_ge(s["u0_made"], h + 1)
                V.tensor_copy(u[:, 0, :], B[7][:, 0:128]).then_inc(s["u_kept"], 1)
                if prepare:
                    normed(h + 1)
                dve.wait_ge(s["ws_made"], h + 1)
                V.tensor_copy(wsT[:], B[5][:, 0:64].rearrange("p (b a c) -> p a b c", a=2, c=DEC_SEQ)).then_inc(s["ws_kept"], 1)
                dve.wait_ge(s["S1_made"], h + 1)
                V.tensor_copy(S1[:, :], B[4][:, 0:128]).then_inc(s["S1_kept"], 1)
                dve.wait_ge(s["u2_made"], h + 1)
                V.tensor_copy(u[:, 1, :], B[7][:, 0:128]).then_inc(s["u_kept"], 1)
                V.tensor_copy(u[0:T_DEC, 2, :], B[7][0:T_DEC, 128:256]).then_inc(s["u_kept"], 1)
                dve.wait_ge(s["o_made"], h + 1)
                o = oT[:, bass.ds(h, 1), :].rearrange("p o t -> p (o t)")
                V.tensor_copy(o, B[6][:, 0:T_ALL]).then_inc(s["oT_kept"], 1)
                dve.wait_ge(s["oT_kept"], h + 1)
                V.tensor_tensor(o2[:, :], o, o, ALU.mult).then_inc(s["o2_made"], 1)
                dve.wait_ge(s["S2_made"], h + 1)
                if not first:
                    dve.wait_ge(s["S_stored"], 32 * h)
                V.scalar_tensor_tensor(S2[:, :], S1[:, :], eLast[:, 1, bass.ds(h, 1)], B[5][:, 0:128], ALU.mult, ALU.add).then_inc(s["S2_kept"], 1)
                if prepare:
                    decays(h + 1)
                dve.wait_ge(s["Sn_decayed"], h + 1)
                dve.wait_ge(s["Sn_made"], h + 1)
                for j in range(2):
                    V.tensor_tensor(Sn[:, 4 * j:4 * j + 4, :], Sn[:, 4 * j:4 * j + 4, :], B[4 + j][:, :].rearrange("p (b v) -> p b v", b=4), ALU.add).then_inc(s["Sn_kept"], 1)

            dve.wait_ge(s["prior_kept"], 1)
            conv_rows(0)
            conv(0, 0, 12)
            conv_rows(1)
            squares(0)
            normed(0)
            decays(0)
            chain(0, True, True)
            pre = st["n"]
            with dve.Fori(1, H - 2) as h:
                st["base"], st["n"] = (h - 1) * V_STEPS + pre, 0
                chain(h, True, True)
                assert st["n"] == V_STEPS, st["n"]
            st["base"], st["n"] = (H - 3) * V_STEPS + pre, 0
            chain(H - 2, True, False)
            chain(H - 1, False, False)
            for j in range(H // 2):
                v, o, z = (x[:, 2 * j:2 * j + 2, :] for x in (osum, oT, ozT))
                dve.wait_ge(s["oroot"], j + 1)
                link(V.tensor_tensor(v, v, o, ALU.mult))
                if j == 0:
                    dve.wait_ge(s["zs_made"], H)
                V.scalar_tensor_tensor(z, v, onorm[:, 0:1], z, ALU.mult, ALU.mult).then_inc(s["oz_made"], 1)
            for t in range(NT):
                r = rows[t]
                for j in range(2):
                    dve.wait_ge(s["out_made"], 2 * t + j + 1)
                    out = B[2 * t + j] if t < 2 else B[4 + j]
                    V.tensor_tensor(resid[0:r, t, 512 * j:512 * j + 512], resid[0:r, t, 512 * j:512 * j + 512], out[0:r, :], ALU.add).then_inc(s["out_kept"], 1)
            dve.wait_ge(s["out_kept"], 2 * NT)

        @block.tensor
        def _(pe):
            T = nc.tensor
            xv = xn[:, :].rearrange("p (c k) -> p k c", k=KT)
            for t in range(NT):
                r = rows[t]
                pe.wait_ge(s["normed"], t + 1)
                if t:
                    pe.wait_ge(s["xT_kept"], 2 * t)
                for k in range(KT):
                    last = T.transpose(B[k // 4][:, 128 * (k % 4):128 * (k % 4) + r], xv[0:r, k, :], ident[0:r, 0:r])
                    if k % 4 == 3:
                        last.then_inc(s["xT_made"], 1)
            pe.wait_ge(s["xT_kept"], 2 * NT)
            for t in range(NT):
                for k in range(KT):
                    last = T.matmul(B[2][0:rows[t], 16 * t:16 * t + 16], xT[:, k, at[t]], w_ab[:, k, :], start=(k == 0), stop=(k == KT - 1))
            last.then_inc(s["ab_made"], 1)

            def project(h, j, lo=0, hi=KT):
                if lo == 0:
                    first = isinstance(h, int) and h == 0
                    pe.wait_ge(slot_in[j], 16 * h + 16)
                    if j == 0 and not first:
                        pe.wait_ge(s["proj_kept"], 6 * h)
                    elif j == 1 and not first:
                        pe.wait_ge(s["z_kept"], h)
                    elif j == 2:
                        pe.wait_ge(s["proj_kept"], 6 * h + 2)
                    elif j == 3:
                        pe.wait_ge(s["proj_kept"], 6 * h + 4)
                for k in range(lo, hi):
                    last = T.matmul(B[j % 2][:, 0:T_ALL], w4[:, j, k, :], xT[:, k, :], start=(k == 0), stop=(k == KT - 1))
                if hi == KT:
                    last.then_inc(s["proj"], 1)

            def conv_rows():
                for j in range(3):
                    last = T.transpose(B[7][:, 28 * j:28 * j + 28], st_in[:, j, :], ident[0:28, 0:28])
                last.then_inc(s["st_T"], 1)

            def norm_sums(h):
                pe.wait_ge(s["squares2"], h + 1)
                for j in range(2):
                    last = T.matmul(B[2 + j][:, 0:T_ALL], ones[:, :], qk2[:, j, :], start=True, stop=True)
                last.then_inc(s["sums2"], 1)

            def broadcasts(h):
                pe.wait_ge(s["src_made"], 6 * h + 6)
                pe.wait_ge(s["roots2"], h + 1)
                for src, bank in ((gsrc, 2), (bsrc, 3)):
                    for t in range(NT):
                        last = T.matmul(B[bank][:, at[t]], ones[0:rows[t], :], src[0:rows[t], at[t]], start=True, stop=True)
                last.then_inc(s["bcast"], 1)

            def chain(h, prepare, projected):
                first = isinstance(h, int) and h == 0
                pe.wait_ge(s["kT_made"], h + 1)
                if not first:
                    pe.wait_ge(s["oT_kept"], h)
                    pe.wait_ge(s["osum_kept"], h)
                for t in range(2):
                    T.transpose(B[6][:, 256 * t:256 * t + 128], kT[:, at[t]], ident[:, :])
                    T.transpose(B[6][:, 256 * t + 128:256 * t + 256], qkv[:, 2, at[t]], ident[:, :])
                T.transpose(B[7][0:T_DEC, 0:128], kT[:, at[2]], ident[:, :])
                T.transpose(B[7][0:T_DEC, 128:256], qkv[:, 2, at[2]], ident[:, :]).then_inc(s["kv_T"], 1)
                pe.wait_ge(s["kb_made"], h + 1)
                if not first:
                    pe.wait_ge(s["Sn_kept"], 2 * h)
                for t in range(2):
                    T.matmul(B[4][:, 256 * t:256 * t + 256].rearrange("p (a i) -> p a i", a=2), kT[:, at[t]], kbq[:, :, at[t]], start=True, stop=True)
                T.matmul(B[5][0:T_DEC, 0:64].rearrange("p (a i) -> p a i", a=2), kT[:, at[2]], kbq[:, :, at[2]], start=True, stop=True).then_inc(s["KQ_made"], 1)
                if projected:
                    project(h + 2, 0, 0, 3)
                pe.wait_ge(s["ends_copied"], 4 * h + 4)
                pe.wait_ge(s["kv_kept"], 9 * h + 9)
                for j in range(3):
                    last = T.transpose(B[7][0:27, 128 * j:128 * j + 128], ends[:, j, :], ident[:, :])
                last.then_inc(s["ends_T"], 1)
                pe.wait_ge(s["lev_made"], h + 1)
                for t in range(2):
                    T.transpose(B[4][:, 128 * t:128 * t + 128], TU[:, t, 1, :], ident[:, :])
                T.transpose(B[4][0:T_DEC, 256:288], TU2[:, 1, :], ident[0:T_DEC, 0:T_DEC]).then_inc(s["T1_made"], 1)
                if projected:
                    project(h + 2, 0, 3, 5)
                fill = {1: ((0, 5, 6), (0, 6, 8)), 2: ((1, 0, 2), (1, 2, 4)), 3: ((1, 4, 6), (1, 6, 8)), 5: ((2, 0, 2), (2, 2, 4)), 6: ((2, 4, 6), (2, 6, 8))}
                for n in range(1, LEVELS):
                    k = (LEVELS - 1) * h + n
                    kept = (LEVELS + 2) * h + n + (1 if n == 1 else 2)
                    pe.wait_ge(s["TU_kept"], kept)
                    pe.wait_ge(s["joined"], (LEVELS - 1) * h + n)
                    if n == 4 and projected:
                        pe.wait_ge(s["st_loaded"], 32 * h + 96)
                    for t in range(2):
                        last = T.matmul(packed(B[4][:, 0:128], n)[:, t], Mlev[:, n, t, :], part(TU[:, :, 0, :], n, 0)[:, t], start=True, stop=True)
                    if n == 1:
                        last = T.matmul(B[4][0:T_DEC, 256:288], M2[:, 1, :], TU2[:, 0, :], start=True, stop=True)
                    last.then_inc(s["Y_made"], 1)
                    if projected and n in fill:
                        project(h + 2, *fill[n][0])
                    pe.wait_ge(s["Y_kept"], k)
                    if n == 1:
                        pe.wait_ge(s["Y2_kept"], h + 1)
                        pe.wait_ge(s["ends_kept"], h + 1)
                    for t in range(2):
                        if n < LEVELS - 1:
                            T.matmul(packed(B[5][:, 0:128], n)[:, t], TU[:, t, 1, :], part(Y[:, n], n, 0)[:, t], start=True, stop=True)
                        last = T.matmul(packed(B[5][:, 128:256], n)[:, t], Y[:, n, t, :], part(TU[:, :, 1, :], n, 1)[:, t], start=True, stop=True)
                    if n == 1:
                        T.matmul(B[7][0:T_DEC, 0:32], TU2[:, 1, :], Y2[:, :], start=True, stop=True)
                        last = T.matmul(B[7][0:T_DEC, 32:64], Y2[:, :], TU2[:, 1, :], start=True, stop=True)
                    last.then_inc(s["TU_made"], 1)
                    if n == 4 and projected:
                        conv_rows()
                    if n == 5 and prepare:
                        norm_sums(h + 1)
                    if projected and n in fill:
                        project(h + 2, *fill[n][1])
                pe.wait_ge(s["TU_kept"], (LEVELS + 2) * h + LEVELS + 2)
                for t in range(NT):
                    r = rows[t]
                    inv = TU[:, t, 1, :] if t < 2 else TU2[:, 1, :]
                    last = T.matmul(B[6][:, at[t]], kg[0:r, t, :], inv, start=True, stop=True)
                last.then_inc(s["W_made"], 1)
                if projected:
                    pe.wait_ge(s["rows_kept"], 4 * h + 12)
                T.matmul(B[7][:, 0:128], TU[:, 0, 1, :], vb[:, 0, :], start=True, stop=True).then_inc(s["u0_made"], 1)
                if prepare:
                    broadcasts(h + 1)
                pe.wait_ge(s["W_kept"], h + 1)
                pe.wait_ge(s["Sd_in"], 16 * h + 16)
                for b in range(DEC_BATCH):
                    c = SEQ + DEC_SEQ * b
                    last = T.matmul(B[5][:, 8 * b:8 * b + 8].rearrange("p (a c) -> p a c", a=2), Sd[:, b, :], WQ[:, :, c:c + DEC_SEQ], start=True, stop=True)
                last.then_inc(s["ws_made"], 1)
                pe.wait_ge(s["u_kept"], 3 * h + 1)
                T.matmul(B[4][:, 0:128], kd[:, 0, :], u[:, 0, :], start=True, stop=True).then_inc(s["S1_made"], 1)
                if projected:
                    project(h + 2, 3, 0, 3)
                pe.wait_ge(s["S1_kept"], h + 1)
                pe.wait_ge(s["ws_kept"], h + 1)
                T.matmul(B[7][:, 0:128], TU[:, 1, 1, :], vb[:, 1, :], start=True, stop=False)
                T.matmul(B[7][:, 0:128], WQ[:, 0, at[1]], S1[:, :], start=False, stop=True)
                T.matmul(B[7][0:T_DEC, 128:256], TU2[:, 1, :], vb[0:T_DEC, 2, :], start=True, stop=False)
                T.matmul(B[7][0:T_DEC, 128:256], wsT[:, 0, :], ident[:, :], start=False, stop=True).then_inc(s["u2_made"], 1)
                T.matmul(B[6][:, at[0]], u[:, 0, :], KQD[:, 0, 1, :], start=True, stop=True)
                if projected:
                    project(h + 2, 3, 3, 6)
                pe.wait_ge(s["u_kept"], 3 * h + 3)
                T.matmul(B[6][:, at[1]], u[:, 1, :], KQD[:, 1, 1, :], start=True, stop=False)
                T.matmul(B[6][:, at[1]], S1[:, :], WQ[:, 1, at[1]], start=False, stop=True)
                T.matmul(B[6][:, at[2]], u[0:T_DEC, 2, :], KQD2[:, 1, :], start=True, stop=False)
                T.matmul(B[6][:, at[2]], ident[:, :], wsT[:, 1, :], start=False, stop=True).then_inc(s["o_made"], 1)
                T.matmul(B[5][:, 0:128], kd[:, 1, :], u[:, 1, :], start=True, stop=True).then_inc(s["S2_made"], 1)
                if projected:
                    project(h + 2, 3, 6, 8)
                pe.wait_ge(s["o2_made"], h + 1)
                T.matmul(B[7][:, 0:T_ALL], ones[:, :], o2[:, :], start=True, stop=True).then_inc(s["osum_made"], 1)
                pe.wait_ge(s["uB_made"], h + 1)
                pe.wait_ge(s["S2_kept"], h + 1)
                for j in range(2):
                    last = T.matmul(B[4 + j][:, :], kd[0:T_DEC, 2, :], uB[:, 4 * j:4 * j + 4, :], start=True, stop=True)
                last.then_inc(s["Sn_made"], 1)

            for j in range(4):
                project(0, j)
            pe.wait_ge(s["st_loaded"], 32)
            conv_rows()
            pe.wait_ge(s["gates_made"], 1)
            for t in range(NT):
                r = rows[t]
                T.matmul(B[2][0:r, 8 * t:8 * t + 8], m["upto"][0:r, at[t]], g[0:r, t, :], start=True, stop=True)
                T.matmul(B[2][0:r, 24 + 8 * t:32 + 8 * t], ones[:, :] if t < 2 else m["dec_same"][0:r, :], g[0:r, t, :], start=True, stop=True)
            T.matmul(B[2][:, 64:128], ones[0:T_DEC, :], decg[:, :, :].rearrange("p b h -> p (b h)"), start=True, stop=True).then_inc(s["sums_made"], 1)
            for j in range(4):
                project(1, j)
            pe.wait_ge(s["rows_kept"], 4)
            pe.wait_ge(s["st_loaded"], 64)
            conv_rows()
            norm_sums(0)
            broadcasts(0)
            chain(0, True, True)
            with pe.Fori(1, H - 2) as h:
                chain(h, True, True)
            chain(H - 2, True, False)
            chain(H - 1, False, False)
            pe.wait_ge(s["wout_in"], 16)
            for t in range(NT):
                for j in range(2):
                    for h in range(H):
                        if t == 0 and j == 0 and h % 2 == 0:
                            pe.wait_ge(s["oz_made"], h // 2 + 1)
                        last = T.matmul((B[2 * t + j] if t < 2 else B[4 + j])[0:rows[t], :], ozT[:, h, at[t]], w_out[:, h, 512 * j:512 * j + 512], start=(h == 0), stop=(h == H - 1))
                    last.then_inc(s["out_made"], 1)

    nc.clear_and_free_semaphores(sems)
    nc.all_engine_barrier(sem_only=True)


LAM_INIT = 0.8 - 0.6 * math.exp(-0.3 * 1)
ROPE_THETA = 10000.0
SCORES = 128 + 256
S_STEPS = 5
P_STEPS = 10


def attn_constants():
    c = {}
    half = DH // 2
    p = np.arange(128)
    pos = np.stack([p, 128 + p, PAST_LEN + p % DEC_SEQ], 1).astype(np.float32)
    inv = (np.float32(ROPE_THETA) ** (-np.arange(half, dtype=np.float32) / np.float32(half))).astype(np.float32)
    ang = pos[:, :, None] * inv
    c["cos"] = np.cos(ang)
    c["sin"] = np.sin(ang)
    causal = np.where(p[None, :] <= p[:, None], 0.0, -FAR)
    c["causal"] = np.concatenate([causal, np.zeros((128, 128)), causal], 1)
    rb, rc, rh, rq = p // 64, (p // 32) % 2, (p // 4) % 8, p % 4
    kb, kq = np.arange(T_DEC) // DEC_SEQ, np.arange(T_DEC) % DEC_SEQ
    pair = np.arange(DEC_BATCH // 2)
    seen = (kb[None, None, :] == 2 * pair[None, :, None] + rb[:, None, None]) & (kq[None, None, :] <= rq[:, None, None])
    c["new_keys"] = np.where(seen, 0.0, -FAR)
    col = np.arange(64)
    c["halves"] = (rb[:, None] == col // 32) & (rh[:, None] == (col // 4) % 8) & (rq[:, None] == col % 4)
    c["first_half"] = rc[:, None] == 0
    c["second_half"] = rc[:, None] == 1
    return c


def attn_phase(nc, m):
    ctx, sems = ExitStack(), []
    with ctx:
        def sb(name, shape, dt=F32):
            return ctx.enter_context(nc.sbuf_tensor(f"at_{name}", shape, dt))

        def sem(name):
            sems.append(nc.alloc_semaphore(f"at_{name}"))
            return sems[-1]

        NT, rows, H = TOK_TILES, TILE_ROWS, HEADS
        at = [slice(128 * t, 128 * t + rows[t]) for t in range(NT)]
        resid, ident, ones = m["resid"], m["ident"], m["ones"]
        ss = sb("ss", [128, NT])
        gains = sb("gains", [128, 2, KT])
        XK = sb("XK", [128, 2, KT, T_ALL])
        kvq = [sb(n, [128, NT, D_MODEL]) for n in ("k", "v", "q")]
        k_t, v_t, q_t = kvq
        rot = sb("rot", [128, 512])
        rot2 = sb("rot2", [128, 512])
        lam_in = sb("lam_in", [128, 4, DH])
        lam = sb("lam", [128, 4])
        coef = sb("coef", [128, 1])
        pages = sb("pages", [1, DEC_BATCH * N_PAGES], I32)
        subln = sb("subln", [128, 1])
        qTd = sb("qTd", [128, H, T_DEC])
        QBs = sb("QBs", [128, 2, H, 64])
        Pu = sb("P", [128, 2, SCORES * 2])
        aTu = sb("aT", [128, 2, 3, 128])
        mxu = sb("mx", [128, 2, 4])
        smu = sb("sm", [128, 2, 4])
        P, aT, mx, sm = Pu[:, 0], aTu[:, 0], mxu[:, 0], smu[:, 0]
        o_ss = sb("o_ss", [128, 2, H])
        oT = sb("oT", [128, H, T_ALL])
        qk_h = XK[:].rearrange("p x k r -> p (x k r)")[:, 0:1024].rearrange("p (u j t e) -> p u j t e", u=2, j=2, t=2)
        qkT = sb("qkT", [128, 2, 2, 256])
        o_t = q_t
        flat = [m["ring"][n][:].rearrange("p a n -> p (a n)") for n in range(3)]
        wslot = [flat[0][:, 0:4096], flat[0][:, 4096:], flat[1][:, 0:4096]]
        wslot = [w.rearrange("p (k n) -> p k n", k=KT) for w in wslot]
        xh = flat[2][:, 0:1024]
        sq = flat[2][:, 1024:2048]
        QB = flat[1][:, 4096:].rearrange("p (b h r) -> p b h r", b=DEC_BATCH, h=H)
        Kc = flat[2][:, 0:4096].rearrange("p (b i n) -> p b i n", b=2, i=N_PAGES)
        Vc = flat[2][:, 4096:].rearrange("p (b i n) -> p b i n", b=2, i=N_PAGES)
        w_out = flat[0].rearrange("p (h n) -> p h n", h=H)
        o_sq = P[:, 0:512]

        BB = [ctx.enter_context(nc.psum_tensor(f"at_pair{i}", [128, 2, 512], F32)) for i in range(2)]
        B = [BB[0][:, 0, :], BB[0][:, 1, :], BB[1][:, 0, :], BB[1][:, 1, :]]
        B += [ctx.enter_context(nc.psum_tensor(f"at_bank{i}", [128, 512], F32)) for i in range(4, 8)]

        s = {n: sem(n) for n in (
            "consts_in w0_in w1_in w2_in squares mean_made roots xh_made xT_made xT_kept lam_in lam_out kv_made kv_kept rotated q_rotated stored "
            "dT_made dT_kept QB_clear QB_made K0_in V0_in KT_made KT_kept QBs_made S_made S_kept S_exp a_made aT_made aT_kept od_made od_kept "
            "rows_kept od_T od_sq od_sum od_root od_done sliced qk_T qkT_kept sc_made sc_kept sc_exp pa_made paT_made paT_kept o_made o_kept on_sq on_root on_made onT_made onT_kept "
            "wout_in out_made out_kept v").split()}
        w_kv = m["w_kv"].rearrange("(p t) n -> p t n", t=KT)
        w_q = m["w_q_b"][0].rearrange("(p t) n -> p t n", t=KT)
        w_src = [w_kv[:, :, 0:D_MODEL], w_kv[:, :, D_MODEL:], w_q]
        slot_in = [s["w0_in"], s["w1_in"], s["w2_in"]]
        outs = [(m["k_prompt"][0].rearrange("l h e -> l (h e)"), m["k_sample"].rearrange("b l h e -> (b l) (h e)")),
                (m["v_prompt"][0].rearrange("l h e -> l (h e)"), m["v_sample"].rearrange("b l h e -> (b l) (h e)"))]
        caches = [m["cache_k"].rearrange("n s h e -> s n (h e)"), m["cache_v"].rearrange("n s h e -> s n (h e)")]
        PAIRS = DEC_BATCH // 2

        def kbank(t):
            return (B[0], B[1], B[2])[t]

        def vbank(t):
            return (B[3], B[4], B[5])[t]

        def qbank(t):
            return (B[6], B[7], B[0])[t]

        def later(step):
            return not (isinstance(step, int) and step == 0)

        block = ctx.enter_context(nc.Block())

        @block.sync
        def _(sp):
            sp.dma_start(gains[:, 0, :], m["kv_norm"].rearrange("(p t) -> p t", t=KT)).then_inc(s["consts_in"], 16)
            sp.dma_start(gains[:, 1, :], m["norm_b"][0].rearrange("(p t) -> p t", t=KT)).then_inc(s["consts_in"], 16)
            sp.dma_start(lam_in[:].rearrange("p a d -> p (a d)"), m["lam_b"].rearrange("a l d -> a (l d)").broadcast_to([128, 4 * DH])).then_inc(s["consts_in"], 16)
            sp.dma_start(subln[:], m["subln_b"].rearrange("a v -> v a")).then_inc(s["consts_in"], 16)
            sp.dma_start(pages[:], m["page_table"].rearrange("(a b) i -> a (b i)", a=1)).then_inc(s["consts_in"], 16)

            def weights(half, first=False):
                for j in range(3):
                    if not first:
                        sp.wait_ge(s["kv_made"], 9 * half - 6 + 3 * j)
                    sp.dma_start(wslot[j], w_src[j][:, :, 512 * half:512 * half + 512]).then_inc(slot_in[j], 16)

            weights(0, True)
            weights(1)
            for j in range(2):
                for t in range(NT):
                    sp.wait_ge((s["rotated"], s["kv_kept"])[j], 6)
                    dst = outs[j][0][at[t], :] if t < 2 else outs[j][1]
                    sp.dma_start(dst, kvq[j][0:rows[t], t, :]).then_inc(s["stored"], 16)

            def cache(j, pair, later):
                for b in range(2):
                    for i in range(N_PAGES):
                        page = sp.value_load(pages[0:1, bass.ds(4 * pair + 2 * b + i, 1)], min_val=0, max_val=N_PHYS - 1)
                        if later and b == 0 and i == 0:
                            if j == 0:
                                sp.wait_ge(s["KT_made"], 8 * pair)
                            else:
                                sp.wait_ge(s["od_made"], pair)
                        dst = (Kc, Vc)[j][:, b, i, :]
                        sp.dma_start(dst, caches[j][:, bass.ds(page, 1), :].rearrange("s o n -> s (o n)")).then_inc((s["K0_in"], s["V0_in"])[j], 16)

            sp.wait_ge(s["consts_in"], 16 * 5)
            sp.wait_ge(s["xT_made"], 2 * NT)
            cache(0, 0, False)
            cache(1, 0, False)
            with sp.Fori(1, PAIRS) as pair:
                cache(0, pair, True)
                cache(1, pair, True)
            sp.wait_ge(s["kv_made"], 18)
            sp.dma_start(w_out, m["w_out_b"][0].rearrange("(h p) n -> p h n", p=128)).then_inc(s["wout_in"], 16)
            sp.wait_ge(s["QBs_made"], PAIRS)
            m["prefetch"](sp, 1, (1,))
            sp.wait_ge(s["od_made"], PAIRS)
            m["prefetch"](sp, 1, (2,))
            sp.wait_ge(s["stored"], 16 * 2 * NT)
            sp.wait_ge(s["out_made"], 2 * NT)
            m["prefetch"](sp, 1, (0,))

        @block.gpsimd
        def _(pool):
            nc.gpsimd.memset(QB[:, :, :, :], 0.0).then_inc(s["QB_clear"], 1)
            pool.wait_ge(s["QB_made"], 2 * H)

            def queries(pair):
                if later(pair):
                    pool.wait_ge(s["S_made"], pair)
                nc.gpsimd.tensor_copy(QBs[:, :, :, :], QB[:, bass.ds(2 * pair, 2), :, :]).then_inc(s["QBs_made"], 1)

            queries(0)
            with pool.Fori(1, PAIRS) as pair:
                queries(pair)

            def cut(i, u):
                h = 2 * i + u
                if later(i):
                    pool.wait_ge(s["qk_T"], h - 1)
                e = bass.ds(256 * i + 128 * u, 128)
                nc.gpsimd.tensor_copy(qk_h[:, u, 0, :, :], q_t[:, 0:2, e]).then_inc(s["sliced"], 1)
                nc.gpsimd.tensor_copy(qk_h[:, u, 1, :, :], k_t[:, 0:2, e]).then_inc(s["sliced"], 1)

            pool.wait_ge(s["S_made"], PAIRS)
            for u in range(2):
                cut(0, u)
            with pool.Fori(1, H // 2) as i:
                for u in range(2):
                    cut(i, u)

        @block.scalar
        def _(act):
            A = nc.scalar
            act.wait_ge(s["squares"], 1)
            for t in range(NT):
                r = rows[t]
                A.activation(sq[0:r, :], resid[0:r, t, :], ACT.Square, accum_out=ss[0:r, t:t + 1]).then_inc(s["squares"], 1)
                act.wait_ge(s["squares"], t + 2)
            act.wait_ge(s["mean_made"], 1)
            A.activation(ss[:, :], ss[:, :], ACT.Sqrt).then_inc(s["roots"], 1)
            act.wait_ge(s["lam_in"], 1)
            A.activation(lam[:, 0:2], lam[:, 0:2], ACT.Exp).then_inc(s["lam_out"], 1)
            for half in range(2):
                for t in range(NT):
                    act.wait_ge(s["kv_made"], 9 * half + 3 + t + 1)
                    A.copy(v_t[0:rows[t], t, 512 * half:512 * half + 512], vbank(t)[0:rows[t], :]).then_inc(s["kv_kept"], 1)
            act.wait_ge(s["dT_made"], 1)
            A.copy(qTd[:, :, :], B[4][:, 0:256].rearrange("p (h r) -> p h r", h=H)).then_inc(s["dT_kept"], 1)
            for b in range(2):
                A.copy(XK[:, b, :, PAST_LEN:], B[5][:, 0:256].rearrange("p (h r) -> p h r", h=H)).then_inc(s["dT_kept"], 1)
            def samples(pair):
                for b in range(2):
                    for j in (1, 3):
                        act.wait_ge(s["KT_made"], 8 * pair + 4 * b + j + 1)
                        if later(pair) and b == 0 and j == 1:
                            act.wait_ge(s["S_made"], pair)
                        A.copy(XK[:, b, 2 * j:2 * j + 2, 0:PAST_LEN], B[4 + j][:, :].rearrange("p (h r) -> p h r", h=2)).then_inc(s["KT_kept"], 1)
                act.wait_ge(s["S_kept"], pair + 1)
                A.activation(P[:, 0:T_ALL], P[:, 0:T_ALL], ACT.Exp, bias=mx[:, 1:2], scale=DH ** -0.5, accum_out=sm[:, 0:1]).then_inc(s["S_exp"], 1)

            samples(0)
            with act.Fori(1, PAIRS) as pair:
                samples(pair)
            act.wait_ge(s["od_sum"], 1)
            A.activation(rot[:, 0:256], B[0][:, 0:256], ACT.Sqrt, scale=1.0 / DK, bias=m["eps"][:, 0:1]).then_inc(s["od_root"], 1)

            def turned(i, u):
                act.wait_ge(s["qk_T"], 2 * i + u + 1)
                A.copy(qkT[:, u, 0, :], B[4 + u][:, 0:256]).then_inc(s["qkT_kept"], 1)
                A.copy(qkT[:, u, 1, :], B[4 + u][:, 256:512]).then_inc(s["qkT_kept"], 1)

            def heads(i, more):
                for u in range(2):
                    act.wait_ge(s["sc_kept"], 2 * i + u + 1)
                    for t in range(2):
                        for c in range(2):
                            lo = SCORES * c + 128 * t
                            n = 128 * (t + 1)
                            A.activation(Pu[:, u, lo:lo + n], Pu[:, u, lo:lo + n], ACT.Exp, bias=mxu[:, u, 2 * t + c:2 * t + c + 1],
                                         scale=DH ** -0.5, accum_out=smu[:, u, 2 * t + c:2 * t + c + 1]).then_inc(s["sc_exp"], 1)
                if more:
                    for u in range(2):
                        turned(i + 1, u)
                for u in range(2):
                    act.wait_ge(s["paT_made"], 2 * i + u + 1)
                    A.copy(aTu[:, u, :, :], B[6 + u][:, 0:384].rearrange("p (j r) -> p j r", j=3)).then_inc(s["paT_kept"], 1)
                for u in range(2):
                    act.wait_ge(s["o_made"], 2 * i + u + 1)
                    A.copy(o_t[:, 0:2, bass.ds(256 * i + 128 * u, 128)], B[4 + u][:, 0:256].rearrange("p (t e) -> p t e", t=2)).then_inc(s["o_kept"], 1)

            for u in range(2):
                turned(0, u)
            heads(0, True)
            with act.Fori(1, H // 2 - 1) as i:
                heads(i, True)
            heads(H // 2 - 1, False)
            act.wait_ge(s["on_sq"], 1)
            A.activation(o_ss[:, :, :], o_ss[:, :, :], ACT.Sqrt, scale=1.0 / DK, bias=m["eps"][:, 0:1]).then_inc(s["on_root"], 1)
            for t in range(2):
                for j in range(2):
                    act.wait_ge(s["onT_made"], 2 * t + j + 1)
                    A.activation(oT[:, 4 * j:4 * j + 4, at[t]], B[2 * t + j][:, :].rearrange("p (h r) -> p h r", h=4), ACT.Copy, scale=subln[:, 0:1]).then_inc(s["onT_kept"], 1)

        @block.vector
        def _(dve):
            V = nc.vector
            st = {"base": 0, "n": 0}

            def link(ins):
                st["n"] += 1
                ins.then_inc(s["v"], 1)
                dve.wait_ge(s["v"], st["base"] + st["n"])

            V.memset(ss[:], 1.0).then_inc(s["squares"], 1)
            dve.wait_ge(s["consts_in"], 16 * 5)
            for j in range(2):
                link(V.tensor_tensor(lam_in[:, 2 * j, :], lam_in[:, 2 * j, :], lam_in[:, 2 * j + 1, :], ALU.mult))
                ins = V.tensor_reduce(lam[:, j:j + 1], lam_in[:, 2 * j, :], AX.X, ALU.add)
                ins.then_inc(s["lam_in"], 1) if j else link(ins)
            dve.wait_ge(s["squares"], NT + 1)
            V.tensor_scalar(ss[:, :], ss[:, :], 1.0 / D_MODEL, EPS, ALU.mult, ALU.add).then_inc(s["mean_made"], 1)
            dve.wait_ge(s["roots"], 1)
            link(V.reciprocal(ss[:, :], ss[:, :]))
            for t in range(NT):
                r = rows[t]
                if t:
                    dve.wait_ge(s["xT_made"], 2 * t)
                V.tensor_scalar(xh[0:r, :], resid[0:r, t, :], ss[0:r, t:t + 1], None, ALU.mult).then_inc(s["xh_made"], 1)
                for j in range(2):
                    dve.wait_ge(s["xT_made"], 2 * t + j + 1)
                    for x in range(2):
                        V.tensor_tensor(XK[:, x, 4 * j:4 * j + 4, at[t]], B[j][:, :].rearrange("p (k r) -> p k r", k=4)[:, :, 0:r],
                                        gains[:, x, 4 * j:4 * j + 4].unsqueeze(2).broadcast_to([128, 4, r]), ALU.mult).then_inc(s["xT_kept"], 1)
            dve.wait_ge(s["lam_out"], 1)
            link(V.tensor_tensor(lam[:, 2:3], lam[:, 1:2], lam[:, 0:1], ALU.subtract))
            link(V.tensor_scalar(lam[:, 2:3], lam[:, 2:3], -LAM_INIT, None, ALU.add))
            link(V.scalar_tensor_tensor(coef[:, :], m["second_half"][:, :], lam[:, 2:3], m["first_half"][:, :], ALU.mult, ALU.add))
            link(V.tensor_scalar(subln[:, :], subln[:, :], 1.0 - LAM_INIT, None, ALU.mult))

            def rotate(half, dst, bank, t):
                r = rows[t]
                G = 512 // DH
                x = bank[0:r, :].rearrange("p (g a d) -> p g a d", g=G, a=2)
                c, sn = (a[0:r, t, :].unsqueeze(1).broadcast_to([r, G, DH // 2]) for a in (m["cos"], m["sin"]))
                y = rot[0:r, :].rearrange("p (g a d) -> p g a d", g=G, a=2)
                z = rot2[0:r, :].rearrange("p (g a d) -> p g a d", g=G, a=2)
                o = dst[0:r, t, 512 * half:512 * half + 512].rearrange("p (g a d) -> p g a d", g=G, a=2)
                for a in range(2):
                    V.tensor_tensor(y[:, :, a, :], x[:, :, a, :], c, ALU.mult)
                    last = V.tensor_tensor(z[:, :, a, :], x[:, :, 1 - a, :], sn, ALU.mult)
                    if a:
                        link(last)
                V.tensor_tensor(o[:, :, 0, :], y[:, :, 0, :], z[:, :, 0, :], ALU.subtract)
                V.tensor_tensor(o[:, :, 1, :], y[:, :, 1, :], z[:, :, 1, :], ALU.add).then_inc(s["rotated"] if dst is k_t else s["q_rotated"], 1)

            for half in range(2):
                for j, (dst, bank, done) in enumerate(((k_t, kbank, s["rotated"]), (q_t, qbank, s["q_rotated"]))):
                    for t in range(NT):
                        dve.wait_ge(s["kv_made"], 9 * half + 6 * j + t + 1)
                        rotate(half, dst, bank(t), t)
                        dve.wait_ge(done, 3 * half + t + 1)
            dve.wait_ge(s["dT_kept"], 3)
            dve.wait_ge(s["QB_clear"], 1)
            for c in range(2):
                for h in range(H):
                    V.tensor_copy(QB[64 * c:64 * c + 64, :, h, 32 * c + 4 * h:32 * c + 4 * h + 4],
                                  qTd[64 * c:64 * c + 64, h, :].rearrange("p (b q) -> p b q", q=DEC_SEQ)).then_inc(s["QB_made"], 1)
            pre = st["n"]

            def samples(pair):
                for b in range(2):
                    for j in (0, 2):
                        dve.wait_ge(s["KT_made"], 8 * pair + 4 * b + j + 1)
                        if later(pair) and b == 0 and j == 0:
                            dve.wait_ge(s["S_made"], pair)
                        V.tensor_copy(XK[:, b, 2 * j:2 * j + 2, 0:PAST_LEN], B[4 + j][:, :].rearrange("p (h r) -> p h r", h=2)).then_inc(s["KT_kept"], 1)
                dve.wait_ge(s["S_made"], pair + 1)
                if later(pair):
                    dve.wait_ge(s["aT_made"], pair)
                link(V.tensor_copy(P[:, 0:PAST_LEN], B[0][:, 0:PAST_LEN]))
                link(V.tensor_tensor(P[:, PAST_LEN:T_ALL], B[0][:, PAST_LEN:T_ALL], m["new_keys"][:, bass.ds(pair, 1), :].rearrange("p o k -> p (o k)"), ALU.add))
                link(V.tensor_reduce(mx[:, 0:1], P[:, 0:T_ALL], AX.X, ALU.max))
                V.tensor_scalar(mx[:, 1:2], mx[:, 0:1], -(DH ** -0.5), None, ALU.mult).then_inc(s["S_kept"], 1)
                dve.wait_ge(s["S_exp"], pair + 1)
                link(V.reciprocal(sm[:, 1:2], sm[:, 0:1]))
                link(V.tensor_tensor(sm[:, 1:2], sm[:, 1:2], coef[:, :], ALU.mult))
                V.tensor_scalar(P[:, 0:T_ALL], P[:, 0:T_ALL], sm[:, 1:2], None, ALU.mult).then_inc(s["a_made"], 1)
                dve.wait_ge(s["aT_made"], pair + 1)
                if later(pair):
                    dve.wait_ge(s["od_made"], pair)
                V.tensor_copy(aT[:, 0:2, 0:64], B[1][:, 0:128].rearrange("p (i r) -> p i r", i=2)).then_inc(s["aT_kept"], 1)
                V.tensor_copy(aT[0:T_DEC, 2, 0:64], B[1][0:T_DEC, 128:192]).then_inc(s["aT_kept"], 1)
                dve.wait_ge(s["od_made"], pair + 1)
                V.tensor_copy(rot[:, :], B[2][:, :]).then_inc(s["rows_kept"], 1)
                dve.wait_ge(s["od_T"], pair + 1)
                for b in range(2):
                    own = (B[3][:, 0:36 * H], B[3][:, 512 - 36 * H:])[b].rearrange("p (h r) -> p h r", h=H)[:, :, (0, 32)[b]:(0, 32)[b] + DEC_SEQ]
                    V.tensor_copy(oT[:, :, bass.ds(8 * pair + (SEQ + DEC_SEQ * b), DEC_SEQ)], own).then_inc(s["od_kept"], 1)

            samples(0)
            assert st["n"] == pre + S_STEPS, st["n"]
            with dve.Fori(1, PAIRS) as pair:
                st["base"], st["n"] = pair * S_STEPS + pre, 0
                samples(pair)
                assert st["n"] == S_STEPS, st["n"]
            st["base"], st["n"] = PAIRS * S_STEPS + pre, 0
            dve.wait_ge(s["od_kept"], 2 * PAIRS)
            V.tensor_tensor(rot2[:, 0:256].rearrange("p (h r) -> p h r", h=H), oT[:, :, SEQ:], oT[:, :, SEQ:], ALU.mult).then_inc(s["od_sq"], 1)
            dve.wait_ge(s["od_root"], 1)
            link(V.reciprocal(rot[:, 0:256], rot[:, 0:256]))
            link(V.scalar_tensor_tensor(oT[:, :, SEQ:], rot[:, 0:256].rearrange("p (h r) -> p h r", h=H), subln[:, 0:1], oT[:, :, SEQ:], ALU.mult, ALU.mult))
            pre = PAIRS * S_STEPS + pre + st["n"]

            def scores(i, u):
                dve.wait_ge(s["sc_made"], 2 * i + u + 1)
                if later(i):
                    dve.wait_ge(s["paT_made"], 2 * i + u - 1)
                v = Pu[:, u, :].rearrange("p (c n) -> p c n", c=2)
                link(V.tensor_tensor(v, BB[u][:, :, 0:SCORES], m["causal"][:, :].unsqueeze(1).broadcast_to([128, 2, SCORES]), ALU.add))
                V.tensor_reduce(mxu[:, u, 0:2], v[:, :, 0:128], AX.X, ALU.max)
                link(V.tensor_reduce(mxu[:, u, 2:4], v[:, :, 128:384], AX.X, ALU.max))
                V.tensor_scalar(mxu[:, u, :], mxu[:, u, :], -(DH ** -0.5), None, ALU.mult).then_inc(s["sc_kept"], 1)

            def weights(i, u):
                dve.wait_ge(s["sc_exp"], 8 * i + 4 * u + 4)
                link(V.reciprocal(smu[:, u, :], smu[:, u, :]))
                for t in range(2):
                    last = V.tensor_scalar(smu[:, u, 2 * t + 1:2 * t + 2], smu[:, u, 2 * t + 1:2 * t + 2], lam[:, 2:3], None, ALU.mult)
                link(last)
                parts = [(Pu[:, u, 128 * t:128 * t + 128 * (t + 1)], Pu[:, u, SCORES + 128 * t:SCORES + 128 * t + 128 * (t + 1)]) for t in range(2)]
                for t in range(2):
                    last = V.tensor_scalar(parts[t][1], parts[t][1], smu[:, u, 2 * t + 1:2 * t + 2], None, ALU.mult)
                link(last)
                for t in range(2):
                    last = V.scalar_tensor_tensor(parts[t][0], parts[t][0], smu[:, u, 2 * t:2 * t + 1], parts[t][1], ALU.mult, ALU.add)
                last.then_inc(s["pa_made"], 1)

            def heads(i):
                for u in range(2):
                    scores(i, u)
                for u in range(2):
                    weights(i, u)

            st["base"], st["n"] = pre, 0
            heads(0)
            with dve.Fori(1, H // 2 - 1) as i:
                st["base"], st["n"] = i * P_STEPS + pre, 0
                heads(i)
                assert st["n"] == P_STEPS, st["n"]
            st["base"], st["n"] = (H // 2 - 1) * P_STEPS + pre, 0
            heads(H // 2 - 1)
            dve.wait_ge(s["o_kept"], H)
            for t in range(2):
                for j in range(2):
                    v = o_t[:, t, 512 * j:512 * j + 512]
                    link(V.tensor_tensor(o_sq, v, v, ALU.mult))
                    ins = V.tensor_reduce(o_ss[:, t, 4 * j:4 * j + 4], o_sq.rearrange("p (h e) -> p h e", h=4), AX.X, ALU.add)
                    ins.then_inc(s["on_sq"], 1) if t and j else link(ins)
            dve.wait_ge(s["on_root"], 1)
            link(V.reciprocal(o_ss[:], o_ss[:]))
            for t in range(2):
                v = o_t[:, t, :].rearrange("p (h e) -> p h e", h=H)
                V.tensor_tensor(v, v, o_ss[:, t, :].unsqueeze(2).broadcast_to([128, H, 128]), ALU.mult).then_inc(s["on_made"], 1)
            for t in range(NT):
                r = rows[t]
                for j in range(2):
                    dve.wait_ge(s["out_made"], 2 * t + j + 1)
                    V.tensor_tensor(resid[0:r, t, 512 * j:512 * j + 512], resid[0:r, t, 512 * j:512 * j + 512], B[4 + j][0:r, :], ALU.add).then_inc(s["out_kept"], 1)
            dve.wait_ge(s["out_kept"], 2 * NT)

        @block.tensor
        def _(pe):
            T = nc.tensor
            xv = xh.rearrange("p (c k) -> p k c", k=KT)
            for t in range(NT):
                r = rows[t]
                pe.wait_ge(s["xh_made"], t + 1)
                if t:
                    pe.wait_ge(s["xT_kept"], 4 * t)
                for k in range(KT):
                    last = T.transpose(B[k // 4][:, 128 * (k % 4):128 * (k % 4) + r], xv[0:r, k, :], ident[0:r, 0:r])
                    if k % 4 == 3:
                        last.then_inc(s["xT_made"], 1)
            pe.wait_ge(s["xT_kept"], 4 * NT)
            for half in range(2):
                for j in range(3):
                    pe.wait_ge(slot_in[j], 16 * half + 16)
                    for t in range(NT):
                        if half:
                            if j == 0:
                                pe.wait_ge(s["q_rotated"] if t == 0 else s["rotated"], 3)
                            elif j == 1:
                                pe.wait_ge(s["kv_kept"], t + 1)
                            else:
                                pe.wait_ge(s["q_rotated"], 3)
                        if j == 2 and t == 2:
                            pe.wait_ge(s["rotated"], 3 * half + 1)
                        bank = (kbank, vbank, qbank)[j](t)
                        for k in range(KT):
                            last = T.matmul(bank[0:rows[t], :], XK[:, 0 if j < 2 else 1, k, at[t]], wslot[j][:, k, :], start=(k == 0), stop=(k == KT - 1))
                        last.then_inc(s["kv_made"], 1)
            pe.wait_ge(s["q_rotated"], 6)
            pe.wait_ge(s["rotated"], 6)
            pe.wait_ge(s["kv_kept"], 6)
            for j, src in ((4, q_t), (5, k_t)):
                for h in range(H):
                    last = T.transpose(B[j][:, 32 * h:32 * h + 32], src[0:T_DEC, 2, 128 * h:128 * h + 128], ident[0:T_DEC, 0:T_DEC])
            last.then_inc(s["dT_made"], 1)
            pe.wait_ge(s["dT_kept"], 3)

            def samples(pair):
                pe.wait_ge(s["K0_in"], 64 * pair + 64)
                for b in range(2):
                    for j in range(4):
                        if b == 0 and later(pair):
                            pe.wait_ge(s["KT_kept"], 8 * pair)
                        elif b and j == 0:
                            pe.wait_ge(s["KT_kept"], 8 * pair + 4)
                        for h in range(2):
                            for i in range(N_PAGES):
                                last = T.transpose(B[4 + j][:, 256 * h + 128 * i:256 * h + 128 * i + 128],
                                                   Kc[:, b, i, 128 * (2 * j + h):128 * (2 * j + h) + 128], ident[:, :])
                        last.then_inc(s["KT_made"], 1)
                pe.wait_ge(s["KT_kept"], 8 * pair + 8)
                if later(pair):
                    pe.wait_ge(s["S_kept"], pair)
                pe.wait_ge(s["QBs_made"], pair + 1)
                for h in range(H):
                    for b in range(2):
                        last = T.matmul(B[0][64 * b:64 * b + 64, 0:T_ALL], QBs[:, b, h, :], XK[:, b, h, :], start=(h == 0), stop=(h == H - 1))
                last.then_inc(s["S_made"], 1)
                pe.wait_ge(s["a_made"], pair + 1)
                T.matmul(B[1][:, 0:64], P[:, 0:128], m["halves"][:, :], start=True, stop=True)
                T.matmul(B[1][:, 64:128], P[:, 128:256], m["halves"][:, :], start=True, stop=True)
                T.matmul(B[1][0:T_DEC, 128:192], P[:, 256:T_ALL], m["halves"][:, :], start=True, stop=True).then_inc(s["aT_made"], 1)
                pe.wait_ge(s["aT_kept"], 2 * pair + 2)
                pe.wait_ge(s["V0_in"], 64 * pair + 64)
                for b in range(2):
                    for f in range(2):
                        for i in range(N_PAGES + 1):
                            for h in range(4 * f, 4 * f + 4):
                                values = Vc[:, b, i, 128 * h:128 * h + 128] if i < N_PAGES else v_t[0:T_DEC, 2, 128 * h:128 * h + 128]
                                weights = aT[:, i, 32 * b:32 * b + 32] if i < N_PAGES else aT[0:T_DEC, 2, 32 * b:32 * b + 32]
                                lane = 32 * (h % 4)
                                last = T.matmul(B[2][lane:lane + 32, 256 * b + 128 * f:256 * b + 128 * f + 128], weights, values,
                                                start=(i == 0), stop=(i == N_PAGES), tile_position=(0, lane))
                last.then_inc(s["od_made"], 1)
                pe.wait_ge(s["rows_kept"], pair + 1)
                if later(pair):
                    pe.wait_ge(s["od_kept"], 2 * pair)
                for j in range(4):
                    last = T.transpose(B[3][:, 128 * j:128 * j + 128], rot[:, 128 * j:128 * j + 128], ident[:, :])
                last.then_inc(s["od_T"], 1)

            samples(0)
            with pe.Fori(1, PAIRS) as pair:
                samples(pair)
            pe.wait_ge(s["od_sq"], 1)
            T.matmul(B[0][:, 0:256], ones[:, :], rot2[:, 0:256], start=True, stop=True).then_inc(s["od_sum"], 1)

            def turn(i, u):
                h = 2 * i + u
                pe.wait_ge(s["sliced"], 2 * h + 2)
                if later(i):
                    pe.wait_ge(s["qkT_kept"], 2 * h - 2)
                    if not (isinstance(i, int) and i == 1):
                        pe.wait_ge(s["o_kept"], h - 3)
                for j in range(2):
                    for t in range(2):
                        last = T.transpose(B[4 + u][:, 256 * j + 128 * t:256 * j + 128 * t + 128], qk_h[:, u, j, t, :], ident[:, :])
                last.then_inc(s["qk_T"], 1)

            def heads(i, more, following):
                for u in range(2):
                    h = 2 * i + u
                    pe.wait_ge(s["qkT_kept"], 2 * h + 2)
                    if later(i):
                        pe.wait_ge(s["sc_kept"], h - 1)
                    for t in range(2):
                        for c in range(2):
                            lane = slice(64 * c, 64 * c + 64)
                            last = T.matmul(BB[u][:, c, 128 * t:128 * t + 128 * (t + 1)], qkT[lane, u, 0, 128 * t:128 * t + 128], qkT[lane, u, 1, 0:128 * (t + 1)],
                                            start=True, stop=True)
                    last.then_inc(s["sc_made"], 1)
                if more:
                    for u in range(2):
                        turn(following, u)
                for u in range(2):
                    h = 2 * i + u
                    pe.wait_ge(s["pa_made"], h + 1)
                    if later(i):
                        pe.wait_ge(s["paT_kept"], h - 1)
                    for j, lo in enumerate((0, 128, 256)):
                        last = T.transpose(B[6 + u][:, 128 * j:128 * j + 128], Pu[:, u, lo:lo + 128], ident[:, :])
                    last.then_inc(s["paT_made"], 1)
                for u in range(2):
                    h = 2 * i + u
                    pe.wait_ge(s["paT_kept"], h + 1)
                    if more:
                        pe.wait_ge(s["qkT_kept"], 2 * h + 6)
                    if later(i):
                        pe.wait_ge(s["o_kept"], h - 1)
                    e = bass.ds(256 * i + 128 * u, 128)
                    out = B[4 + u]
                    T.matmul(out[:, 0:128], aTu[:, u, 0, :], v_t[:, 0, e], start=True, stop=True)
                    T.matmul(out[:, 128:256], aTu[:, u, 1, :], v_t[:, 0, e], start=True, stop=False)
                    T.matmul(out[:, 128:256], aTu[:, u, 2, :], v_t[:, 1, e], start=False, stop=True).then_inc(s["o_made"], 1)

            for u in range(2):
                turn(0, u)
            heads(0, True, 1)
            with pe.Fori(1, H // 2 - 1) as i:
                heads(i, True, i + 1)
            heads(H // 2 - 1, False, None)
            for t in range(2):
                pe.wait_ge(s["on_made"], t + 1)
                for j in range(2):
                    for h in range(4):
                        last = T.transpose(B[2 * t + j][:, 128 * h:128 * h + 128], o_t[:, t, 128 * (4 * j + h):128 * (4 * j + h) + 128], ident[:, :])
                    last.then_inc(s["onT_made"], 1)
            pe.wait_ge(s["onT_kept"], 4)
            pe.wait_ge(s["wout_in"], 16)
            for t in range(NT):
                if t:
                    pe.wait_ge(s["out_kept"], 2 * t)
                for j in range(2):
                    for h in range(H):
                        last = T.matmul(B[4 + j][0:rows[t], :], oT[:, h, at[t]], w_out[:, h, 512 * j:512 * j + 512], start=(h == 0), stop=(h == H - 1))
                    last.then_inc(s["out_made"], 1)

    nc.clear_and_free_semaphores(sems)
    nc.all_engine_barrier(sem_only=True)


def moe_phase(nc, m, layer):
    ctx, sems = ExitStack(), []
    with ctx:
        def sb(name, shape, dt=F32):
            return ctx.enter_context(nc.sbuf_tensor(f"moe{layer}_{name}", shape, dt))

        def pb(name, shape, dt=F32):
            return ctx.enter_context(nc.psum_tensor(f"moe{layer}_{name}", shape, dt))

        def sem(name):
            sems.append(nc.alloc_semaphore(f"moe{layer}_{name}"))
            return sems[-1]

        NT = TOK_TILES
        rows = TILE_ROWS
        resid, ident = m["resid"], m["ident"]
        norm_b = sb("norm_b", [128, D_MODEL])
        w_router = sb("w_router", [128, KT, N_GROUPS + N_EXPERTS])
        b_router = sb("b_router", [128, N_GROUPS + N_EXPERTS])
        xn = sb("xn", [128, NT, D_MODEL])
        xnT = sb("xnT", [128, KT, T_ALL])
        logT = sb("logT", [N_GROUPS + N_EXPERTS, T_ALL])
        logits = sb("logits", [128, NT, N_GROUPS + N_EXPERTS])
        sq = sb("sq", [128, D_MODEL])
        ss = sb("ss", [128, NT])
        rstd = sb("rstd", [128, NT])
        gmax = sb("gmax", [128, NT])
        gexp = sb("gexp", [128, NT, N_GROUPS])
        gsum = sb("gsum", [128, NT])
        gpick = sb("gpick", [128, NT, N_GROUPS])
        gbest = sb("gbest", [128, NT])
        masked = sb("masked", [128, NT, N_EXPERTS])
        etmp = sb("etmp", [128, NT, N_EXPERTS])
        ktmp = sb("ktmp", [128, TOP_K, NT, N_EXPERTS])
        ctmp = sb("ctmp", [128, TOP_K, NT, N_EXPERTS])
        rkm = sb("rkm", [128, TOP_K, NT])
        spare = sb("spare", [128, TOP_K, NT])
        ebest = sb("ebest", [128, NT])
        top = sb("top", [128, TOP_K, NT])
        oneh = sb("oneh", [128, TOP_K, NT, N_EXPERTS])
        both = sb("both", [128, NT, N_EXPERTS])
        gate = sb("gate", [128, TOP_K, NT])
        ratio = sb("ratio", [128, NT])
        rank = sb("rank", [128, NT, N_EXPERTS])
        counts = sb("counts", [128, N_EXPERTS])
        nover = sb("nover", [128, N_EXPERTS])
        cend = sb("cend", [128, N_EXPERTS])
        cstart = sb("cstart", [128, N_EXPERTS])
        rk = sb("rk", [128, TOP_K, NT])
        inmain = sb("inmain", [128, TOP_K, NT])
        lmain = sb("lmain", [128, TOP_K, NT])
        opos = sb("opos", [128, TOP_K, NT])
        oge = sb("oge", [128, TOP_K, NT, OVER_GROUPS + 1])
        olow = sb("olow", [128, TOP_K, NT])
        lpos = sb("lpos", [128, TOP_K, NT])
        colhot = sb("colhot", [128, TOP_K, NT, N_COLS])
        entry = sb("entry", [128, TOP_K, NT, 2, N_COLS])
        place = sb("place", [128, TOP_K, NT, 128])
        tabf = sb("tabf", [128, 2, N_COLS])
        tabz = sb("tabz", [128, 2, N_COLS])
        table = sb("table", [128, 2, N_COLS], U32)
        obf = sb("obf", [1, 2 * OVER_GROUPS, N_EXPERTS])
        obf2 = sb("obf2", [1, 2 * OVER_GROUPS, N_EXPERTS])
        ovalf = sb("ovalf", [1, 2 * OVER_GROUPS + 2])
        ngf = sb("ngf", [1, 4])
        steer = sb("steer", [1, 2 * OVER_GROUPS + 2], I32)
        xg = sb("xg", [128, D_MODEL])
        xgT = sb("xgT", [128, KT, 128])
        silu = sb("silu", [128, D_FF_EXPERT])
        hid = sb("hid", [128, D_FF_EXPERT])
        hidT = sb("hidT", [128, FT, 128])
        y_sb = sb("y_sb", [128, D_MODEL])
        rows_in = sb("rows_in", [128, 1], U32)
        rows_out = sb("rows_out", [128, 1], U32)

        ps_x = pb("ps_x", [128, 2, 4, 128])
        ps_gate = pb("ps_gate", [128, D_FF_EXPERT])
        ps_up = pb("ps_up", [128, D_FF_EXPERT])
        ps_hid = pb("ps_hid", [128, FT, 128])
        ps_y = pb("ps_y", [128, 2, 512])
        ps_rank = ps_gate[:, 0:NT * N_EXPERTS].rearrange("p (a e) -> p a e", a=NT)
        ps_count = ps_gate[:, NT * N_EXPERTS:NT * N_EXPERTS + N_EXPERTS]
        ps_tab = ps_up[:, 0:2 * N_COLS]
        at = [slice(128 * t, 128 * t + rows[t]) for t in range(NT)]
        ps_xT = [ps_x, ps_y[:].rearrange("p a (k r) -> p a k r", k=4), ps_x]
        ps_logT = [ps_gate, ps_up, ps_gate]
        ps_log = ps_hid[:, 0:NT, 0:N_GROUPS + N_EXPERTS]

        consts_in = sem("consts_in")
        squares = sem("squares")
        roots = sem("roots")
        normed = sem("normed")
        xn_stored = sem("xn_stored")
        xT_made = sem("xT_made")
        xT_kept = sem("xT_kept")
        logT_made = sem("logT_made")
        logT_kept = sem("logT_kept")
        logits_made = sem("logits_made")
        logits_kept = sem("logits_kept")
        gdiff = sem("gdiff")
        gexped = sem("gexped")
        tdiff = sem("tdiff")
        texped = sem("texped")
        hots = sem("hots")
        ranked = sem("ranked")
        placed = sem("placed")
        tabbed = sem("tabbed")
        table_ready = sem("table_ready")
        vchain = sem("vchain")
        cleared = sem("cleared")
        weights_in = m["weights_of"][layer]
        weights_used = [sem(f"{n}_products") for n in ("gate", "up", "down")]
        gate_made, up_made, y_made = weights_used
        gathered = sem("gathered")
        gx_T = sem("gx_T")
        gx_kept = sem("gx_kept")
        silued = sem("silued")
        hidden = sem("hidden")
        hid_T = sem("hid_T")
        hid_kept = sem("hid_kept")
        y_kept = sem("y_kept")
        scattered = sem("scattered")
        y_back = [sem(f"y_back{t}") for t in range(NT)]
        scattered_all = sem("scattered_all")
        mean_made = sem("mean_made")
        ss_cleared = sem("ss_cleared")
        waits_held = sem("waits_held")
        in_copied = sem("in_copied")
        out_copied = sem("out_copied")
        xn_dram, y_dram = m["xn_dram"], m["y_dram"][layer]
        y_rows = y_dram.rearrange("(t k) d -> t k d", k=TOP_K)
        ring = m["ring"]
        W = m["expert_views"][layer]

        block = ctx.enter_context(nc.Block())

        @block.sync
        def _(sp):
            sp.dma_start(norm_b[:], m["norm_m"][layer:layer + 1, :].broadcast_to([128, D_MODEL])).then_inc(consts_in, 16)
            sp.dma_start(w_router[:, :, 0:N_GROUPS], m["w_rg"][layer].rearrange("(p t) n -> p t n", t=KT)).then_inc(consts_in, 16)
            sp.dma_start(w_router[:, :, N_GROUPS:], m["w_re"][layer].rearrange("(p t) n -> p t n", t=KT)).then_inc(consts_in, 16)
            sp.dma_start(b_router[:, 0:N_GROUPS], m["b_rg"][layer:layer + 1, :].broadcast_to([128, N_GROUPS])).then_inc(consts_in, 16)
            sp.dma_start(b_router[:, N_GROUPS:], m["b_re"][layer:layer + 1, :].broadcast_to([128, N_EXPERTS])).then_inc(consts_in, 16)
            sp.wait_ge(normed, NT)
            for t in range(NT):
                sp.dma_start(xn_dram[128 * t:128 * t + rows[t], :], xn[0:rows[t], t, :]).then_inc(xn_stored, 16)
            with sp.Fori(1, MAIN_GROUPS) as g:
                for n in range(3):
                    sp.wait_ge(weights_used[n], g)
                    for e in range(2):
                        sp.dma_start(ring[n][:, e:e + 1, :], W[n][:, bass.ds(2 * g + e, 1), :]).then_inc(weights_in[n][e], 16)
            sp.wait_ge(table_ready, 1)
            groups = sp.value_load(steer[0:1, 0:1], min_val=MAIN_GROUPS, max_val=MAIN_GROUPS + OVER_GROUPS)
            with sp.If(groups > MAIN_GROUPS):
                with sp.Fori(MAIN_GROUPS, groups) as g:
                    for e in range(2):
                        expert = sp.value_load(steer[0:1, bass.ds(2 * (g - MAIN_GROUPS) + 1 + e, 1)], min_val=0, max_val=N_EXPERTS - 1)
                        for n in range(3):
                            sp.wait_ge(weights_used[n], g)
                            sp.dma_start(ring[n][:, e:e + 1, :], W[n][:, bass.ds(expert, 1), :]).then_inc(weights_in[n][e], 16)
            sp.wait_ge(scattered_all, 1)
            for t in range(NT):
                sp.dma_start(ring[0][0:rows[t], :, :].rearrange("p a n -> p (a n)")[:, 2048 * t:2048 * t + 2048].rearrange("p (k d) -> p k d", k=2),
                             y_rows[128 * t:128 * t + rows[t], :, :]).then_inc(y_back[t], 16)

        @block.gpsimd
        def _(pool):
            nc.gpsimd.memset(xg[:], 0.0).then_inc(cleared, 1)
            pool.wait_ge(cleared, 1)
            pool.wait_ge(xn_stored, 16 * NT)
            pool.wait_ge(table_ready, 1)
            last_group = pool.value_load(steer[0:1, 2 * OVER_GROUPS + 1:2 * OVER_GROUPS + 2], min_val=MAIN_GROUPS - 1, max_val=N_COLS - 1)

            def gather(g):
                if not (isinstance(g, int) and g == 0):
                    pool.wait_ge(gathered, 16 * g)
                nc.gpsimd.tensor_copy(rows_in[:, :], table[:, 0, bass.ds(g, 1)]).then_inc(in_copied, 1)
                pool.wait_ge(in_copied, g + 1)
                if not (isinstance(g, int) and g == 0):
                    pool.wait_ge(gx_T, g)
                pool.sem_inc(waits_held, 1)
                pool.indirect_dma_start(xg[:, :], None, xn_dram[:, :], bass.IndirectOffsetOnAxis(rows_in[:, :], 0),
                                        bounds_check=T_ALL - 1, oob_is_err=False).then_inc(gathered, 16)

            def scatter(g, first):
                if not first:
                    pool.wait_ge(scattered, 16 * g)
                nc.gpsimd.tensor_copy(rows_out[:, :], table[:, 1, bass.ds(g, 1)]).then_inc(out_copied, 1)
                pool.wait_ge(out_copied, g + 1)
                pool.wait_ge(y_kept, 2 * g + 2)
                pool.sem_inc(waits_held, 1)
                pool.indirect_dma_start(y_dram[:, :], bass.IndirectOffsetOnAxis(rows_out[:, :], 0), y_sb[:, :], None,
                                        bounds_check=TOP_K * T_ALL - 1, oob_is_err=False).then_inc(scattered, 16)

            gather(0)
            gather(1)
            scatter(0, True)
            with pool.Fori(1, last_group) as g:
                gather(g + 1)
                scatter(g, False)
            scatter(last_group, False)
            pool.wait_ge(scattered, 16 * last_group + 16)
            pool.sem_inc(scattered_all, 1)

        @block.scalar
        def _(act):
            act.wait_ge(ss_cleared, 1)
            for t in range(NT):
                r = rows[t]
                nc.scalar.activation(sq[0:r, :], resid[0:r, t, :], ACT.Square, accum_out=ss[0:r, t:t + 1]).then_inc(squares, 1)
                act.wait_ge(squares, t + 1)
            act.wait_ge(mean_made, 1)
            nc.scalar.activation(rstd[:, :], ss[:, :], ACT.Sqrt).then_inc(roots, 1)
            for t in range(NT):
                for j in range(2):
                    act.wait_ge(xT_made, 2 * t + j + 1)
                    nc.scalar.copy(xnT[:, 4 * j:4 * j + 4, at[t]], ps_xT[t][:, j, :, 0:rows[t]]).then_inc(xT_kept, 1)
            act.wait_ge(gdiff, 1)
            nc.scalar.activation(gexp[:], gexp[:], ACT.Exp).then_inc(gexped, 1)
            act.wait_ge(tdiff, 1)
            nc.scalar.activation(ratio[:], ratio[:], ACT.Exp).then_inc(texped, 1)
            act.wait_ge(table_ready, 1)
            groups = act.value_load(steer[0:1, 0:1], min_val=MAIN_GROUPS, max_val=MAIN_GROUPS + OVER_GROUPS)

            def group(g, first):
                act.wait_ge(gx_T, g + 1)
                if not first:
                    act.wait_ge(up_made, g)
                nc.scalar.copy(xgT[:, 4:8, :], ps_x[:, 1]).then_inc(gx_kept, 1)
                act.wait_ge(gate_made, g + 1)
                if not first:
                    act.wait_ge(hidden, g)
                nc.scalar.activation(silu[:], ps_gate[:], ACT.Silu).then_inc(silued, 1)
                act.wait_ge(y_made, g + 1)
                if not first:
                    act.wait_ge(scattered, 16 * g)
                nc.scalar.copy(y_sb[:, 512:1024], ps_y[:, 1]).then_inc(y_kept, 1)

            group(0, True)
            with act.Fori(1, groups) as g:
                group(g, False)


        @block.vector
        def _(dve):
            n = [0]

            def link(ins):
                n[0] += 1
                ins.then_inc(vchain, 1)
                dve.wait_ge(vchain, n[0])

            V = nc.vector
            link(V.memset(logits[:], 0.0))
            V.memset(ss[:], 1.0).then_inc(ss_cleared, 1)
            dve.wait_ge(squares, NT)
            V.tensor_scalar(ss[:, :], ss[:, :], 1.0 / D_MODEL, EPS, ALU.mult, ALU.add).then_inc(mean_made, 1)
            dve.wait_ge(roots, 1)
            link(V.reciprocal(rstd[:, :], rstd[:, :]))
            dve.wait_ge(consts_in, 16 * 5)
            for t in range(NT):
                r = rows[t]
                V.scalar_tensor_tensor(xn[0:r, t, :], resid[0:r, t, :], rstd[0:r, t:t + 1], norm_b[0:r, :], ALU.mult, ALU.mult).then_inc(normed, 1)
            for t in range(NT):
                r = rows[t]
                dve.wait_ge(logT_made, t + 1)
                V.tensor_copy(logT[:, at[t]], ps_logT[t][0:N_GROUPS + N_EXPERTS, 0:r]).then_inc(logT_kept, 1)
            dve.wait_ge(logits_made, 1)
            for t in range(NT):
                r = rows[t]
                V.tensor_tensor(logits[0:r, t, :], ps_log[0:r, t, :], b_router[0:r, :], ALU.add).then_inc(logits_kept, 1)
            dve.wait_ge(logits_kept, NT)
            lg, le = logits[:, :, 0:N_GROUPS], logits[:, :, N_GROUPS:]

            def bc(a, k):
                return a.unsqueeze(2).broadcast_to([128, NT, k])

            link(V.tensor_reduce(gmax[:], lg, AX.X, ALU.max))
            V.tensor_tensor(gexp[:], lg, bc(gmax[:], N_GROUPS), ALU.subtract).then_inc(gdiff, 1)
            link(V.tensor_tensor(gpick[:], lg, bc(gmax[:], N_GROUPS), ALU.is_equal))
            link(V.tensor_tensor(gpick[:], gpick[:], m["falling"][:, 0:N_GROUPS].unsqueeze(1).broadcast_to([128, NT, N_GROUPS]), ALU.mult))
            link(V.tensor_reduce(gbest[:], gpick[:], AX.X, ALU.max))
            link(V.tensor_tensor(gpick[:], gpick[:], bc(gbest[:], N_GROUPS), ALU.is_equal))
            link(V.tensor_scalar(gpick[:], gpick[:], 1.0, FAR, ALU.subtract, ALU.mult))
            link(V.tensor_tensor(masked[:].rearrange("p t (g e) -> p t g e", g=N_GROUPS), le.rearrange("p t (g e) -> p t g e", g=N_GROUPS),
                                 gpick[:].unsqueeze(3).broadcast_to([128, NT, N_GROUPS, EXP_PER_GROUP]), ALU.add))
            for k in range(TOP_K):
                link(V.tensor_reduce(top[:, k, :], masked[:], AX.X, ALU.max))
                link(V.tensor_tensor(etmp[:], masked[:], bc(top[:, k, :], N_EXPERTS), ALU.is_equal))
                link(V.tensor_tensor(etmp[:], etmp[:], m["falling"][:, 0:N_EXPERTS].unsqueeze(1).broadcast_to([128, NT, N_EXPERTS]), ALU.mult))
                link(V.tensor_reduce(ebest[:], etmp[:], AX.X, ALU.max))
                link(V.tensor_tensor(oneh[:, k], etmp[:], bc(ebest[:], N_EXPERTS), ALU.is_equal))
                if k == 0:
                    link(V.scalar_tensor_tensor(masked[:], oneh[:, k], -3.0 * FAR, masked[:], ALU.mult, ALU.add))
            V.tensor_tensor(ratio[:], top[:, 1, :], top[:, 0, :], ALU.subtract).then_inc(tdiff, 1)
            link(V.tensor_tensor(oneh[:], oneh[:], m["valid"][:, :].unsqueeze(1).unsqueeze(3).broadcast_to([128, TOP_K, NT, N_EXPERTS]), ALU.mult))
            V.tensor_tensor(both[:], oneh[:, 0], oneh[:, 1], ALU.add).then_inc(hots, 1)

            def by_expert(a):
                return a.unsqueeze(1).unsqueeze(1).broadcast_to([128, TOP_K, NT, N_EXPERTS])

            def bk(a, n):
                return a.unsqueeze(3).broadcast_to([128, TOP_K, NT, n])

            dve.wait_ge(gexped, 1)
            V.tensor_tensor(ctmp[:], oneh[:], by_expert(m["odd_slots"][:, :]), ALU.mult)
            link(V.tensor_reduce(gsum[:], gexp[:], AX.X, ALU.add))
            dve.wait_ge(texped, 1)
            V.tensor_reduce(lmain[:], ctmp[:], AX.X, ALU.add)
            V.tensor_reduce(colhot[:, :, :, 0:MAIN_GROUPS], oneh[:].rearrange("p k a (g e) -> p (k a) g e", e=2), AX.X, ALU.add)
            V.reciprocal(gsum[:], gsum[:])
            link(V.tensor_scalar(ebest[:], ratio[:], 1.0, None, ALU.add))
            link(V.reciprocal(ebest[:], ebest[:]))
            link(V.tensor_tensor(gate[:, 0, :], gsum[:], ebest[:], ALU.mult))
            link(V.tensor_tensor(gate[:, 1, :], gate[:, 0, :], ratio[:], ALU.mult))
            dve.wait_ge(ranked, 1)
            V.tensor_copy(rank[:], ps_rank)
            link(V.tensor_copy(counts[:], ps_count))
            V.tensor_scalar(nover[:], counts[:], float(SLOTS), None, ALU.is_gt)
            link(V.tensor_tensor(ktmp[:], oneh[:], rank[:].unsqueeze(1).broadcast_to([128, TOP_K, NT, N_EXPERTS]), ALU.mult))
            V.tensor_reduce(rk[:], ktmp[:], AX.X, ALU.add)
            for j in range(2, OVER_LEVELS + 1):
                link(V.scalar_tensor_tensor(nover[:], counts[:], float(SLOTS * j), nover[:], ALU.is_gt, ALU.add))
                if j == 2:
                    V.tensor_tensor(lmain[:], lmain[:], rk[:], ALU.add)
                    V.tensor_scalar(inmain[:], rk[:], float(SLOTS), None, ALU.is_lt)
                    V.tensor_scalar(rkm[:], rk[:], -float(SLOTS), None, ALU.add)
            V.tensor_tensor(colhot[:, :, :, 0:MAIN_GROUPS], colhot[:, :, :, 0:MAIN_GROUPS], bk(inmain[:], MAIN_GROUPS), ALU.mult)
            V.tensor_scalar(spare[:], inmain[:], -1.0, 1.0, ALU.mult, ALU.add)
            link(V.tensor_tensor_scan(cend[:], nover[:], nover[:], 0.0, ALU.add, ALU.bypass))
            V.tensor_tensor(spare[:], spare[:], m["valid"][:, :].unsqueeze(1).broadcast_to([128, TOP_K, NT]), ALU.mult)
            link(V.tensor_tensor(cstart[:], cend[:], nover[:], ALU.subtract))
            link(V.tensor_tensor(ctmp[:], oneh[:], by_expert(cstart[:, :]), ALU.mult))
            link(V.tensor_reduce(opos[:], ctmp[:], AX.X, ALU.add))
            link(V.scalar_tensor_tensor(opos[:], opos[:], float(SLOTS), rkm[:], ALU.mult, ALU.add))
            link(V.tensor_tensor(oge[:], bk(opos[:], OVER_GROUPS + 1), m["block_starts"][:, :].unsqueeze(1).unsqueeze(1).broadcast_to([128, TOP_K, NT, OVER_GROUPS + 1]), ALU.is_ge))
            V.tensor_tensor(colhot[:, :, :, MAIN_GROUPS:], oge[:, :, :, 0:OVER_GROUPS], oge[:, :, :, 1:OVER_GROUPS + 1], ALU.subtract)
            link(V.tensor_reduce(olow[:], oge[:, :, :, 1:OVER_GROUPS], AX.X, ALU.add))
            V.tensor_tensor(colhot[:, :, :, MAIN_GROUPS:], colhot[:, :, :, MAIN_GROUPS:], bk(spare[:], OVER_GROUPS), ALU.mult)
            link(V.scalar_tensor_tensor(olow[:], olow[:], -128.0, opos[:], ALU.mult, ALU.add))
            link(V.tensor_tensor(lmain[:], lmain[:], olow[:], ALU.subtract))
            link(V.tensor_tensor(lmain[:], lmain[:], inmain[:], ALU.mult))
            link(V.tensor_tensor(lpos[:], lmain[:], olow[:], ALU.add))
            for k in range(TOP_K):
                for t in range(NT):
                    V.tensor_scalar(place[:, k, t, :], m["lanes"][:, :], lpos[:, k, t:t + 1], None, ALU.is_equal)
                for j in range(2):
                    last = V.tensor_tensor(entry[:, k, :, j, :], colhot[:, k], bc(m["token_no"][:, k, j, :], N_COLS), ALU.mult)
                last.then_inc(placed, 1)
            V.tensor_tensor(obf[:], cend[0:1, :].unsqueeze(1).broadcast_to([1, 2 * OVER_GROUPS, N_EXPERTS]),
                            m["block_no"][0:1, :].unsqueeze(2).broadcast_to([1, 2 * OVER_GROUPS, N_EXPERTS]), ALU.is_le)
            V.memset(ovalf[:], float(MAIN_GROUPS))
            link(V.tensor_reduce(ngf[:, 0:1], nover[0:1, :], AX.X, ALU.add))
            V.tensor_reduce(ovalf[:, 1:2 * OVER_GROUPS + 1], obf[:], AX.X, ALU.add)
            for j in range(OVER_GROUPS):
                link(V.scalar_tensor_tensor(ovalf[:, 0:1], ngf[:, 0:1], 2.0 * j, ovalf[:, 0:1], ALU.is_gt, ALU.add))
            V.tensor_scalar(ovalf[:, 1:2 * OVER_GROUPS + 1], ovalf[:, 1:2 * OVER_GROUPS + 1], float(N_EXPERTS - 1), None, ALU.min)
            link(V.tensor_scalar(ovalf[:, 2 * OVER_GROUPS + 1:], ovalf[:, 0:1], -1.0, None, ALU.add))
            link(V.tensor_copy(steer[:], ovalf[:]))
            dve.wait_ge(tabbed, 1)
            tf = tabf[:].rearrange("p a c -> p (a c)")
            tz = tabz[:].rearrange("p a c -> p (a c)")
            link(V.tensor_copy(tf, ps_tab))
            link(V.tensor_scalar(tz, tf, 0.0, NOWHERE, ALU.is_equal, ALU.mult))
            link(V.scalar_tensor_tensor(tf, tf, -1.0, tz, ALU.add, ALU.add))
            V.tensor_copy(table[:].rearrange("p a c -> p (a c)"), tf).then_inc(table_ready, 1)
            dve.wait_ge(table_ready, 1)
            groups = dve.value_load(steer[0:1, 0:1], min_val=MAIN_GROUPS, max_val=MAIN_GROUPS + OVER_GROUPS)

            def group(g, first):
                dve.wait_ge(gx_T, g + 1)
                if not first:
                    dve.wait_ge(up_made, g)
                V.tensor_copy(xgT[:, 0:4, :], ps_x[:, 0]).then_inc(gx_kept, 1)
                dve.wait_ge(up_made, g + 1)
                dve.wait_ge(silued, g + 1)
                if not first:
                    dve.wait_ge(hid_T, g)
                V.tensor_tensor(hid[:], silu[:], ps_up[:], ALU.mult).then_inc(hidden, 1)
                dve.wait_ge(hid_T, g + 1)
                if not first:
                    dve.wait_ge(y_made, g)
                V.tensor_copy(hidT[:], ps_hid[:]).then_inc(hid_kept, 1)
                dve.wait_ge(y_made, g + 1)
                if not first:
                    dve.wait_ge(scattered, 16 * g)
                V.tensor_copy(y_sb[:, 0:512], ps_y[:, 0]).then_inc(y_kept, 1)

            group(0, True)
            with dve.Fori(1, groups) as g:
                group(g, False)
            back = ring[0][:].rearrange("p a n -> p (a n)")
            for t in range(NT):
                r = rows[t]
                dve.wait_ge(y_back[t], 16)
                for k in range(TOP_K):
                    link(V.scalar_tensor_tensor(resid[0:r, t, :], back[0:r, 2048 * t + 1024 * k:2048 * t + 1024 * k + 1024], gate[0:r, k, t:t + 1],
                                                resid[0:r, t, :], ALU.mult, ALU.add))

        @block.tensor
        def _(pe):
            T = nc.tensor

            def transposes(t):
                pe.wait_ge(normed, t + 1)
                if t == 2:
                    pe.wait_ge(xT_kept, 2)
                xv = xn[0:rows[t], t, :].rearrange("p (c k) -> p k c", k=KT)
                for k in range(KT):
                    last = T.transpose(ps_xT[t][:, k // 4, k % 4, 0:rows[t]], xv[:, k, :], ident[0:rows[t], 0:rows[t]])
                    if k % 4 == 3:
                        last.then_inc(xT_made, 1)

            def router(t):
                pe.wait_ge(xT_kept, 2 * t + 2)
                if t == 2:
                    pe.wait_ge(logT_kept, 1)
                for k in range(KT):
                    last = T.matmul(ps_logT[t][0:N_GROUPS + N_EXPERTS, 0:rows[t]], w_router[:, k, :], xnT[:, k, at[t]], start=(k == 0), stop=(k == KT - 1))
                last.then_inc(logT_made, 1)

            transposes(0)
            transposes(1)
            router(0)
            transposes(2)
            router(1)
            router(2)
            for t in range(NT):
                pe.wait_ge(logT_kept, t + 1)
                last = T.transpose(ps_log[0:rows[t], t, :], logT[:, at[t]], ident[0:N_GROUPS + N_EXPERTS, 0:N_GROUPS + N_EXPERTS])
            last.then_inc(logits_made, 1)
            pe.wait_ge(hots, 1)
            for t in range(NT):
                for s in range(t):
                    T.matmul(ps_rank[:, t, :], m["ones"][:, :], both[:, s, :], start=(s == 0), stop=False)
                T.matmul(ps_rank[:, t, :], m["before"][:, :], both[:, t, :], start=(t == 0), stop=True)
            for s in range(NT):
                last = T.matmul(ps_count, m["ones"][:, :], both[:, s, :], start=(s == 0), stop=(s == NT - 1))
            last.then_inc(ranked, 1)
            for k in range(TOP_K):
                pe.wait_ge(placed, k + 1)
                for t in range(NT):
                    last = T.matmul(ps_tab, place[:, k, t, :], entry[:, k, t].rearrange("p a c -> p (a c)"),
                                    start=(k == 0 and t == 0), stop=(k == TOP_K - 1 and t == NT - 1))
            last.then_inc(tabbed, 1)
            pe.wait_ge(table_ready, 1)
            groups = pe.value_load(steer[0:1, 0:1], min_val=MAIN_GROUPS, max_val=MAIN_GROUPS + OVER_GROUPS)
            xgv = xg[:, :].rearrange("p (c k) -> p k c", k=KT)
            hidv = hid[:, :].rearrange("p (c k) -> p k c", k=FT)

            def group(g, first):
                pe.wait_ge(gathered, 16 * g + 16)
                if not first:
                    pe.wait_ge(gx_kept, 2 * g)
                for k in range(KT):
                    last = T.transpose(ps_x[:, k // 4, k % 4, :], xgv[:, k, :], ident[:, :])
                last.then_inc(gx_T, 1)
                pe.wait_ge(gx_kept, 2 * g + 2)
                if not first:
                    pe.wait_ge(silued, g)
                for n, ps in ((0, ps_gate), (1, ps_up)):
                    if n == 1 and not first:
                        pe.wait_ge(hidden, g)
                    for e in range(2):
                        pe.wait_ge(weights_in[n][e], 16 * g + 16)
                    for k in range(KT):
                        for e in range(2):
                            last = T.matmul(ps[64 * e:64 * e + 64, :], xgT[:, k, 64 * e:64 * e + 64],
                                            ring[n][:, e, 512 * k:512 * k + 512], start=(k == 0), stop=(k == KT - 1))
                    last.then_inc(weights_used[n], 1)
                pe.wait_ge(hidden, g + 1)
                if not first:
                    pe.wait_ge(hid_kept, g)
                for k in range(FT):
                    last = T.transpose(ps_hid[:, k, :], hidv[:, k, :], ident[:, :])
                last.then_inc(hid_T, 1)
                pe.wait_ge(hid_kept, g + 1)
                if not first:
                    pe.wait_ge(y_kept, 2 * g)
                for e in range(2):
                    pe.wait_ge(weights_in[2][e], 16 * g + 16)
                for h in range(2):
                    for k in range(FT):
                        for e in range(2):
                            last = T.matmul(ps_y[64 * e:64 * e + 64, h, :], hidT[:, k, 64 * e:64 * e + 64],
                                            ring[2][:, e, 1024 * k + 512 * h:1024 * k + 512 * h + 512], start=(k == 0), stop=(k == FT - 1))
                last.then_inc(weights_used[2], 1)

            group(0, True)
            with pe.Fori(1, groups) as g:
                group(g, False)

    nc.clear_and_free_semaphores(sems)
    nc.all_engine_barrier(sem_only=True)


def final_phase(nc, m):
    ctx, sems = ExitStack(), []
    with ctx:
        def sem(name):
            sems.append(nc.alloc_semaphore(f"fin_{name}"))
            return sems[-1]

        NT, rows = TOK_TILES, TILE_ROWS
        norm_b = ctx.enter_context(nc.sbuf_tensor("fin_norm", [128, D_MODEL], F32))
        sq = ctx.enter_context(nc.sbuf_tensor("fin_sq", [128, D_MODEL], F32))
        ss = ctx.enter_context(nc.sbuf_tensor("fin_ss", [128, NT], F32))
        cleared, squares, mean_made, roots, inverse, norm_in, normed, stored = (sem(n) for n in (
            "cleared", "squares", "mean_made", "roots", "inverse", "norm_in", "normed", "stored"))
        block = ctx.enter_context(nc.Block())

        @block.sync
        def _(sp):
            sp.dma_start(norm_b[:], m["final_norm"].rearrange("(a d) -> a d", a=1).broadcast_to([128, D_MODEL])).then_inc(norm_in, 16)
            for t in range(NT):
                sp.wait_ge(normed, t + 1)
                dst = m["y_prompt"][0, 128 * t:128 * t + 128, :] if t < 2 else m["y_sample"].rearrange("b l d -> (b l) d")
                sp.dma_start(dst, m["resid"][0:rows[t], t, :]).then_inc(stored, 16)
            sp.wait_ge(stored, 16 * NT)

        @block.scalar
        def _(act):
            act.wait_ge(cleared, 1)
            for t in range(NT):
                r = rows[t]
                nc.scalar.activation(sq[0:r, :], m["resid"][0:r, t, :], ACT.Square, accum_out=ss[0:r, t:t + 1]).then_inc(squares, 1)
                act.wait_ge(squares, t + 1)
            act.wait_ge(mean_made, 1)
            nc.scalar.activation(ss[:, :], ss[:, :], ACT.Sqrt).then_inc(roots, 1)

        @block.vector
        def _(dve):
            nc.vector.memset(ss[:], 1.0).then_inc(cleared, 1)
            dve.wait_ge(squares, NT)
            nc.vector.tensor_scalar(ss[:, :], ss[:, :], 1.0 / D_MODEL, EPS, ALU.mult, ALU.add).then_inc(mean_made, 1)
            dve.wait_ge(roots, 1)
            nc.vector.reciprocal(ss[:, :], ss[:, :]).then_inc(inverse, 1)
            dve.wait_ge(inverse, 1)
            dve.wait_ge(norm_in, 16)
            for t in range(NT):
                r = rows[t]
                nc.vector.scalar_tensor_tensor(m["resid"][0:r, t, :], m["resid"][0:r, t, :], ss[0:r, t:t + 1], norm_b[0:r, :],
                                               ALU.mult, ALU.mult).then_inc(normed, 1)

    nc.clear_and_free_semaphores(sems)
    nc.all_engine_barrier(sem_only=True)

def decoder_step(nc, m, shapes):
    m["xn_dram"] = nc.dram_tensor("xn_rows", (T_ALL, D_MODEL), F32, kind="Internal").ap()
    m["y_dram"] = [nc.dram_tensor(f"expert_rows{i}", (TOP_K * T_ALL, D_MODEL), F32, kind="Internal").ap() for i in range(LAYERS)]
    with ExitStack() as ctx:
        def sb(name, shape):
            return ctx.enter_context(nc.sbuf_tensor(name, shape, F32))

        m["resid"] = sb("resid", [128, TOK_TILES, D_MODEL])
        m["consts"] = sb("consts", [128, sum(shapes.values())])
        start = 0
        for name, width in shapes.items():
            m[name] = m["consts"][:, start:start + width]
            start += width
        m["token_no"] = m["token_no"].rearrange("p (k j t) -> p k j t", k=TOP_K, j=2)
        m["levels"] = m["levels"].rearrange("p (n i) -> p n i", n=LEVELS)
        m["cos"] = m["cos"].rearrange("p (t d) -> p t d", t=TOK_TILES)
        m["sin"] = m["sin"].rearrange("p (t d) -> p t d", t=TOK_TILES)
        m["new_keys"] = m["new_keys"].rearrange("p (a k) -> p a k", k=T_DEC)
        m["ring"] = [sb(f"ring_{n}", [128, 2, KT * D_FF_EXPERT]) for n in ("gate", "up", "down")]
        m["expert_views"] = [[w[i].rearrange("e (p t) n -> p e (t n)", p=128) for w in (m["w_gate_e"], m["w_up_e"], m["w_down_e"])] for i in range(LAYERS)]
        m["weights_of"] = [[[ctx.enter_context(nc.semaphore(f"{n}{e}_in_{i}")) for e in range(2)] for n in ("gate", "up", "down")] for i in range(LAYERS)]

        def prefetch(eng, layer, kinds):
            for n in kinds:
                for e in range(2):
                    eng.dma_start(m["ring"][n][:, e:e + 1, :], m["expert_views"][layer][n][:, e:e + 1, :]).then_inc(m["weights_of"][layer][n][e], 16)

        m["prefetch"] = prefetch
        gdn_phase(nc, m)
        moe_phase(nc, m, 0)
        attn_phase(nc, m)
        moe_phase(nc, m, 1)
        final_phase(nc, m)


_OUTS = [("y_prompt", (1, SEQ, D_MODEL)), ("y_sample", (DEC_BATCH, DEC_SEQ, D_MODEL)),
         ("sd_prompt", (1, 1, HEADS, DK, DK)), ("sc_prompt", (1, 1, CONV_W - 1, CONV_CH)),
         ("k_prompt", (1, SEQ, HEADS, 2 * DH)), ("v_prompt", (1, SEQ, HEADS, 2 * DH)),
         ("sd_sample", (1, DEC_BATCH, HEADS, DK, DK)), ("sc_sample", (1, DEC_BATCH, CONV_W - 1, CONV_CH)),
         ("k_sample", (DEC_BATCH, DEC_SEQ, HEADS, 2 * DH)), ("v_sample", (DEC_BATCH, DEC_SEQ, HEADS, 2 * DH))]


def kernel(**inputs):
    import concourse.bacc as _bacc
    from concourse.bass_utils import run_bass_kernel_spmd as _run

    nc = _bacc.Bacc("TRN2", target_bir_lowering=False, num_devices=1)
    tables = shape_constants()
    arrays, aps = {}, {}

    def give(name, a):
        arrays[f"in_{name}_dram"] = a
        aps[name] = nc.dram_tensor(f"in_{name}_dram", a.shape, mybir.dt.from_np(a.dtype), kind="ExternalInput").ap()

    for name, a in inputs.items():
        give(name, np.ascontiguousarray(a))
    give("consts_dram", np.ascontiguousarray(np.concatenate(list(tables.values()), 1)))
    for name, shape in _OUTS:
        aps[name] = nc.dram_tensor(f"out_{name}_dram", shape, F32, kind="ExternalOutput").ap()
    decoder_step(nc, aps, {n: a.shape[1] for n, a in tables.items()})
    r = _run(nc, [arrays], core_ids=[0])
    return tuple(r.results[0][f"out_{name}_dram"] for name, _ in _OUTS)
```
